# Optimizing a Trainium2 kernel written in Bass

```python
import jax
import jax.numpy as jnp
from jax import lax
import numpy as np

D_MODEL = 1024
BATCH = 1
SEQ = 512
DEPTH = 2
DEC_BATCH = 8
DEC_SEQ = 8
PAST_LEN = 512
PAGE_SIZE = 128

HEAD_DIM = 64
N_ATTN_HEADS = 8
D_ATTN = N_ATTN_HEADS * HEAD_DIM
D_CONV = D_MODEL - D_ATTN
D_MIX = D_ATTN + D_CONV
D_IN = 3 * D_ATTN + 2 * D_CONV
CONV_WIDTH = 31
CONV_HIST = CONV_WIDTH - 1
DIL_PAIRS = ((128, 1), (512, 4), (2048, 16))
WINDOW_MAX = max(w for w, _ in DIL_PAIRS)
QBLOCK = 128
ROT_DIM = HEAD_DIM // 4
ROPE_THETA = 500000.0
D_FF = -(-8 * D_MODEL // (3 * 256)) * 256
DN_ALPHA = (2 * DEPTH) ** 0.25
DN_BETA = (8 * DEPTH) ** -0.25
LN_EPS = 1e-5
NEG_INF = -1e30

kernel_name = 'hymba_dilated_conformer_decoder_step'

def _layernorm(x, g, b):
    xf = x.astype(jnp.float32)
    mu = jnp.mean(xf, axis=-1, keepdims=True)
    var = jnp.mean(jnp.square(xf - mu), axis=-1, keepdims=True)
    y = (xf - mu) * lax.rsqrt(var + LN_EPS)
    return (y * g.astype(jnp.float32) + b.astype(jnp.float32)).astype(x.dtype)

def _rmsnorm(x, g):
    xf = x.astype(jnp.float32)
    y = xf * lax.rsqrt(jnp.mean(jnp.square(xf), axis=-1, keepdims=True) + LN_EPS)
    return (y * g.astype(jnp.float32)).astype(x.dtype)

def _rope(x, pos):
    half = ROT_DIM // 2
    inv_freq = jnp.power(ROPE_THETA, -jnp.arange(half, dtype=jnp.float32) * 2.0 / ROT_DIM)
    ang = pos.astype(jnp.float32)[:, None] * inv_freq[None, :]
    cos = jnp.cos(ang)[None, :, None, :]
    sin = jnp.sin(ang)[None, :, None, :]
    xf = x.astype(jnp.float32)
    x1 = xf[..., :half]
    x2 = xf[..., half:ROT_DIM]
    out = jnp.concatenate([x1 * cos - x2 * sin, x2 * cos + x1 * sin, xf[..., ROT_DIM:]], axis=-1)
    return out.astype(x.dtype)

def _band_attention(q, k, v, w_sub):
    n, l, h, dh = q.shape
    nb = -(-l // QBLOCK)
    lp = nb * QBLOCK
    pad = lp - l
    qb = jnp.pad(q, ((0, 0), (0, pad), (0, 0), (0, 0))).reshape(n, nb, QBLOCK, h, dh)

    def key_blocks(t):
        tp = jnp.pad(t, ((0, 0), (QBLOCK, pad), (0, 0), (0, 0))).reshape(n, nb + 1, QBLOCK, h, dh)
        return jnp.concatenate([tp[:, :-1], tp[:, 1:]], axis=2)

    kb = key_blocks(k)
    vb = key_blocks(v)
    s = jnp.einsum('nbqhd,nbkhd->nbhqk', qb, kb, preferred_element_type=jnp.float32)
    blk = jnp.arange(nb)[:, None, None] * QBLOCK
    qpos = blk + jnp.arange(QBLOCK)[None, :, None]
    kpos = blk - QBLOCK + jnp.arange(2 * QBLOCK)[None, None, :]
    mask = (kpos >= 0) & (kpos <= qpos) & (kpos >= qpos - w_sub)
    s = jnp.where(mask[None, :, None], s, NEG_INF)
    lse = jax.nn.logsumexp(s, axis=-1)
    p = jnp.exp(s - lse[..., None])
    o = jnp.einsum('nbhqk,nbkhd->nbqhd', p.astype(vb.dtype), vb, preferred_element_type=jnp.float32)
    o = o.reshape(n, lp, h, dh)[:, :l]
    lse = lse.transpose(0, 1, 3, 2).reshape(n, lp, h)[:, :l]
    return o, lse

def _merge_dilations(outs, lses):
    wts = jax.nn.softmax(jnp.stack(lses, axis=0), axis=0)
    return jnp.sum(wts[..., None] * jnp.stack(outs, axis=0), axis=0)

def _by_residue(t, dil):
    b, s, h, dh = t.shape
    return t.reshape(b, s // dil, dil, h, dh).transpose(0, 2, 1, 3, 4).reshape(b * dil, s // dil, h, dh)

def _dilated_attention_prompt(q, k, v):
    b, s, h, dh = q.shape
    outs, lses = [], []
    for window, dil in DIL_PAIRS:
        l = s // dil
        o, lse = _band_attention(_by_residue(q, dil), _by_residue(k, dil), _by_residue(v, dil), window // dil)
        outs.append(o.reshape(b, dil, l, h, dh).transpose(0, 2, 1, 3, 4).reshape(b, s, h, dh))
        lses.append(lse.reshape(b, dil, l, h).transpose(0, 2, 1, 3).reshape(b, s, h))
    return _merge_dilations(outs, lses)

def _dilated_attention_sample(q, k_all, v_all):
    b, t, h, dh = q.shape
    buf = k_all.shape[1] - t
    outs, lses = [], []
    for window, dil in DIL_PAIRS:
        n_keys = window // dil + 1
        idx = buf + jnp.arange(t)[:, None] - dil * jnp.arange(n_keys)[None, :]
        valid = idx >= 0
        idx = jnp.maximum(idx, 0)
        kg = k_all[:, idx]
        vg = v_all[:, idx]
        s = jnp.einsum('bthd,btjhd->bthj', q, kg, preferred_element_type=jnp.float32)
        s = jnp.where(valid[None, :, None, :], s, NEG_INF)
        lse = jax.nn.logsumexp(s, axis=-1)
        p = jnp.exp(s - lse[..., None])
        outs.append(jnp.einsum('bthj,btjhd->bthd', p.astype(vg.dtype), vg, preferred_element_type=jnp.float32))
        lses.append(lse)
    return _merge_dilations(outs, lses)

def _dwconv_causal(u_hist, conv_w, conv_b):
    y = lax.conv_general_dilated(u_hist, conv_w[:, None, :], window_strides=(1,), padding='VALID',
                                 dimension_numbers=('NWC', 'WIO', 'NWC'), feature_group_count=D_CONV)
    return y + conv_b

def _mixer(h, pos, w_in, conv_w, conv_b, conv_ln_g, conv_ln_b, beta_attn, beta_conv, w_out, kv_past, conv_past):
    b, l, _ = h.shape
    z = h @ w_in
    q, k, v, g = jnp.split(z, [D_ATTN, 2 * D_ATTN, 3 * D_ATTN], axis=-1)
    q = _rope(q.reshape(b, l, N_ATTN_HEADS, HEAD_DIM), pos) * (HEAD_DIM ** -0.5)
    k = _rope(k.reshape(b, l, N_ATTN_HEADS, HEAD_DIM), pos)
    v = v.reshape(b, l, N_ATTN_HEADS, HEAD_DIM)
    if kv_past is None:
        o = _dilated_attention_prompt(q, k, v)
    else:
        k_all = jnp.concatenate([kv_past[0], k], axis=1)
        v_all = jnp.concatenate([kv_past[1], v], axis=1)
        o = _dilated_attention_sample(q, k_all, v_all)
    o = o.astype(h.dtype).reshape(b, l, D_ATTN)
    ga, gb = jnp.split(g, 2, axis=-1)
    u = ga * jax.nn.sigmoid(gb)
    if conv_past is None:
        u_hist = jnp.pad(u, ((0, 0), (CONV_HIST, 0), (0, 0)))
    else:
        u_hist = jnp.concatenate([conv_past, u], axis=1)
    cz = jax.nn.silu(_layernorm(_dwconv_causal(u_hist, conv_w, conv_b), conv_ln_g, conv_ln_b))
    merged = jnp.concatenate([_rmsnorm(o, beta_attn), _rmsnorm(cz, beta_conv)], axis=-1) @ w_out
    return merged, k, v, u_hist[:, -CONV_HIST:]

def _forward(x, c, pos, past_k, past_v, past_conv, params):
    (w_in, conv_w, conv_b, conv_ln_g, conv_ln_b, beta_attn, beta_conv, w_out,
     ln1_g, ln1_b, w_gate, w_up, w_down, ln2_g, ln2_b, w_ada, b_ada) = params
    new_k, new_v, new_conv = [], [], []
    for i in range(DEPTH):
        mod = jax.nn.silu(c) @ w_ada[i] + b_ada[i]
        sh1, sc1, g1, sh2, sc2, g2 = jnp.split(mod[:, None, :], 6, axis=-1)
        h = x * (1 + sc1) + sh1
        if past_k is None:
            kv_past, conv_past = None, None
        else:
            kv_past, conv_past = (past_k[i], past_v[i]), past_conv[i]
        mix, k, v, conv_state = _mixer(h, pos, w_in[i], conv_w[i], conv_b[i], conv_ln_g[i], conv_ln_b[i],
                                       beta_attn[i], beta_conv[i], w_out[i], kv_past, conv_past)
        x = _layernorm(DN_ALPHA * x + g1 * mix, ln1_g[i], ln1_b[i])
        h = x * (1 + sc2) + sh2
        f = (jax.nn.silu(h @ w_gate[i]) * (h @ w_up[i])) @ w_down[i]
        x = _layernorm(DN_ALPHA * x + g2 * f, ln2_g[i], ln2_b[i])
        if past_k is None:
            keep = min(WINDOW_MAX, x.shape[1])
            k = k[:, -keep:]
            v = v[:, -keep:]
        new_k.append(k)
        new_v.append(v)
        new_conv.append(conv_state)
    return x, jnp.stack(new_k), jnp.stack(new_v), jnp.stack(new_conv)

def setup_inputs(seed: int = 0) -> dict:
    key = jax.random.key(seed)
    ks = jax.random.split(key, 26)
    f32 = jnp.float32

    def nrm(k, shape, scale):
        return jax.random.normal(k, shape, f32) * scale

    buf = min(WINDOW_MAX, PAST_LEN)
    col_scale = jnp.ones((D_IN,), f32).at[2 * D_ATTN:3 * D_ATTN].set(DN_BETA)
    return {
        'x_prompt': nrm(ks[0], (BATCH, SEQ, D_MODEL), 1.0),
        'x_sample': nrm(ks[1], (DEC_BATCH, DEC_SEQ, D_MODEL), 1.0),
        'cache_k': nrm(ks[2], (DEPTH, DEC_BATCH, buf, N_ATTN_HEADS, HEAD_DIM), 1.0),
        'cache_v': nrm(ks[3], (DEPTH, DEC_BATCH, buf, N_ATTN_HEADS, HEAD_DIM), 1.0),
        'state_conv': nrm(ks[4], (DEPTH, DEC_BATCH, CONV_HIST, D_CONV), 0.5),
        'c_prompt': nrm(ks[5], (BATCH, D_MODEL), 1.0),
        'c_sample': nrm(ks[6], (DEC_BATCH, D_MODEL), 1.0),
        'w_in': nrm(ks[7], (DEPTH, D_MODEL, D_IN), D_MODEL ** -0.5) * col_scale,
        'conv_w': nrm(ks[8], (DEPTH, CONV_WIDTH, D_CONV), CONV_WIDTH ** -0.5),
        'conv_b': nrm(ks[9], (DEPTH, D_CONV), 0.02),
        'conv_ln_g': 1.0 + nrm(ks[10], (DEPTH, D_CONV), 0.05),
        'conv_ln_b': nrm(ks[11], (DEPTH, D_CONV), 0.02),
        'beta_attn': 1.0 + nrm(ks[12], (DEPTH, D_ATTN), 0.05),
        'beta_conv': 1.0 + nrm(ks[13], (DEPTH, D_CONV), 0.05),
        'w_out': nrm(ks[14], (DEPTH, D_MIX, D_MODEL), D_MIX ** -0.5 * DN_BETA),
        'ln1_g': 1.0 + nrm(ks[15], (DEPTH, D_MODEL), 0.05),
        'ln1_b': nrm(ks[16], (DEPTH, D_MODEL), 0.02),
        'w_gate': nrm(ks[17], (DEPTH, D_MODEL, D_FF), D_MODEL ** -0.5),
        'w_up': nrm(ks[18], (DEPTH, D_MODEL, D_FF), D_MODEL ** -0.5),
        'w_down': nrm(ks[19], (DEPTH, D_FF, D_MODEL), D_FF ** -0.5 * DN_BETA),
        'ln2_g': 1.0 + nrm(ks[20], (DEPTH, D_MODEL), 0.05),
        'ln2_b': nrm(ks[21], (DEPTH, D_MODEL), 0.02),
        'w_ada': nrm(ks[22], (DEPTH, D_MODEL, 6 * D_MODEL), 0.5 * D_MODEL ** -0.5),
        'b_ada': nrm(ks[23], (DEPTH, 6 * D_MODEL), 0.02),
    }

def reference(x_prompt, x_sample, cache_k, cache_v, state_conv, c_prompt, c_sample, w_in, conv_w, conv_b,
              conv_ln_g, conv_ln_b, beta_attn, beta_conv, w_out, ln1_g, ln1_b, w_gate, w_up, w_down,
              ln2_g, ln2_b, w_ada, b_ada):
    params = (w_in, conv_w, conv_b, conv_ln_g, conv_ln_b, beta_attn, beta_conv, w_out,
              ln1_g, ln1_b, w_gate, w_up, w_down, ln2_g, ln2_b, w_ada, b_ada)
    pos_prompt = jnp.arange(x_prompt.shape[1])
    pos_sample = PAST_LEN + jnp.arange(x_sample.shape[1])
    y_prompt, k_p, v_p, conv_p = _forward(x_prompt, c_prompt, pos_prompt, None, None, None, params)
    y_sample, k_s, v_s, conv_s = _forward(x_sample, c_sample, pos_sample, cache_k, cache_v, state_conv, params)
    return (y_prompt, y_sample, k_p, v_p, conv_p, k_s, v_s, conv_s)


_drawn_inputs = setup_inputs


def setup_inputs(seed=0):
    import zlib

    import numpy as np

    out = dict(_drawn_inputs(seed))
    spreads = {}
    factors = {'conv_b': 8.0, 'conv_ln_g': 8.0, 'conv_ln_b': 31.539, 'beta_attn': 8.0, 'beta_conv': 8.0}
    for name, (base, spread) in spreads.items():
        noise = np.random.default_rng([zlib.crc32(name.encode()), seed]).standard_normal(out[name].shape)
        drawn = base * np.exp(spread * noise) if base else spread * noise
        out[name] = jnp.asarray(drawn.astype(out[name].dtype))
    for name, factor in factors.items():
        out[name] = (out[name] * factor).astype(out[name].dtype)
    return out
```

```python
from contextlib import ExitStack

import numpy as np

import concourse.bass as bass
from concourse import mybir

F32 = mybir.dt.float32
F32R = mybir.dt.float32r
ACT = mybir.ActivationFunctionType
ALU = mybir.AluOpType
AX = mybir.AxisListType

P = 128
D = 1024
DEPTH = 2
SEQ = 512
NB, NT = 8, 8
NS = NB * NT
T = SEQ + NS
H = T // 2
HP_ = SEQ - H
KT = D // P
HD = 64
NH = 8
DA = NH * HD
CT = DA // P
FF = 2816
FT = FF // P
CW = 31
HIST = CW - 1
PAST = 512
NVEC = CT * CW + 5 * CT + 4 * KT + 6 * KT
EPS = 1e-5
ALPHA = (2 * DEPTH) ** 0.25
SCALE = HD ** -0.5
NEG = -1e30
LEAST = -3.0e38

UNIT = KT * P
N_ADA, N_IN, N_OUT, N_GU = 6 * KT, 2 * CT + 3 * CT, KT, 2 * FT
DN_K = (8, 8, 6)
N_DN = KT * len(DN_K)
ADA0 = 0
IN0 = ADA0 + N_ADA
OUT0 = IN0 + N_IN
GU0 = OUT0 + N_OUT
DN0 = GU0 + N_GU
UL = DN0 + N_DN
Z_IN = 0
Z_OUT = Z_IN + N_IN // 2
Z_GU = Z_OUT + N_OUT // 2
Z_DN = Z_GU + N_GU // 2
ZL = Z_DN + KT // 2

V_CW = 0
V_CB = V_CW + CT * CW
V_CG = V_CB + CT
V_CLB = V_CG + CT
V_BA = V_CLB + CT
V_BC = V_BA + CT
V_G1 = V_BC + CT
V_B1 = V_G1 + KT
V_G2 = V_B1 + KT
V_B2 = V_G2 + KT
V_ADA = V_B2 + KT
SH1, SC1, G1, SH2, SC2, G2 = (j * KT for j in range(6))

QB = SEQ // P
E_OFF = [P * (q * (q + 1) // 2) for q in range(QB)]
E_ALL = P * QB * (QB + 1) // 2
PT_OFF = [0]
for _k in range(QB - 1):
    PT_OFF.append(PT_OFF[-1] + (QB - _k) * P)
S_BANK = [(4, 0), (4, P), (5, 0), (6, 0)]

SWAP = [i + 8 if i < 8 else i - 8 if i < 16 else i for i in range(32)]

PER = dict(lo_ready=UL, w_used=UL, hi_ready=UL, z_free=ZL, ada_out=N_ADA, mod_ready=1, hs_f=2, h_f=2 * KT, h_hi=2 * KT,
           hs_hi=2, h_lo=2 * (KT + 1), rope_cos=2 * CT, rope_done=2 * CT, vt_ps=QB + 1, vnat_ready=QB + 1,
           staged=CT, conv_staged=CT, s_ps=3 * NH, s_free=QB * NH, nm_ready=NH, exp_ready=QB * NH, p_ready=NH, pt_ps=QB * NH, pt_ready=QB * NH,
           o_ps=CT, o_free=CT, ss_ps=CT, ss_free=CT, nms_ready=CT, exps_ready=CT, ps_ready=CT, pts_ps=CT, pts_ready=2 * CT,
           os_ps=CT, os_ready=CT, ost_ps=CT, o_done=2 * CT, conv_done=CT, samp_done=CT, m_sum=1, m_mean=1, m_cent=1, m_sq=3, m_var=3,
           m_sd=3, m_mul=1, m_norm=1, cz=CT, m_f=2 * CT, m_hi=2 * CT, m_lo=2 * CT, gm_act=4 * KT, ln_sum=2, ln_mean=2,
           ln_cent=4, ln_sq=4, ln_var=2, ln_sd=2, ln_done=2 * KT, a_hi=FT, a_lo=FT, hist_zero=1)
FREE = dict(lo_ready=2, w_used=2, z_free=1, ada_out=2, s_free=QB, pt_ready=2, o_free=1, rope_done=2, samp_done=1, conv_done=1, ln_done=1, a_lo=1)


class Steps:

    def __init__(self, eng, sem):
        self.eng, self.sem, self.n = eng, sem, 0

    def of(self, ins):
        ins.then_inc(self.sem, 1)
        self.n += 1
        return self.n

    def wait(self, n):
        self.eng.wait_ge(self.sem, n)

    def link(self, ins):
        self.wait(self.of(ins))

    def restart(self):
        if self.n:
            self.wait(self.n)
            self.eng.sem_clear(self.sem)
            self.n = 0


def trunk(nc, xT, cT, w_ada, w_mix, w_dn, kc_d, vc_d, st_d, vec_d, rope_d, eye_d, mp_d, msc_d, msn_d,
          y_d, k_d, v_d, cp_d, cs_d):
    with ExitStack() as ctx:
        def sb(name, shape, dt=F32, where=ctx):
            return where.enter_context(nc.sbuf_tensor("sb_" + name, shape, dt))

        sems = {}
        for name in list(PER) + ["consts", "kc0", "kc1", "vc0", "vc1", "hist", "c_ready", "w_in0", "w_in1", "vec_in",
                                 "act_steps", "dve_steps", "pool_steps", "k_st", "v_st", "cv_st", "y_st", "carrier", "z_free1"]:
            sems[name] = ctx.enter_context(nc.semaphore(name))
        w_in = [sems["w_in0"], sems["w_in1"]]
        z_free = [sems["z_free"], sems["z_free1"]]
        kc_in = [sems["kc0"], sems["kc1"]]
        vc_in = [sems["vc0"], sems["vc1"]]

        def behind(eng, sem, value):
            eng.wait_ge(sem, value)
            eng.sem_inc(sems["carrier"], 1)

        def nth(l, name, k):
            return l * PER[name] + (k + 1 + FREE.get(name, 0))

        def slot(l, name, k):
            return l * PER[name] + (k + 1)

        x = sb("x", [P, KT, T])
        w_raw = sb("w_raw", [P, 2, UNIT])
        w_hi = sb("w_hi", [P, 2, UNIT], F32R)
        w_lo = sb("w_lo", [P, 2, UNIT], F32R)
        eye = sb("eye", [P, P])
        ones = sb("ones", [P, P])
        rope = sb("rope", [P, 2, T])
        mp = sb("mp", [P, 2, SEQ])
        msc = sb("msc", [P, 2, PAST])
        msn = sb("msn", [P, CT, 2, NS])
        mod = sb("mod", [P, 6 * KT, NB + 1])
        vec = sb("vec", [P, NVEC])
        c_in = sb("c_in", [P, KT, NB + 1])
        c_sp = sb("c_sp", [P, KT, 2, NB + 1], F32R)
        small = sb("small", [P, 40])
        eps = small[:, 39:40]
        mx4, nm4, den4, rden4 = ([small[:, 8 * k + 4 * e:8 * k + 4 * e + 4] for e in range(2)] for k in range(4))
        mxs, dens, rdens, nms = small[:, 32:34], small[:, 34:36], small[:, 36:38], small[:, 38:39]
        with nc.sbuf_tensor("kc", [P, 2, CT, PAST], F32) as kc, nc.sbuf_tensor("vc", [P, 2, PAST // P, DA], F32) as vc:
            pass
        h_hi = sb("h_hi", [P, KT, T], F32R)
        h_lo = sb("h_lo", [P, KT, T], F32R)
        with ExitStack() as a:
            qk = sb("qk", [P, 2 * CT, T], where=a)
            vT = sb("vT", [P, CT, T], where=a)
            vnat = sb("vnat", [P, QB + 1, DA], where=a)
            uP = sb("uP", [P, CT, HIST + SEQ], where=a)
            uS = sb("uS", [P, CT, NB, HIST + NT], where=a)
            y = sb("y", [P, CT, T], where=a)
            oT = sb("oT", [P, CT, T], where=a)
            with ExitStack() as b:
                sg = sb("sg", [P, T], where=b)
                zraw = sb("zraw", [P, 2, T], where=b)
                zcos = sb("zcos", [P, 2, T], where=b)
                zswap = sb("zswap", [P, T], where=b)
            with ExitStack() as b:
                E = sb("E", [P, 2, E_ALL], where=b)
                PT = sb("PT", [P, 2, E_ALL], where=b)
                Es = sb("Es", [P, T], where=b)
                PTs = sb("PTs", [P, QB + 1, P], where=b)
                Os = sb("Os", [P, DA], where=b)
                Qbd = sb("Qbd", [P, 2, CT, NH * NT], where=b)
                Qst = sb("Qst", [P, T], where=b)
                Kst = sb("Kst", [P, SEQ], where=b)
                Vst = sb("Vst", [P, QB, P], where=b)
                uPst = sb("uPst", [P, HIST + SEQ], where=b)
                uSst = sb("uSst", [P, NB, HIST + NT], where=b)
                cwst = sb("cwst", [P, CW + 1], where=b)
                yst = sb("yst", [P, T], where=b)
                mnst = sb("mnst", [P, 2, NS], where=b)
            with ExitStack() as b:
                sqm = sb("sqm", [P, CT, T], where=b)
                meanm = sb("meanm", [P, T], where=b)
                sdm = sb("sdm", [P, T], where=b)
                rstdm = sb("rstdm", [P, T], where=b)
                mt = sb("mt", [P, 2, T], where=b)
                gm = sb("gm", [P, 2, T], where=b)
        with ExitStack() as a:
            a_hi = sb("a_hi", [P, FT, T], F32R, where=a)
            a_lo = sb("a_lo", [P, FT, T], F32R, where=a)
            gate = sb("gate", [P, T], where=a)
            af = sb("af", [P, T], where=a)
        with ExitStack() as a:
            sq = sb("sq", [P, KT, T], where=a)
            mean = sb("mean", [P, T], where=a)
            sd = sb("sd", [P, T], where=a)
            rstd = sb("rstd", [P, T], where=a)
            hf = sb("hf", [P, 2, SEQ], where=a)
            hs = sb("hs", [P, KT, NS], where=a)
        ps = ctx.enter_context(nc.psum_tensor("ps", [P, 8, 512], F32))
        Z = [ps[:, 0:2, 0:H], ps[:, 2:4, 0:H]]
        STAT = [ps[:, 4:6, 0:H], ps[:, 6:8, 0:H]]

        def halves(t):
            return t.rearrange("p (h n) -> p h n", h=2)

        def by_seq(t):
            return t.rearrange("p (b t) -> p b t", b=NB)

        def unit(l, base, i, s, u):
            return u % 2, l * UL + i * s + (base + u), l * (UL // 2) + i * (s // 2) + (base // 2 + u // 2)

        consts = [(x[:], xT), (c_in[:], cT), (eye[:], eye_d), (rope[:], rope_d), (mp[:], mp_d), (msc[:], msc_d), (msn[:], msn_d)]
        s = sems
        block = ctx.enter_context(nc.Block())

        @block.sync
        def _(sp):
            for name, n in FREE.items():
                sp.sem_inc(s[name], n)
            sp.sem_inc(s["z_free1"], 1)
            for dst, src in consts:
                sp.dma_start(dst, src).then_inc(s["consts"], 16)

            def fetch(l, base, i, st, u, src, n=UNIT):
                j, seq, _ = unit(l, base, i, st, u)
                sp.wait_ge(s["lo_ready"], seq + 1)
                sp.dma_start(w_raw[:, j, 0:n], src).then_inc(w_in[j], 16)

            with sp.Fori(0, DEPTH) as l:
                sp.wait_ge(s["ln_done"], slot(l, "ln_done", 0))
                sp.dma_start(vec[:], vec_d[l]).then_inc(s["vec_in"], 16)
                with sp.Fori(0, N_ADA // 2) as i:
                    for u in range(2):
                        fetch(l, ADA0, i, 2, u, w_ada[l, i * 2 + u])
                with sp.Fori(0, N_IN // 2) as i:
                    for u in range(2):
                        fetch(l, IN0, i, 2, u, w_mix[l, i * 2 + u])
                for u in range(2):
                    fetch(l, OUT0, 0, 2, u, w_mix[l, N_IN + u])
                behind(sp, s["w_used"], nth(l, "w_used", OUT0 - 1))
                with sp.Fori(0, CT) as i:
                    sp.wait_ge(s["samp_done"], l * CT + i + 1)
                    for b in range(2):
                        sp.dma_start(kc[:, b], kc_d[l, i * 2 + b]).then_inc(kc_in[b], 16)
                        sp.dma_start(vc[:, b], vc_d[l, i * 2 + b]).then_inc(vc_in[b], 16)
                with sp.Fori(1, N_OUT // 2) as i:
                    for u in range(2):
                        fetch(l, OUT0, i, 2, u, w_mix[l, i * 2 + (N_IN + u)])
                with sp.Fori(0, N_GU // 2) as i:
                    for u in range(2):
                        fetch(l, GU0, i, 2, u, w_mix[l, i * 2 + (N_IN + N_OUT + u)])
                with sp.Fori(0, KT // 2) as i:
                    for u in range(6):
                        k0 = sum(DN_K[:u % 3]) * P
                        n = DN_K[u % 3] * P
                        fetch(l, DN0, i, 6, u, w_dn[l, i * 2 + u // 3, :, k0:k0 + n], n)
            sp.wait_ge(s["ln_done"], 2 * KT * DEPTH + 1)
            sp.dma_start(y_d, x[:]).then_inc(s["y_st"], 16)
            sp.wait_ge(s["y_st"], 16)
            sp.wait_ge(s["k_st"], 16 * DEPTH)
            sp.wait_ge(s["v_st"], 16 * DEPTH)
            sp.wait_ge(s["cv_st"], 32 * DEPTH)

        @block.gpsimd
        def _(pool):
            st = Steps(pool, s["pool_steps"])
            with pool.Fori(0, DEPTH) as l:
                behind(pool, s["w_used"], nth(l, "w_used", IN0))
                pool.dma_start(uS[:, :, :, 0:HIST], st_d[l]).then_inc(s["hist"], 16)
                nc.gpsimd.memset(uP[:, :, 0:HIST], 0.0).then_inc(s["hist_zero"], 1)
                with pool.Fori(0, CT) as i:
                    for j in range(2):
                        pool.wait_ge(z_free[j], l * ZL + i + (CT + 2))
                        pool.wait_ge(s["rope_done"], l * 2 * CT + i * 2 + (j + 1))
                        nc.gpsimd.tensor_tensor(zcos[:, j, :], zraw[:, j, :], rope[:, 0, :], ALU.mult)\
                            .then_inc(s["rope_cos"], 1)
                behind(pool, s["rope_done"], nth(l, "rope_done", 2 * CT - 1))
                pool.dma_start(k_d[l], qk[:, CT:2 * CT, :]).then_inc(s["k_st"], 16)
                for j in range(2):
                    behind(pool, z_free[j], l * ZL + (Z_OUT + 1))
                pool.dma_start(v_d[l], vT[:]).then_inc(s["v_st"], 16)
                pool.dma_start(cp_d[l], uP[:, :, SEQ:SEQ + HIST]).then_inc(s["cv_st"], 16)
                behind(pool, s["hist"], l * 16 + 16)
                pool.dma_start(cs_d[l], uS[:, :, :, NT:NT + HIST]).then_inc(s["cv_st"], 16)
                pool.wait_ge(s["vnat_ready"], nth(l, "vnat_ready", QB))
                behind(pool, s["hist_zero"], l + 1)
                st.link(nc.gpsimd.memset(Qbd[:], 0.0))
                st.restart()
                with pool.Fori(0, CT) as i:
                    pool.wait_ge(s["samp_done"], l * CT + i + 1)
                    pool.wait_ge(s["conv_done"], l * CT + i + 1)
                    st.of(nc.gpsimd.tensor_copy(Qst[:], qk[:, i, :]))
                    st.of(nc.gpsimd.tensor_copy(Kst[:], qk[:, i + CT, 0:SEQ]))
                    st.of(nc.gpsimd.tensor_copy(Vst[:], vnat[:, 0:QB, bass.ds(i * P, P)]))
                    for e in range(2):
                        st.wait(st.n)
                        own = Qbd[e * HD:(e + 1) * HD, 0, 0, e * NT:]
                        own = bass.AP(own.tensor, own.offset, [list(own.ap[0]), [CT * NH * NT, 2], [NH * NT + 2 * NT, CT], [1, NT]])
                        st.of(nc.gpsimd.tensor_copy(
                            own, qk[e * HD:(e + 1) * HD, 0:CT, bass.ds(i * 2 * NT + SEQ, 2 * NT)]
                            .rearrange("p c (b t) -> p b c t", b=2)))
                    st.wait(st.n)
                    st.of(nc.gpsimd.tensor_copy(mnst[:], msn[:, i]))
                    st.wait(st.n)
                    pool.sem_inc(s["staged"], 1)
                    st.of(nc.gpsimd.tensor_copy(uPst[:], uP[:, i, :]))
                    st.of(nc.gpsimd.tensor_copy(uSst[:], uS[:, i]))
                    st.of(nc.gpsimd.tensor_copy(cwst[:, 0:CW], vec[:, bass.ds(i * CW + V_CW, CW)]))
                    st.of(nc.gpsimd.tensor_copy(cwst[:, CW:CW + 1], vec[:, bass.ds(i + V_CB, 1)]))
                    st.wait(st.n)
                    pool.sem_inc(s["conv_staged"], 1)
                    st.restart()

        Z_OF = {IN0: Z_IN, OUT0: Z_OUT, GU0: Z_GU, DN0: Z_DN}

        def z_taken(l, i, z0):
            return l * ZL + i + (z0 + 2)

        def z_before(l, i, z0):
            return l * ZL + i + (z0 + 1)

        @block.scalar
        def _(act):
            st = Steps(act, s["act_steps"])

            def split(l, base, i, n, u):
                j, seq, half = unit(l, base, i, n, u)
                act.wait_ge(w_in[j], half * 16 + 16)
                act.wait_ge(s["w_used"], seq + 1)
                nc.scalar.activation(w_hi[:, j, :], w_raw[:, j, :], ACT.Copy).then_inc(s["hi_ready"], 1)

            def computed(l, base, i, n, u):
                act.wait_ge(s["w_used"], unit(l, base, i, n, u)[1] + 3)

            def h_parts(l, q):
                for kt in range(KT):
                    act.wait_ge(s["h_f"], nth(l, "h_f", q * KT + kt))
                    nc.scalar.activation(h_hi[:, kt, 0:SEQ], hf[:, kt % 2, :], ACT.Copy).then_inc(s["h_hi"], 1)
                act.wait_ge(s["hs_f"], nth(l, "hs_f", q))
                nc.scalar.activation(h_hi[:, :, SEQ:T], hs[:], ACT.Copy).then_inc(s["hs_hi"], 1)

            def gated(l, dst, u, m, g):
                scale = mod[:, bass.ds(m + g, 1), 0] if not isinstance(m, int) else mod[:, m + g, 0:1]
                nc.scalar.activation(dst[:, 0:H], Z[u][:, 0], ACT.Copy, scale=scale).then_inc(s["gm_act"], 1)
                nc.scalar.activation(dst[:, H:SEQ], Z[u][:, 1, 0:HP_], ACT.Copy, scale=scale).then_inc(s["gm_act"], 1)

            def norm(l, q):
                act.wait_ge(s["ln_sum"], nth(l, "ln_sum", q))
                nc.scalar.activation(halves(mean[:]), STAT[0], ACT.Copy, scale=1.0 / D).then_inc(s["ln_mean"], 1)
                for c in range(2):
                    act.wait_ge(s["ln_cent"], nth(l, "ln_cent", 2 * q + c))
                    part = slice(c * KT // 2, (c + 1) * KT // 2)
                    nc.scalar.activation(sq[:, part], x[:, part], ACT.Square).then_inc(s["ln_sq"], 1)
                act.wait_ge(s["ln_var"], nth(l, "ln_var", q))
                nc.scalar.activation(halves(sd[:]), STAT[1], ACT.Sqrt, scale=1.0 / D, bias=eps).then_inc(s["ln_sd"], 1)

            act.wait_ge(s["consts"], 16 * len(consts))
            st.link(nc.scalar.activation(c_in[:], c_in[:], ACT.Silu))
            st.of(nc.scalar.activation(c_sp[:, :, 0, :], c_in[:], ACT.Copy))
            st.wait(st.n)
            act.sem_inc(s["c_ready"], 1)
            st.restart()
            with act.Fori(0, DEPTH) as l:
                split(l, ADA0, 0, 2, 0)
                with act.Fori(0, N_ADA // 2) as i:
                    for u in range(2):
                        split(l, ADA0, i, 2, u + 1)
                h_parts(l, 0)
                nc.scalar.preload_act_table(ACT.Sigmoid)
                with act.Fori(0, CT) as i:
                    split(l, IN0, i, 2, 1)
                    computed(l, IN0, i, 2, 0)
                    act.wait_ge(z_free[1], z_before(l, i, Z_IN))
                    nc.scalar.activation(halves(sg[:]), Z[0], ACT.Sigmoid).then_inc(z_free[0], 1)
                    split(l, IN0, i, 2, 2)
                with act.Fori(0, CT) as i:
                    for u in range(2):
                        split(l, IN0 + 2 * CT, i, 2, u + 1)
                        computed(l, IN0 + 2 * CT, i, 2, u)
                        act.wait_ge(s["rope_done"], l * 2 * CT + i * 2 + (u + 1))
                        nc.scalar.activation(halves(zraw[:, u]), Z[u], ACT.Copy).then_inc(z_free[u], 1)
                with act.Fori(0, CT // 2) as i:
                    for u in range(2):
                        split(l, IN0 + 4 * CT, i, 2, u + 1)
                        computed(l, IN0 + 4 * CT, i, 2, u)
                        nc.scalar.activation(halves(vT[:, i * 2 + u]), Z[u], ACT.Copy).then_inc(z_free[u], 1)
                for t in range(QB + 1):
                    rows = P if t < QB else NS
                    act.wait_ge(s["vt_ps"], nth(l, "vt_ps", t))
                    nc.scalar.activation(vnat[0:rows, t, :], ps[0:rows, 4 + t % 4, :], ACT.Copy).then_inc(s["vnat_ready"], 1)
                nc.scalar.preload_act_table(ACT.Exp)
                with act.Fori(0, CT) as i:
                    def exps(e):
                        act.wait_ge(s["nm_ready"], l * NH + i * 2 + (e + 1))
                        for q in range(QB):
                            blk = E[:, e, E_OFF[q]:E_OFF[q] + (q + 1) * P]
                            nc.scalar.activation(blk, blk, ACT.Exp, bias=nm4[e][:, q:q + 1], scale=SCALE)\
                                .then_inc(s["exp_ready"], 1)

                    exps(0)
                    act.wait_ge(s["nms_ready"], l * CT + i + 1)
                    nc.scalar.activation(Es[:], Es[:], ACT.Exp, bias=nms, scale=SCALE).then_inc(s["exps_ready"], 1)
                    exps(1)
                    for e in range(2):
                        for k in range(QB):
                            n = (QB - k) * P
                            act.wait_ge(s["pt_ps"], (l * NH + i * 2) * QB + (e * QB + k + 1))
                            nc.scalar.activation(PT[:, e, PT_OFF[k]:PT_OFF[k] + n], ps[:, k % 2, 0:n], ACT.Copy)\
                                .then_inc(s["pt_ready"], 1)
                    act.wait_ge(s["o_ps"], l * CT + i + 1)
                    nc.scalar.activation(oT[:, i, 0:SEQ], ps[:, 2, :], ACT.Copy).then_inc(s["o_free"], 1)
                    act.wait_ge(s["pts_ps"], l * CT + i + 1)
                    nc.scalar.activation(PTs[:, 0:QB, :], ps[:, 3, :].rearrange("p (k n) -> p k n", k=QB), ACT.Copy)\
                        .then_inc(s["pts_ready"], 1)
                    nc.scalar.activation(PTs[0:NS, QB, :], ps[0:NS, 7, 0:P], ACT.Copy).then_inc(s["pts_ready"], 1)
                    act.wait_ge(s["os_ps"], l * CT + i + 1)
                    nc.scalar.activation(Os[:], ps[:, 3, :], ACT.Copy).then_inc(s["os_ready"], 1)
                    act.wait_ge(s["ost_ps"], l * CT + i + 1)
                    for e in range(2):
                        own = ps[e * HD:(e + 1) * HD, 7, e * NT:]
                        own = bass.AP(own.tensor, own.offset, [list(own.ap[0]), [P + 2 * NT, CT], [NH * NT, 2], [1, NT]])
                        nc.scalar.activation(
                            oT[e * HD:(e + 1) * HD, :, bass.ds(i * 2 * NT + SEQ, 2 * NT)]
                            .rearrange("p c (b t) -> p c b t", b=2), own, ACT.Copy).then_inc(s["o_done"], 1)

                def root(q, src):
                    act.wait_ge(s["m_var"], nth(l, "m_var", q))
                    nc.scalar.activation(halves(sdm[:]), STAT[1], ACT.Sqrt, scale=1.0 / DA, bias=eps).then_inc(s["m_sd"], 1)

                def m_parts(q):
                    for c in range(CT):
                        act.wait_ge(s["m_f"], nth(l, "m_f", q * CT + c))
                        nc.scalar.activation(h_hi[:, q * CT + c, :], mt[:, c % 2, :], ACT.Copy).then_inc(s["m_hi"], 1)

                act.wait_ge(s["o_done"], nth(l, "o_done", 2 * CT - 1))
                act.wait_ge(s["samp_done"], nth(l, "samp_done", CT - 1))
                act.wait_ge(s["o_free"], nth(l, "o_free", CT - 1))
                act.wait_ge(s["conv_done"], nth(l, "conv_done", CT - 1))
                nc.scalar.activation(sqm[:], oT[:], ACT.Square).then_inc(s["m_sq"], 1)
                root(0, None)
                m_parts(0)
                act.wait_ge(s["m_sum"], l + 1)
                nc.scalar.activation(halves(meanm[:]), STAT[0], ACT.Copy, scale=1.0 / DA).then_inc(s["m_mean"], 1)
                act.wait_ge(s["m_cent"], l + 1)
                nc.scalar.activation(sqm[:], y[:], ACT.Square).then_inc(s["m_sq"], 1)
                root(1, None)
                act.wait_ge(s["m_norm"], l + 1)
                for c in range(CT):
                    nc.scalar.activation(y[:, c, :], y[:, c, :], ACT.Silu, scale=vec[:, V_CG + c:V_CG + c + 1],
                                         bias=vec[:, V_CLB + c:V_CLB + c + 1]).then_inc(s["cz"], 1)
                act.wait_ge(s["cz"], nth(l, "cz", CT - 1))
                nc.scalar.activation(sqm[:], y[:], ACT.Square).then_inc(s["m_sq"], 1)
                root(2, None)
                m_parts(1)
                with act.Fori(0, N_OUT // 2) as i:
                    for u in range(2):
                        split(l, OUT0, i, 2, u + 1)
                        computed(l, OUT0, i, 2, u)
                        act.wait_ge(z_free[u], z_before(l, i, Z_OUT))
                        gated(l, gm[:, u], u, i * 2 + u, G1)
                act.wait_ge(s["k_st"], l * 16 + 16)
                act.wait_ge(s["v_st"], l * 16 + 16)
                act.wait_ge(s["cv_st"], l * 32 + 32)
                norm(l, 0)
                h_parts(l, 1)
                nc.scalar.preload_act_table(ACT.Silu)
                with act.Fori(0, FT) as i:
                    split(l, GU0, i, 2, 1)
                    computed(l, GU0, i, 2, 0)
                    act.wait_ge(z_free[1], z_before(l, i, Z_GU))
                    nc.scalar.activation(halves(gate[:]), Z[0], ACT.Silu).then_inc(z_free[0], 1)
                    split(l, GU0, i, 2, 2)
                    act.wait_ge(z_free[1], z_taken(l, i, Z_GU))
                    nc.scalar.activation(a_hi[:, i], af[:], ACT.Copy).then_inc(s["a_hi"], 1)

                def down(i, last):
                    for u in range(6):
                        if not (last and u == 5):
                            split(l, DN0, i, 6, u + 1)
                        if u % 3 == 2:
                            computed(l, DN0, i, 6, u)
                            act.wait_ge(z_free[u // 3], z_before(l, i, Z_DN))
                            gated(l, (gate, af)[u // 3], u // 3, i * 2 + u // 3, G2)

                with act.Fori(0, KT // 2 - 1) as i:
                    down(i, False)
                down(KT // 2 - 1, True)
                norm(l, 1)

        @block.vector
        def _(dve):
            st = Steps(dve, s["dve_steps"])

            def split(l, base, i, n, u):
                j, seq, _ = unit(l, base, i, n, u)
                dve.wait_ge(s["hi_ready"], seq + 1)
                nc.vector.tensor_tensor(w_lo[:, j, :], w_raw[:, j, :], w_hi[:, j, :].bitcast(F32), ALU.subtract)\
                    .then_inc(s["lo_ready"], 1)

            def computed(l, base, i, n, u):
                dve.wait_ge(s["w_used"], unit(l, base, i, n, u)[1] + 3)

            def per_seq(j):
                return mod[:, j:j + KT, 1:].unsqueeze(3).to_broadcast([P, KT, NB, NT])

            def modulate(l, q, sh, sc):
                hs4 = hs[:].rearrange("p k (b t) -> p k b t", b=NB)
                xs4 = x[:, :, SEQ:T].rearrange("p k (b t) -> p k b t", b=NB)
                st.link(nc.vector.tensor_tensor(hs4, xs4, per_seq(sc), ALU.mult))
                nc.vector.tensor_tensor(hs4, hs4, per_seq(sh), ALU.add).then_inc(s["hs_f"], 1)
                for kt in range(KT + 1):
                    if kt < KT:
                        if kt >= 2:
                            dve.wait_ge(s["h_lo"], nth(l, "h_lo", q * (KT + 1) + kt - 2))
                        nc.vector.tensor_scalar(hf[:, kt % 2, :], x[:, kt, 0:SEQ], mod[:, sc + kt, 0:1],
                                                mod[:, sh + kt, 0:1], ALU.mult, ALU.add).then_inc(s["h_f"], 1)
                    if kt:
                        k = kt - 1
                        dve.wait_ge(s["h_hi"], nth(l, "h_hi", q * KT + k))
                        nc.vector.tensor_tensor(h_lo[:, k, 0:SEQ], hf[:, k % 2, :], h_hi[:, k, 0:SEQ].bitcast(F32),
                                                ALU.subtract).then_inc(s["h_lo"], 1)
                dve.wait_ge(s["hs_hi"], nth(l, "hs_hi", q))
                nc.vector.tensor_tensor(h_lo[:, :, SEQ:T], hs[:], h_hi[:, :, SEQ:T].bitcast(F32), ALU.subtract)\
                    .then_inc(s["h_lo"], 1)

            def residual(l, dst, u, i, m, g, z0, done_gm):
                out4 = Z[u][:, 1, HP_:H].rearrange("p (b t) -> p b t", b=NB)
                gs = mod[:, bass.ds(m + g, 1), 1:].rearrange("p o b -> p (o b)") if not isinstance(m, int) else mod[:, m + g, 1:]
                dve.wait_ge(s["gm_act"], done_gm)
                st.link(nc.vector.tensor_tensor(by_seq(dst[:, SEQ:T]), out4, gs.unsqueeze(2).to_broadcast([P, NB, NT]), ALU.mult))
                nc.vector.scalar_tensor_tensor(out=x[:, m, :], in0=x[:, m, :], scalar=ALPHA, in1=dst,
                                               op0=ALU.mult, op1=ALU.add).then_inc(z_free[u], 1)

            def norm(l, q, g, b):
                dve.wait_ge(s["ln_mean"], nth(l, "ln_mean", q))
                half = KT // 2
                for c in range(2):
                    part = x[:, c * half:(c + 1) * half]
                    nc.vector.tensor_tensor(part, part, mean[:].unsqueeze(1).to_broadcast([P, half, T]), ALU.subtract)\
                        .then_inc(s["ln_cent"], 1)
                dve.wait_ge(s["ln_sd"], nth(l, "ln_sd", q))
                st.link(nc.vector.reciprocal(rstd[:], sd[:]))
                for c in range(2):
                    part = x[:, c * half:(c + 1) * half]
                    st.of(nc.vector.tensor_tensor(part, part, rstd[:].unsqueeze(1).to_broadcast([P, half, T]), ALU.mult))
                st.wait(st.n)
                for kt in range(KT):
                    nc.vector.tensor_scalar(x[:, kt, :], x[:, kt, :], vec[:, g + kt:g + kt + 1], vec[:, b + kt:b + kt + 1],
                                            ALU.mult, ALU.add).then_inc(s["ln_done"], 1)
                behind(dve, s["ln_done"], nth(l, "ln_done", (q + 1) * KT - 1))
                st.restart()

            st.of(nc.vector.memset(ones[:], 1.0))
            st.of(nc.vector.memset(eps, EPS))
            dve.wait_ge(s["c_ready"], 1)
            nc.vector.tensor_tensor(c_sp[:, :, 1, :], c_in[:], c_sp[:, :, 0, :].bitcast(F32), ALU.subtract)\
                .then_inc(s["c_ready"], 1)
            st.restart()
            with dve.Fori(0, DEPTH) as l:
                split(l, ADA0, 0, 2, 0)
                with dve.Fori(0, N_ADA // 2) as i:
                    for u in range(2):
                        split(l, ADA0, i, 2, u + 1)
                        computed(l, ADA0, i, 2, u)
                        nc.vector.tensor_reduce(
                            mod[:, bass.ds(i * 2 + u, 1), :].rearrange("p o c -> p (o c)"),
                            ps[:, 4 + u, 0:2 * (NB + 1)].rearrange("p (s c) -> p c s", s=2), AX.X, ALU.add)\
                            .then_inc(s["ada_out"], 1)
                dve.wait_ge(s["vec_in"], l * 16 + 16)
                dve.wait_ge(s["ada_out"], nth(l, "ada_out", N_ADA - 1))
                st.link(nc.vector.tensor_tensor(mod[:], mod[:], vec[:, V_ADA:V_ADA + 6 * KT].unsqueeze(2)
                                                .to_broadcast([P, 6 * KT, NB + 1]), ALU.add))
                st.of(nc.vector.tensor_scalar(mod[:, SC1:SC1 + KT, :], mod[:, SC1:SC1 + KT, :], 1.0, None, ALU.add))
                st.of(nc.vector.tensor_scalar(mod[:, SC2:SC2 + KT, :], mod[:, SC2:SC2 + KT, :], 1.0, None, ALU.add))
                st.wait(st.n)
                modulate(l, 0, SH1, SC1)
                st.restart()
                with dve.Fori(0, CT) as i:
                    split(l, IN0, i, 2, 1)
                    split(l, IN0, i, 2, 2)
                    computed(l, IN0, i, 2, 1)
                    dve.wait_ge(z_free[0], z_taken(l, i, Z_IN))
                    st.of(nc.vector.tensor_tensor(uP[:, i, HIST:HIST + H], Z[1][:, 0], sg[:, 0:H], ALU.mult))
                    st.of(nc.vector.tensor_tensor(uP[:, i, HIST + H:HIST + SEQ], Z[1][:, 1, 0:HP_], sg[:, H:SEQ], ALU.mult))
                    st.restart()
                    nc.vector.tensor_tensor(uS[:, i, :, HIST:HIST + NT], by_seq(Z[1][:, 1, HP_:H]), by_seq(sg[:, SEQ:T]),
                                            ALU.mult).then_inc(z_free[1], 1)
                with dve.Fori(0, CT) as i:
                    for u in range(2):
                        split(l, IN0 + 2 * CT, i, 2, u + 1)
                        behind(dve, z_free[u], z_taken(l, i, Z_IN + CT))
                        st.link(nc.vector.stream_shuffle(zswap[:], zraw[:, u, :], SWAP))
                        st.link(nc.vector.tensor_tensor(zswap[:], zswap[:], rope[:, 1, :], ALU.mult))
                        dve.wait_ge(s["rope_cos"], l * 2 * CT + i * 2 + (u + 1))
                        nc.vector.tensor_tensor(qk[:, i * 2 + u, :], zcos[:, u, :], zswap[:], ALU.add)\
                            .then_inc(s["rope_done"], 1)
                        behind(dve, s["rope_done"], l * 2 * CT + i * 2 + (u + 3))
                        st.restart()
                with dve.Fori(0, CT // 2) as i:
                    for u in range(2):
                        split(l, IN0 + 4 * CT, i, 2, u + 1)
                with dve.Fori(0, CT) as i:
                    def head_max(e):
                        for q in range(QB):
                            w = (q + 1) * P
                            if q != 1:
                                behind(dve, s["s_ps"], l * 3 * NH + i * 6 + (3 * e + max(q, 1)))
                            bank, o = S_BANK[q]
                            nc.vector.tensor_tensor_reduce(E[:, e, E_OFF[q]:E_OFF[q] + w], ps[:, bank, o:o + w],
                                                           mp[:, 0, SEQ - w:SEQ], 1.0, LEAST, ALU.add, ALU.max,
                                                           mx4[e][:, q:q + 1]).then_inc(s["s_free"], 1)
                        dve.wait_ge(s["s_free"], (l * NH + i * 2) * QB + ((e + 1) * QB + FREE["s_free"]))
                        nc.vector.tensor_scalar(nm4[e], mx4[e], -SCALE, None, ALU.mult).then_inc(s["nm_ready"], 1)

                    def head_prob(e):
                        for q in range(QB):
                            blk = E[:, e, E_OFF[q]:E_OFF[q] + (q + 1) * P]
                            behind(dve, s["exp_ready"], (l * NH + i * 2) * QB + (e * QB + q + 1))
                            st.of(nc.vector.tensor_tensor_reduce(blk, blk, mp[:, 1, SEQ - (q + 1) * P:SEQ], 1.0, 0.0, ALU.mult,
                                                                 ALU.add, den4[e][:, q:q + 1]))
                        st.wait(st.n)
                        st.link(nc.vector.reciprocal(rden4[e], den4[e]))
                        for q in range(QB):
                            blk = E[:, e, E_OFF[q]:E_OFF[q] + (q + 1) * P]
                            nc.vector.tensor_scalar(blk, blk, rden4[e][:, q:q + 1], None, ALU.mult).then_inc(s["p_ready"], 1)

                    behind(dve, s["samp_done"], slot(l, "samp_done", 0) + i)
                    head_max(0)
                    behind(dve, s["ss_ps"], l * CT + i + 1)
                    behind(dve, s["staged"], l * CT + i + 1)
                    st.link(nc.vector.tensor_tensor_reduce(Es[:, 0:PAST], ps[:, 3, :], msc[:, 0], 1.0, LEAST, ALU.add, ALU.max,
                                                           mxs[:, 0:1]))
                    st.link(nc.vector.tensor_tensor_reduce(Es[:, PAST:T], ps[:, 7, 0:NS], mnst[:, 0], 1.0, mxs[:, 0:1], ALU.add,
                                                           ALU.max, mxs[:, 1:2]))
                    nc.vector.tensor_scalar(nms, mxs[:, 1:2], -SCALE, None, ALU.mult).then_inc(s["nms_ready"], 1)
                    head_max(1)
                    head_prob(0)
                    behind(dve, s["exps_ready"], l * CT + i + 1)
                    st.link(nc.vector.tensor_tensor_reduce(Es[:, 0:PAST], Es[:, 0:PAST], msc[:, 1], 1.0, 0.0, ALU.mult, ALU.add,
                                                           dens[:, 0:1]))
                    st.link(nc.vector.tensor_tensor_reduce(Es[:, PAST:T], Es[:, PAST:T], mnst[:, 1], 1.0, dens[:, 0:1], ALU.mult,
                                                           ALU.add, dens[:, 1:2]))
                    st.link(nc.vector.reciprocal(rdens[:, 0:1], dens[:, 1:2]))
                    nc.vector.tensor_scalar(Es[:], Es[:], rdens[:, 0:1], None, ALU.mult).then_inc(s["ps_ready"], 1)
                    head_prob(1)
                    behind(dve, s["conv_staged"], l * CT + i + 1)
                    yp, ys = yst[:, 0:SEQ], by_seq(yst[:, SEQ:T])
                    for w in range(CW):
                        up, us, tap = uPst[:, w:w + SEQ], uSst[:, :, w:w + NT], cwst[:, w:w + 1]
                        if w == 0:
                            st.of(nc.vector.tensor_scalar(yp, up, tap, cwst[:, CW:CW + 1], ALU.mult, ALU.add))
                            st.of(nc.vector.tensor_scalar(ys, us, tap, cwst[:, CW:CW + 1], ALU.mult, ALU.add))
                            continue
                        op, os_ = (yp, ys) if w < CW - 1 else (y[:, i, 0:SEQ], by_seq(y[:, i, SEQ:T]))
                        st.wait(st.n - 1)
                        st.of(nc.vector.scalar_tensor_tensor(out=op, in0=up, scalar=tap, in1=yp, op0=ALU.mult, op1=ALU.add))
                        st.wait(st.n - 1)
                        st.of(nc.vector.scalar_tensor_tensor(out=os_, in0=us, scalar=tap, in1=ys, op0=ALU.mult, op1=ALU.add))
                    st.restart()
                    dve.sem_inc(s["conv_done"], 1)

                def scaled(q, src, beta):
                    dve.wait_ge(s["m_sd"], nth(l, "m_sd", 0 if q == 0 else 2))
                    st.link(nc.vector.reciprocal(rstdm[:], sdm[:]))
                    for c in range(CT + 1):
                        if c < CT:
                            if c >= 2 or q:
                                dve.wait_ge(s["m_lo"], nth(l, "m_lo", q * CT + c - 2))
                            nc.vector.scalar_tensor_tensor(out=mt[:, c % 2, :], in0=src[:, c, :], scalar=vec[:, beta + c:beta + c + 1],
                                                           in1=rstdm[:], op0=ALU.mult, op1=ALU.mult).then_inc(s["m_f"], 1)
                        if c:
                            k = c - 1
                            dve.wait_ge(s["m_hi"], nth(l, "m_hi", q * CT + k))
                            nc.vector.tensor_tensor(h_lo[:, q * CT + k, :], mt[:, k % 2, :], h_hi[:, q * CT + k, :].bitcast(F32),
                                                    ALU.subtract).then_inc(s["m_lo"], 1)

                scaled(0, oT, V_BA)
                dve.wait_ge(s["m_mean"], l + 1)
                nc.vector.tensor_tensor(y[:], y[:], meanm[:].unsqueeze(1).to_broadcast([P, CT, T]), ALU.subtract)\
                    .then_inc(s["m_cent"], 1)
                dve.wait_ge(s["m_lo"], nth(l, "m_lo", CT - 1))
                dve.wait_ge(s["m_sd"], nth(l, "m_sd", 1))
                st.link(nc.vector.reciprocal(rstdm[:], sdm[:]))
                nc.vector.tensor_tensor(y[:], y[:], rstdm[:].unsqueeze(1).to_broadcast([P, CT, T]), ALU.mult)\
                    .then_inc(s["m_norm"], 1)
                scaled(1, y, V_BC)
                st.restart()
                with dve.Fori(0, N_OUT // 2) as i:
                    for u in range(2):
                        split(l, OUT0, i, 2, u + 1)
                        computed(l, OUT0, i, 2, u)
                        residual(l, gm[:, u], u, i, i * 2 + u, G1, Z_OUT, l * 4 * KT + i * 4 + (2 * u + 2))
                    st.restart()
                norm(l, 0, V_G1, V_B1)
                modulate(l, 1, SH2, SC2)
                st.restart()
                with dve.Fori(0, FT) as i:
                    split(l, GU0, i, 2, 1)
                    split(l, GU0, i, 2, 2)
                    computed(l, GU0, i, 2, 1)
                    dve.wait_ge(z_free[0], z_taken(l, i, Z_GU))
                    dve.wait_ge(s["a_lo"], l * FT + i + FREE["a_lo"])
                    nc.vector.tensor_tensor(halves(af[:]), Z[1], halves(gate[:]), ALU.mult).then_inc(z_free[1], 1)
                    dve.wait_ge(s["a_hi"], l * FT + i + 1)
                    nc.vector.tensor_tensor(a_lo[:, i], af[:], a_hi[:, i].bitcast(F32), ALU.subtract).then_inc(s["a_lo"], 1)

                def down(i, last):
                    for u in range(6):
                        if not (last and u == 5):
                            split(l, DN0, i, 6, u + 1)
                        if u % 3 == 2:
                            j = u // 3
                            computed(l, DN0, i, 6, u)
                            residual(l, (gate, af)[j][:], j, i, i * 2 + j, G2, Z_DN, l * 4 * KT + i * 4 + (2 * KT + 2 * j + 2))
                    st.restart()

                with dve.Fori(0, KT // 2 - 1) as i:
                    down(i, False)
                down(KT // 2 - 1, True)
                norm(l, 1, V_G2, V_B2)

        @block.tensor
        def _(pe):
            def product(l, base, i, n, u, hi, lo, k0, nk, z, first=True, last=True):
                j, seq, _ = unit(l, base, i, n, u)
                pe.wait_ge(s["lo_ready"], seq + 3)
                for k in range(nk):
                    w = slice(k * P, (k + 1) * P)
                    for t, (a, b) in enumerate(((w_hi, hi), (w_lo, hi), (w_hi, lo))):
                        for h in range(2):
                            ins = nc.tensor.matmul(z[:, h], a[:, j, w], b[:, k0 + k, h * H:(h + 1) * H],
                                                   start=first and k == 0 and t == 0, stop=last and k == nk - 1 and t == 2)
                ins.then_inc(s["w_used"], 1)

            def column_sums(src, stat, tiles, start=True, stop=True):
                for h in range(2):
                    for k in tiles:
                        ins = nc.tensor.matmul(stat[:, h], ones[:], src[:, k, h * H:(h + 1) * H],
                                               start=start and k == tiles[0], stop=stop and k == tiles[-1])
                return ins

            def norm(l, q, z0):
                for j in range(2):
                    pe.wait_ge(z_free[j], l * ZL + (z0 + KT // 2 + 1))
                column_sums(x, STAT[0], range(KT)).then_inc(s["ln_sum"], 1)
                half = KT // 2
                for c in range(2):
                    pe.wait_ge(s["ln_sq"], nth(l, "ln_sq", 2 * q + c))
                    ins = column_sums(sq, STAT[1], range(c * half, (c + 1) * half), c == 0, c == 1)
                ins.then_inc(s["ln_var"], 1)

            pe.wait_ge(s["c_ready"], 2)
            pe.wait_ge(s["consts"], 16 * len(consts))
            with pe.Fori(0, DEPTH) as l:
                with pe.Fori(0, N_ADA // 2) as i:
                    for u in range(2):
                        j, seq, _ = unit(l, ADA0, i, 2, u)
                        pe.wait_ge(s["lo_ready"], seq + 3)
                        pe.wait_ge(s["ada_out"], l * N_ADA + i * 2 + (u + 1))
                        for k in range(KT):
                            for t, w in enumerate((w_hi, w_lo)):
                                ins = nc.tensor.matmul(ps[:, 4 + u, 0:2 * (NB + 1)], w[:, j, k * P:(k + 1) * P],
                                                       c_sp[:, k].rearrange("p s c -> p (s c)"),
                                                       start=k == 0 and t == 0, stop=k == KT - 1 and t == 1)
                        ins.then_inc(s["w_used"], 1)
                behind(pe, s["h_lo"], nth(l, "h_lo", KT))
                with pe.Fori(0, N_IN // 2) as i:
                    for u in range(2):
                        pe.wait_ge(z_free[u], z_before(l, i, Z_IN))
                        product(l, IN0, i, 2, u, h_hi, h_lo, 0, KT, Z[u])
                for j in range(2):
                    pe.wait_ge(z_free[j], l * ZL + (Z_OUT + 1))
                for t in range(QB + 1):
                    rows = P if t < QB else NS
                    if t == QB:
                        behind(pe, s["vnat_ready"], nth(l, "vnat_ready", 0))
                    for c in range(CT):
                        ins = nc.tensor.transpose(ps[0:rows, 4 + t % 4, c * P:(c + 1) * P], vT[:, c, t * P:t * P + rows], eye[:])
                    ins.then_inc(s["vt_ps"], 1)
                behind(pe, s["vnat_ready"], nth(l, "vnat_ready", QB))
                with pe.Fori(0, CT) as i:
                    def scores(e):
                        f = slice(e * HD, (e + 1) * HD)
                        pe.wait_ge(s["s_free"], (l * NH + i * 2) * QB + (e + 1) * QB)
                        for q in range(QB):
                            bank, o = S_BANK[q]
                            ins = nc.tensor.matmul(ps[:, bank, o:o + (q + 1) * P], Qst[f, q * P:(q + 1) * P],
                                                   Kst[f, 0:(q + 1) * P], start=True, stop=True)
                            if q:
                                ins.then_inc(s["s_ps"], 1)

                    def turn(e):
                        for k in range(QB):
                            pe.wait_ge(s["p_ready"], (l * NH + i * 2) * QB + (e + 1) * QB)
                            pe.wait_ge(s["pt_ready"], (l * NH + i * 2) * QB + (e * QB + k + 1))
                            for q in range(k, QB):
                                o = E_OFF[q] + k * P
                                ins = nc.tensor.transpose(ps[:, k % 2, (q - k) * P:(q - k + 1) * P], E[:, e, o:o + P], eye[:])
                            ins.then_inc(s["pt_ps"], 1)

                    def outputs(e):
                        f = slice(e * HD, (e + 1) * HD)
                        for k in range(QB):
                            n = (QB - k) * P
                            pe.wait_ge(s["pt_ready"], (l * NH + i * 2) * QB + (e * QB + k + 1 + FREE["pt_ready"]))
                            ins = nc.tensor.matmul(ps[f, 2, k * P:SEQ], Vst[:, k, f], PT[:, e, PT_OFF[k]:PT_OFF[k] + n],
                                                   start=k == 0, stop=k == QB - 1)
                        return ins

                    pe.wait_ge(s["staged"], l * CT + i + 1)
                    scores(0)
                    for b in range(2):
                        rows = slice(b * HD, (b + 1) * HD)
                        pe.wait_ge(kc_in[b], (l * CT + i) * 16 + 16)
                        for c in range(CT):
                            nc.tensor.matmul(ps[rows, 3, :], Qbd[:, b, c, :], kc[:, b, c, :], start=c == 0, stop=c == CT - 1)
                        for c in range(CT):
                            ins = nc.tensor.matmul(ps[rows, 7, 0:NS], Qbd[:, b, c, :], qk[:, CT + c, SEQ:T],
                                                   start=c == 0, stop=c == CT - 1)
                    ins.then_inc(s["ss_ps"], 1)
                    scores(1)
                    turn(0)
                    pe.wait_ge(s["o_free"], l * CT + i + 1)
                    outputs(0)
                    turn(1)
                    outputs(1).then_inc(s["o_ps"], 1)
                    pe.wait_ge(s["ps_ready"], l * CT + i + 1)
                    for k in range(QB):
                        nc.tensor.transpose(ps[:, 3, k * P:(k + 1) * P], Es[:, k * P:(k + 1) * P], eye[:])
                    nc.tensor.transpose(ps[0:NS, 7, 0:P], Es[:, PAST:T], eye[:]).then_inc(s["pts_ps"], 1)
                    pe.wait_ge(s["pts_ready"], (l * CT + i) * 2 + 2)
                    for b in range(2):
                        rows = slice(b * HD, (b + 1) * HD)
                        pe.wait_ge(vc_in[b], (l * CT + i) * 16 + 16)
                        for k in range(QB):
                            nc.tensor.matmul(ps[rows, 3, :], PTs[:, k, rows], vc[:, b, k, :], start=k == 0, stop=False)
                        ins = nc.tensor.matmul(ps[rows, 3, :], PTs[0:NS, QB, rows], vnat[0:NS, QB, :], start=False, stop=True)
                    ins.then_inc(s["os_ps"], 1)
                    pe.wait_ge(s["os_ready"], l * CT + i + 1)
                    for c in range(CT):
                        ins = nc.tensor.transpose(ps[:, 7, c * P:(c + 1) * P], Os[:, c * P:(c + 1) * P], eye[:])
                    ins.then_inc(s["ost_ps"], 1)
                    pe.wait_ge(s["o_done"], (l * CT + i) * 2 + 2)
                    pe.sem_inc(s["samp_done"], 1)
                for q in range(2):
                    pe.wait_ge(s["m_sq"], nth(l, "m_sq", q))
                    column_sums(sqm, STAT[1], range(CT)).then_inc(s["m_var"], 1)
                    if q == 0:
                        pe.wait_ge(s["conv_done"], nth(l, "conv_done", CT - 1))
                        column_sums(y, STAT[0], range(CT)).then_inc(s["m_sum"], 1)
                        pe.wait_ge(s["m_sd"], nth(l, "m_sd", 0))
                pe.wait_ge(s["m_sd"], nth(l, "m_sd", 1))
                pe.wait_ge(s["m_sq"], nth(l, "m_sq", 2))
                column_sums(sqm, STAT[1], range(CT)).then_inc(s["m_var"], 1)
                behind(pe, s["m_lo"], nth(l, "m_lo", 2 * CT - 1))
                with pe.Fori(0, N_OUT // 2) as i:
                    for u in range(2):
                        pe.wait_ge(z_free[u], z_before(l, i, Z_OUT))
                        product(l, OUT0, i, 2, u, h_hi, h_lo, 0, KT, Z[u])
                norm(l, 0, Z_OUT)
                behind(pe, s["h_lo"], nth(l, "h_lo", 2 * KT + 1))
                with pe.Fori(0, FT) as i:
                    for u in range(2):
                        pe.wait_ge(z_free[u], z_before(l, i, Z_GU))
                        product(l, GU0, i, 2, u, h_hi, h_lo, 0, KT, Z[u])
                behind(pe, s["a_lo"], nth(l, "a_lo", FT - 1))
                with pe.Fori(0, KT // 2) as i:
                    for u in range(6):
                        r = u % 3
                        if r == 0:
                            pe.wait_ge(z_free[u // 3], z_before(l, i, Z_DN))
                        product(l, DN0, i, 6, u, a_hi, a_lo, sum(DN_K[:r]), DN_K[r], Z[u // 3], r == 0, r == 2)
                norm(l, 1, Z_DN)


def kernel(**v):
    import concourse.bacc as bacc
    from concourse.bass_utils import run_bass_kernel_spmd

    f = np.float32
    v = {k: np.asarray(a) for k, a in v.items()}

    def fm(a):
        return a.T.reshape(-1, P, a.shape[0]).transpose(1, 0, 2)

    def tiles(w):
        k, m = w.shape
        return w.reshape(k // P, P, m // P, P).transpose(2, 1, 0, 3).reshape(m // P, P, k)

    mix = []
    for l in range(DEPTH):
        wi = tiles(v["w_in"][l])
        wg, wu = tiles(v["w_gate"][l]), tiles(v["w_up"][l])
        g0 = 3 * CT
        glu = [wi[g0 + k] for c in range(CT) for k in (CT + c, c)]
        mix.append(np.stack(glu + list(wi[:g0]) + list(tiles(v["w_out"][l])) + [t for p in zip(wg, wu) for t in p]))
    vecs = []
    for l in range(DEPTH):
        cols = [v["conv_w"][l].T.reshape(CT, P, CW).transpose(1, 0, 2).reshape(P, -1)]
        for name in ("conv_b", "conv_ln_g", "conv_ln_b", "beta_attn", "beta_conv", "ln1_g", "ln1_b", "ln2_g", "ln2_b", "b_ada"):
            cols.append(v[name][l].reshape(-1, P).T)
        vecs.append(np.concatenate(cols, axis=1))

    pos = np.concatenate([np.arange(SEQ), np.tile(PAST + np.arange(NT), NB)]).astype(f)
    half = HD // 8
    inv = np.power(f(500000.0), -np.arange(half, dtype=f) * f(2.0) / f(2 * half)).astype(f)
    ang = (pos[None, :] * inv[:, None]).astype(f).astype(np.float64)
    cos, sin = np.ones((P, T)), np.zeros((P, T))
    for h0 in (0, HD):
        cos[h0:h0 + half] = cos[h0 + half:h0 + 2 * half] = np.cos(ang)
        sin[h0:h0 + half], sin[h0 + half:h0 + 2 * half] = -np.sin(ang), np.sin(ang)
    rope = np.stack([cos, sin], axis=1).astype(f)

    def masks(diff, bound4=PAST):
        ok = diff >= 0
        n = (ok & (diff <= 128)).astype(f) + (ok & (diff % 4 == 0) & (diff <= bound4)) + (ok & (diff % 16 == 0))
        return np.stack([np.where(n > 0, f(0), f(NEG)), n], axis=1).astype(f)

    i = np.arange(P)[:, None]
    mp = masks(np.concatenate([d * P + i - np.arange(P)[None] for d in range(QB - 1, -1, -1)], axis=1))
    t = i % NT
    msc = masks(PAST + t - np.arange(PAST)[None])
    msn = []
    for pair in range(CT):
        key = np.arange(NS)[None]
        same = key // NT == 2 * pair + i // HD
        msn.append(masks(np.where(same, t - key % NT, -1)))
    msn = np.stack(msn, axis=1)

    x_all = np.concatenate([v["x_prompt"][0], v["x_sample"].reshape(NS, D)], axis=0)
    c_all = np.concatenate([v["c_prompt"], v["c_sample"]], axis=0)
    ck = v["cache_k"].reshape(DEPTH, NB, PAST, CT, P).transpose(0, 1, 4, 3, 2)
    cv = v["cache_v"].reshape(DEPTH, NB, PAST // P, P, DA).transpose(0, 1, 3, 2, 4)
    sc = v["state_conv"].reshape(DEPTH, NB, HIST, CT, P).transpose(0, 4, 3, 1, 2)
    ins = dict(
        xT=fm(x_all), cT=fm(c_all), w_ada=np.stack([tiles(w) for w in v["w_ada"]]), w_mix=np.stack(mix),
        w_dn=np.stack([tiles(w) for w in v["w_down"]]), kc_d=ck, vc_d=cv, st_d=sc, vec_d=np.stack(vecs), rope_d=rope,
        eye_d=np.eye(P, dtype=f), mp_d=mp, msc_d=msc, msn_d=msn)
    outs = dict(y_d=(P, KT, T), k_d=(DEPTH, P, CT, T), v_d=(DEPTH, P, CT, T), cp_d=(DEPTH, P, CT, HIST),
                cs_d=(DEPTH, P, CT, NB, HIST))
    nc = bacc.Bacc("TRN2", target_bir_lowering=False, num_devices=1)
    arrays, args = {}, {}
    for name, a in ins.items():
        arrays[name] = np.ascontiguousarray(a)
        args[name] = nc.dram_tensor(name, a.shape, F32, kind="ExternalInput").ap()
    for name, shape in outs.items():
        args[name] = nc.dram_tensor(name, shape, F32, kind="ExternalOutput").ap()
    trunk(nc, **args)
    r = run_bass_kernel_spmd(nc, [arrays], core_ids=[0]).results[0]

    def rows(a):
        a = np.moveaxis(a, -1, -3)
        return np.swapaxes(a, -1, -2).reshape(*a.shape[:-2], -1)

    yy, kk, vv = rows(r["y_d"]), rows(r["k_d"]), rows(r["v_d"])
    heads = (NH, HD)
    cp = r["cp_d"].transpose(0, 3, 2, 1).reshape(DEPTH, 1, HIST, DA)
    cs = r["cs_d"].transpose(0, 3, 4, 2, 1).reshape(DEPTH, NB, HIST, DA)
    return (yy[None, :SEQ], yy[SEQ:].reshape(NB, NT, D),
            kk[:, None, :SEQ].reshape(DEPTH, 1, SEQ, *heads), vv[:, None, :SEQ].reshape(DEPTH, 1, SEQ, *heads), cp,
            kk[:, SEQ:].reshape(DEPTH, NB, NT, *heads), vv[:, SEQ:].reshape(DEPTH, NB, NT, *heads), cs)
```

```python
from contextlib import ExitStack

import numpy as np

import concourse.bass as bass
from concourse import mybir

F32 = mybir.dt.float32
F32R = mybir.dt.float32r
ACT = mybir.ActivationFunctionType
ALU = mybir.AluOpType
AX = mybir.AxisListType

P = 128
D = 1024
DEPTH = 2
SEQ = 512
NB, NT = 8, 8
NS = NB * NT
T = SEQ + NS
H = T // 2
HP_ = SEQ - H
KT = D // P
HD = 64
NH = 8
DA = NH * HD
CT = DA // P
FF = 2816
FT = FF // P
CW = 31
HIST = CW - 1
PAST = 512
NVEC = CT * CW + 5 * CT + 4 * KT
EPS = 1e-5
ALPHA = (2 * DEPTH) ** 0.25
SCALE = HD ** -0.5
NEG = -1e30
LEAST = -3.0e38

UNIT = KT * P
N_IN, N_OUT, N_GU = 2 * CT + 3 * CT, KT, 2 * FT
DN_K = (8, 8, 6)
N_DN = KT * len(DN_K)
IN0 = 0
OUT0 = IN0 + N_IN
GU0 = OUT0 + N_OUT
DN0 = GU0 + N_GU
UL = DN0 + N_DN
NC_ = NB + 1
V_EARLY = 2 * DEPTH
V_LATE = 4
A_UNITS, A_SLOTS = KT, 4
Z_IN = 0
Z_OUT = Z_IN + N_IN // 2
Z_GU = Z_OUT + N_OUT // 2
Z_DN = Z_GU + N_GU // 2
ZL = Z_DN + KT // 2

V_CW = 0
V_CB = V_CW + CT * CW
V_CG = V_CB + CT
V_CLB = V_CG + CT
V_BA = V_CLB + CT
V_BC = V_BA + CT
V_G1 = V_BC + CT
V_B1 = V_G1 + KT
V_G2 = V_B1 + KT
V_B2 = V_G2 + KT
SH1, SC1 = 0, KT
G1, SH2, SC2, G2 = (j * KT for j in range(4))

QB = SEQ // P
E_OFF = [P * (q * (q + 1) // 2) for q in range(QB)]
E_ALL = P * QB * (QB + 1) // 2
PT_OFF = [0]
for _k in range(QB - 1):
    PT_OFF.append(PT_OFF[-1] + (QB - _k) * P)
S_BANK = [(4, 0), (4, P), (5, 0), (6, 0)]

SWAP = [i + 8 if i < 8 else i - 8 if i < 16 else i for i in range(32)]

PER = dict(lo_ready=UL, w_used=UL, hi_ready=UL, z_free=ZL, hs_f=2, h_f=2 * KT, h_hi=2 * KT,
           hs_hi=2, h_lo=2 * (KT + 1), rope_done=2 * CT, vt_ps=QB + 1, vnat_ready=QB + 1,
           q_zero=1, qk_staged=CT, v_staged=CT, s_ps=3 * NH, s_free=QB * NH, nm_ready=NH, exp_ready=QB * NH, p_ready=NH, pt_ps=QB * NH, pt_ready=QB * NH,
           o_ps=CT, o_free=CT, ss_ps=CT, ss_free=CT, nms_ready=CT, exps_ready=CT, ps_ready=CT, pts_ps=CT, pts_ready=2 * CT,
           os_ps=CT, os_ready=CT, ost_ps=CT, o_done=2 * CT, conv_done=CT // 2, conv_dve=CT // 2, m_sum=1, m_mean=1, m_cent=1, m_sq=3, m_var=3,
           m_sd=3, m_mul=1, m_norm=1, cz=CT, m_f=2 * CT, m_hi=2 * CT, m_lo=2 * CT, gm_act=4 * KT, ln_sum=2, ln_mean=2,
           ln_cent=4, ln_sq=4, ln_var=2, ln_sd=2, ln_done=2 * KT, a_hi=FT, a_lo=FT, hist_zero=1)
FREE = dict(lo_ready=2, w_used=2, z_free=1, ada_used=A_SLOTS, ada_sb=2, ada_t=1, ada_out=1, s_free=QB, s_ps=6, pt_ps=2 * QB,
            pt_ready=2, o_ps=1, o_free=1, ss_ps=1, ps_ready=1, pts_ps=1, os_ps=1, rope_done=2, conv_done=1, ln_done=1, a_lo=1)


class Steps:

    def __init__(self, eng, sem):
        self.eng, self.sem, self.n = eng, sem, 0

    def of(self, ins):
        ins.then_inc(self.sem, 1)
        self.n += 1
        return self.n

    def wait(self, n):
        self.eng.wait_ge(self.sem, n)

    def link(self, ins):
        self.wait(self.of(ins))

    def restart(self):
        if self.n:
            self.wait(self.n)
            self.eng.sem_clear(self.sem)
            self.n = 0


def trunk(nc, xT, cT, ba_d, w_mod1, w_mod2, w_mix, w_dn, kc_d, vc_d, st_d, vec_d, rope_d, eye_d, mp_d, msc_d, msn_d,
          y_d, k_d, v_d, cp_d, cs_d):
    with ExitStack() as ctx:
        def sb(name, shape, dt=F32, where=ctx):
            return where.enter_context(nc.sbuf_tensor("sb_" + name, shape, dt))

        sems = {}
        for name in list(PER) + ["consts", "kc0", "kc1", "vc0", "vc1", "hist", "c_ready", "w_in0", "w_in1", "vec_in", "ada_used", "ada_sb", "ada_t", "ada_out",
                                 "act_steps", "dve_steps", "pool_steps", "k_st", "v_st", "cv_st", "y_st", "carrier", "z_free1"]:
            sems[name] = ctx.enter_context(nc.semaphore(name))
        w_in = [sems["w_in0"], sems["w_in1"]]
        ada_in = [ctx.enter_context(nc.semaphore(f"ada_in{j}")) for j in range(A_SLOTS)]
        z_free = [sems["z_free"], sems["z_free1"]]
        kc_in = [sems["kc0"], sems["kc1"]]
        vc_in = [sems["vc0"], sems["vc1"]]

        def behind(eng, sem, value):
            eng.wait_ge(sem, value)
            eng.sem_inc(sems["carrier"], 1)

        def nth(l, name, k):
            return l * PER[name] + (k + 1 + FREE.get(name, 0))

        def slot(l, name, k):
            return l * PER[name] + (k + 1)

        x = sb("x", [P, KT, T])
        w_raw = sb("w_raw", [P, 2, UNIT])
        with ExitStack() as a:
            ada_ring = sb("ada_ring", [P, 2, UNIT], where=a)
            ada_o = sb("ada_o", [NB + 1, 2, 512], where=a)
        w_hi = sb("w_hi", [P, 2, UNIT], F32R)
        w_lo = sb("w_lo", [P, 2, UNIT], F32R)
        eye = sb("eye", [P, P])
        ones = sb("ones", [P, P])
        rope = sb("rope", [P, 2, T])
        mp = sb("mp", [P, 2, SEQ])
        msc = sb("msc", [P, 2, PAST])
        msn = sb("msn", [P, CT, 2, NS])
        mod1 = sb("mod1", [P, V_EARLY * KT, NC_])
        mod = sb("mod", [P, V_LATE * KT, NC_])
        b_ada = sb("b_ada", [P, (V_EARLY + DEPTH * V_LATE) * KT])
        vec = sb("vec", [P, NVEC])
        c_in = sb("c_in", [P, KT, NC_])
        small = sb("small", [P, 40])
        eps = small[:, 39:40]
        mx4, nm4, den4, rden4 = ([small[:, 8 * k + 4 * e:8 * k + 4 * e + 4] for e in range(2)] for k in range(4))
        mxs, dens, rdens, nms = small[:, 32:34], small[:, 34:36], small[:, 36:38], small[:, 38:39]
        with nc.sbuf_tensor("kc", [P, 2, CT, PAST], F32) as kc, nc.sbuf_tensor("vc", [P, 2, PAST // P, DA], F32) as vc:
            pass
        h_hi = sb("h_hi", [P, KT, T], F32R)
        h_lo = sb("h_lo", [P, KT, T], F32R)
        with ExitStack() as a:
            qk = sb("qk", [P, 2 * CT, T], where=a)
            vT = sb("vT", [P, CT, T], where=a)
            vnat = sb("vnat", [P, QB + 1, DA], where=a)
            with ExitStack() as b:
                sqc = sb("sqc", [P, CT, T], where=b)
                meanc = sb("meanc", [P, T], where=b)
            uP = sb("uP", [P, CT, HIST + SEQ], where=a)
            uS = sb("uS", [P, CT, NB, HIST + NT], where=a)
            y = sb("y", [P, CT, T], where=a)
            oT = sb("oT", [P, CT, T], where=a)
            with ExitStack() as b:
                sg = sb("sg", [P, T], where=b)
                zraw = sb("zraw", [P, 2, T], where=b)
                zcos = sb("zcos", [P, T], where=b)
                zswap = sb("zswap", [P, T], where=b)
            with ExitStack() as b:
                E = sb("E", [P, 2, E_ALL], where=b)
                PT = sb("PT", [P, 2, E_ALL], where=b)
                Es = sb("Es", [P, T], where=b)
                PTs = sb("PTs", [P, QB + 1, P], where=b)
                Os = Es[:, 0:DA]
                Qbd = sb("Qbd", [P, 2, CT, NH * NT], where=b)
                Qst = sb("Qst", [P, T], where=b)
                Kst = sb("Kst", [P, SEQ], where=b)
                Vst = sb("Vst", [P, QB, P], where=b)
                mnst = sb("mnst", [P, 2, NS], where=b)
                with ExitStack() as d:
                    sdc = sb("sdc", [P, T], where=d)
                    rstdc = sb("rstdc", [P, T], where=d)
                uPst = sb("uPst", [P, HIST + SEQ], where=b)
                uSst = sb("uSst", [P, NB, HIST + NT], where=b)
                cwst = sb("cwst", [P, CW + 1], where=b)
                yst = sb("yst", [P, 2, T], where=b)
            with ExitStack() as b:
                sqm = sb("sqm", [P, CT, T], where=b)
                sdm = sb("sdm", [P, T], where=b)
                rstdm = sb("rstdm", [P, T], where=b)
                mt = sb("mt", [P, 2, T], where=b)
                gm = sb("gm", [P, 2, T], where=b)
        with ExitStack() as a:
            a_hi = sb("a_hi", [P, FT, T], F32R, where=a)
            a_lo = sb("a_lo", [P, FT, T], F32R, where=a)
            gate = sb("gate", [P, T], where=a)
            af = sb("af", [P, T], where=a)
        with ExitStack() as a:
            sq = sb("sq", [P, KT, T], where=a)
            mean = sb("mean", [P, T], where=a)
            sd = sb("sd", [P, T], where=a)
            rstd = sb("rstd", [P, T], where=a)
            hf = sb("hf", [P, 2, SEQ], where=a)
            hs = sb("hs", [P, KT, NS], where=a)
        ps = ctx.enter_context(nc.psum_tensor("ps", [P, 8, 512], F32))
        Z = [ps[:, 0:2, 0:H], ps[:, 2:4, 0:H]]
        STAT = [ps[:, 4:6, 0:H], ps[:, 6:8, 0:H]]

        ada_w = [w_raw[:, 0], w_raw[:, 1], ada_ring[:, 0], ada_ring[:, 1]]

        def halves(t):
            return t.rearrange("p (h n) -> p h n", h=2)

        def by_seq(t):
            return t.rearrange("p (b t) -> p b t", b=NB)

        def ada_before(l):
            return l * V_LATE + V_EARLY

        def unit(l, base, i, s, u):
            return u % 2, l * UL + i * s + (base + u), l * (UL // 2) + i * (s // 2) + (base // 2 + u // 2)

        def z_taken(l, i, z0):
            return l * ZL + i + (z0 + 2)

        def z_before(l, i, z0):
            return l * ZL + i + (z0 + 1)

        consts = [(x[:], xT), (c_in[:], cT), (b_ada[:], ba_d), (eye[:], eye_d), (rope[:], rope_d), (mp[:], mp_d), (msc[:], msc_d), (msn[:], msn_d)]
        s = sems
        block = ctx.enter_context(nc.Block())

        @block.sync
        def _(sp):
            for name, n in FREE.items():
                sp.sem_inc(s[name], n)
            sp.sem_inc(s["z_free1"], 1)
            for dst, src in consts:
                sp.dma_start(dst, src).then_inc(s["consts"], 16)

            def fetch(l, base, i, st, u, src, n=UNIT):
                j, seq, _ = unit(l, base, i, st, u)
                sp.wait_ge(s["lo_ready"], seq + 1)
                sp.dma_start(w_raw[:, j, 0:n], src).then_inc(w_in[j], 16)

            def fetch_ada(v, src):
                for q in range(A_UNITS):
                    sp.wait_ge(s["ada_used"], v * A_UNITS + (q + 1))
                    sp.dma_start(ada_w[q % A_SLOTS], src(q)).then_inc(ada_in[q % A_SLOTS], 16)

            with sp.Fori(0, V_EARLY) as v:
                fetch_ada(v, lambda q: w_mod1[v, q])
            with sp.Fori(0, DEPTH) as l:
                sp.wait_ge(s["ada_used"], ada_before(l) * A_UNITS + A_SLOTS)
                sp.wait_ge(s["ln_done"], slot(l, "ln_done", 0))
                sp.dma_start(vec[:], vec_d[l]).then_inc(s["vec_in"], 16)
                with sp.Fori(0, N_IN // 2) as i:
                    for u in range(2):
                        fetch(l, IN0, i, 2, u, w_mix[l, i * 2 + u])
                behind(sp, s["w_used"], nth(l, "w_used", OUT0 - 1))

                def keys(i):
                    sp.wait_ge(s["ss_ps"], l * CT + i + 1)
                    for b in range(2):
                        sp.dma_start(kc[:, b], kc_d[l, i * 2 + b]).then_inc(kc_in[b], 16)

                def values(i):
                    sp.wait_ge(s["os_ps"], l * CT + i + 1)
                    for b in range(2):
                        sp.dma_start(vc[:, b], vc_d[l, i * 2 + b]).then_inc(vc_in[b], 16)

                keys(0)
                with sp.Fori(0, CT - 1) as i:
                    fetch_ada(ada_before(l) + i, lambda q: w_mod2[l, i, q])
                    values(i)
                    keys(i + 1)
                fetch_ada(ada_before(l) + (CT - 1), lambda q: w_mod2[l, CT - 1, q])
                values(CT - 1)
                behind(sp, s["ada_used"], ada_before(l) * A_UNITS + (V_LATE * A_UNITS + A_SLOTS))
                with sp.Fori(0, N_OUT // 2) as i:
                    for u in range(2):
                        fetch(l, OUT0, i, 2, u, w_mix[l, i * 2 + (N_IN + u)])
                with sp.Fori(0, N_GU // 2) as i:
                    for u in range(2):
                        fetch(l, GU0, i, 2, u, w_mix[l, i * 2 + (N_IN + N_OUT + u)])
                with sp.Fori(0, KT // 2) as i:
                    for u in range(6):
                        k0 = sum(DN_K[:u % 3]) * P
                        n = DN_K[u % 3] * P
                        fetch(l, DN0, i, 6, u, w_dn[l, i * 2 + u // 3, :, k0:k0 + n], n)
            sp.wait_ge(s["ln_done"], 2 * KT * DEPTH + 1)
            sp.dma_start(y_d, x[:]).then_inc(s["y_st"], 16)
            sp.wait_ge(s["y_st"], 16)
            sp.wait_ge(s["k_st"], 16 * DEPTH)
            sp.wait_ge(s["v_st"], 16 * DEPTH)
            sp.wait_ge(s["cv_st"], 32 * DEPTH)

        @block.gpsimd
        def _(pool):
            st = Steps(pool, s["pool_steps"])
            with pool.Fori(0, DEPTH) as l:
                behind(pool, s["w_used"], nth(l, "w_used", IN0))
                pool.dma_start(uS[:, :, :, 0:HIST], st_d[l]).then_inc(s["hist"], 16)
                nc.gpsimd.memset(uP[:, :, 0:HIST], 0.0).then_inc(s["hist_zero"], 1)
                st.link(nc.gpsimd.memset(Qbd[:], 0.0))
                st.restart()
                pool.sem_inc(s["q_zero"], 1)
                behind(pool, z_free[1], z_taken(l, CT - 1, Z_IN))
                behind(pool, s["hist_zero"], l + 1)
                pool.dma_start(cp_d[l], uP[:, :, SEQ:SEQ + HIST]).then_inc(s["cv_st"], 16)
                behind(pool, s["hist"], l * 16 + 16)
                pool.dma_start(cs_d[l], uS[:, :, :, NT:NT + HIST]).then_inc(s["cv_st"], 16)
                behind(pool, s["vec_in"], l * 16 + 16)
                with pool.Fori(0, CT // 2) as i:
                    st.of(nc.gpsimd.tensor_copy(uPst[:], uP[:, i, :]))
                    st.of(nc.gpsimd.tensor_copy(uSst[:], uS[:, i]))
                    st.of(nc.gpsimd.tensor_copy(cwst[:, 0:CW], vec[:, bass.ds(i * CW + V_CW, CW)]))
                    st.link(nc.gpsimd.tensor_copy(cwst[:, CW:CW + 1], vec[:, bass.ds(i + V_CB, 1)]))
                    acc, prod = yst[:, 0], yst[:, 1]
                    for w in range(CW):
                        up, us, tap = uPst[:, w:w + SEQ], uSst[:, :, w:w + NT], cwst[:, w:w + 1]
                        if w == 0:
                            st.of(nc.gpsimd.tensor_scalar(acc[:, 0:SEQ], up, tap, cwst[:, CW:CW + 1], ALU.mult, ALU.add))
                            st.link(nc.gpsimd.tensor_scalar(by_seq(acc[:, SEQ:T]), us, tap, cwst[:, CW:CW + 1], ALU.mult, ALU.add))
                            continue
                        st.of(nc.gpsimd.tensor_scalar(prod[:, 0:SEQ], up, tap, None, ALU.mult))
                        st.link(nc.gpsimd.tensor_scalar(by_seq(prod[:, SEQ:T]), us, tap, None, ALU.mult))
                        st.link(nc.gpsimd.tensor_tensor(acc, acc, prod, ALU.add))
                    st.restart()
                    nc.gpsimd.tensor_copy(y[:, i, :], acc).then_inc(s["conv_done"], 1)
                    behind(pool, s["conv_done"], l * CT // 2 + i + 2)
                behind(pool, s["rope_done"], nth(l, "rope_done", 2 * CT - 1))
                pool.dma_start(k_d[l], qk[:, CT:2 * CT, :]).then_inc(s["k_st"], 16)
                for j in range(2):
                    behind(pool, z_free[j], l * ZL + (Z_OUT + 1))
                pool.dma_start(v_d[l], vT[:]).then_inc(s["v_st"], 16)

        @block.scalar
        def _(act):
            st = Steps(act, s["act_steps"])

            def split(l, base, i, n, u):
                j, seq, half = unit(l, base, i, n, u)
                act.wait_ge(w_in[j], half * 16 + 16)
                act.wait_ge(s["w_used"], seq + 1)
                nc.scalar.activation(w_hi[:, j, :], w_raw[:, j, :], ACT.Copy).then_inc(s["hi_ready"], 1)

            def computed(l, base, i, n, u):
                act.wait_ge(s["w_used"], unit(l, base, i, n, u)[1] + 3)

            def h_parts(l, q):
                for kt in range(KT):
                    act.wait_ge(s["h_f"], nth(l, "h_f", q * KT + kt))
                    nc.scalar.activation(h_hi[:, kt, 0:SEQ], hf[:, kt % 2, :], ACT.Copy).then_inc(s["h_hi"], 1)
                act.wait_ge(s["hs_f"], nth(l, "hs_f", q))
                nc.scalar.activation(h_hi[:, :, SEQ:T], hs[:], ACT.Copy).then_inc(s["hs_hi"], 1)

            def gated(l, dst, u, m, g):
                scale = mod[:, bass.ds(m + g, 1), 0] if not isinstance(m, int) else mod[:, m + g, 0:1]
                nc.scalar.activation(dst[:, 0:H], Z[u][:, 0], ACT.Copy, scale=scale).then_inc(s["gm_act"], 1)
                nc.scalar.activation(dst[:, H:SEQ], Z[u][:, 1, 0:HP_], ACT.Copy, scale=scale).then_inc(s["gm_act"], 1)

            def norm(l, q):
                act.wait_ge(s["ln_sum"], nth(l, "ln_sum", q))
                nc.scalar.activation(halves(mean[:]), STAT[0], ACT.Copy, scale=1.0 / D).then_inc(s["ln_mean"], 1)
                for c in range(2):
                    act.wait_ge(s["ln_cent"], nth(l, "ln_cent", 2 * q + c))
                    part = slice(c * KT // 2, (c + 1) * KT // 2)
                    nc.scalar.activation(sq[:, part], x[:, part], ACT.Square).then_inc(s["ln_sq"], 1)
                act.wait_ge(s["ln_var"], nth(l, "ln_var", q))
                nc.scalar.activation(halves(sd[:]), STAT[1], ACT.Sqrt, scale=1.0 / D, bias=eps).then_inc(s["ln_sd"], 1)

            act.wait_ge(s["consts"], 16 * len(consts))
            def ada_copy(v, banks):
                for g in range(2):
                    act.wait_ge(s["ada_used"], v * A_UNITS + (A_SLOTS + (g + 1) * A_UNITS // 2))
                    act.wait_ge(s["ada_t"], v + 1)
                    nc.scalar.activation(ada_o[:, g], ps[0:NC_, banks[g], :], ACT.Copy).then_inc(s["ada_sb"], 1)

            nc.scalar.activation(c_in[:], c_in[:], ACT.Silu).then_inc(s["c_ready"], 1)
            with act.Fori(0, V_EARLY) as v:
                ada_copy(v, (0, 1))
            with act.Fori(0, DEPTH) as l:
                split(l, IN0, 0, 2, 0)
                h_parts(l, 0)
                nc.scalar.preload_act_table(ACT.Sigmoid)
                with act.Fori(0, CT) as i:
                    split(l, IN0, i, 2, 1)
                    computed(l, IN0, i, 2, 0)
                    act.wait_ge(z_free[1], z_before(l, i, Z_IN))
                    nc.scalar.activation(halves(sg[:]), Z[0], ACT.Sigmoid).then_inc(z_free[0], 1)
                    split(l, IN0, i, 2, 2)
                with act.Fori(0, CT) as i:
                    for u in range(2):
                        split(l, IN0 + 2 * CT, i, 2, u + 1)
                        computed(l, IN0 + 2 * CT, i, 2, u)
                        act.wait_ge(s["rope_done"], l * 2 * CT + i * 2 + (u + 1))
                        nc.scalar.activation(halves(zraw[:, u]), Z[u], ACT.Copy).then_inc(z_free[u], 1)
                for u in range(CT):
                    if u < CT - 1:
                        split(l, IN0 + 4 * CT, 0, 2, u + 1)
                    computed(l, IN0 + 4 * CT, 0, 2, u)
                    nc.scalar.activation(halves(vT[:, u]), Z[u % 2], ACT.Copy).then_inc(z_free[u % 2], 1)
                for t in range(QB + 1):
                    rows = P if t < QB else NS
                    act.wait_ge(s["vt_ps"], nth(l, "vt_ps", t))
                    nc.scalar.activation(vnat[0:rows, t, :], ps[0:rows, 4 + t % 4, :], ACT.Copy).then_inc(s["vnat_ready"], 1)
                nc.scalar.preload_act_table(ACT.Exp)
                with act.Fori(0, CT) as i:
                    def exps(e):
                        act.wait_ge(s["nm_ready"], l * NH + i * 2 + (e + 1))
                        for q in range(QB):
                            blk = E[:, e, E_OFF[q]:E_OFF[q] + (q + 1) * P]
                            nc.scalar.activation(blk, blk, ACT.Exp, bias=nm4[e][:, q:q + 1], scale=SCALE)\
                                .then_inc(s["exp_ready"], 1)

                    exps(0)
                    act.wait_ge(s["nms_ready"], l * CT + i + 1)
                    nc.scalar.activation(Es[:], Es[:], ACT.Exp, bias=nms, scale=SCALE).then_inc(s["exps_ready"], 1)
                    exps(1)
                    ada_copy(ada_before(l) + i, (2, 1))
                    for e in range(2):
                        for k in range(QB):
                            n = (QB - k) * P
                            act.wait_ge(s["pt_ps"], (l * NH + i * 2) * QB + (e * QB + k + 1 + FREE["pt_ps"]))
                            nc.scalar.activation(PT[:, e, PT_OFF[k]:PT_OFF[k] + n], ps[:, k % 2, 0:n], ACT.Copy)\
                                .then_inc(s["pt_ready"], 1)
                    act.wait_ge(s["o_ps"], l * CT + i + 2)
                    nc.scalar.activation(oT[:, i, 0:SEQ], ps[:, 2, :], ACT.Copy).then_inc(s["o_free"], 1)
                    act.wait_ge(s["pts_ps"], l * CT + i + 2)
                    nc.scalar.activation(PTs[:, 0:QB, :], ps[:, 3, :].rearrange("p (k n) -> p k n", k=QB), ACT.Copy)\
                        .then_inc(s["pts_ready"], 1)
                    nc.scalar.activation(PTs[0:NS, QB, :], ps[0:NS, 7, 0:P], ACT.Copy).then_inc(s["pts_ready"], 1)
                    act.wait_ge(s["os_ps"], l * CT + i + 2)
                    nc.scalar.activation(Os[:], ps[:, 3, :], ACT.Copy).then_inc(s["os_ready"], 1)
                    act.wait_ge(s["ost_ps"], l * CT + i + 1)
                    for e in range(2):
                        own = ps[e * HD:(e + 1) * HD, 7, e * NT:]
                        own = bass.AP(own.tensor, own.offset, [list(own.ap[0]), [P + 2 * NT, CT], [NH * NT, 2], [1, NT]])
                        nc.scalar.activation(
                            oT[e * HD:(e + 1) * HD, :, bass.ds(i * 2 * NT + SEQ, 2 * NT)]
                            .rearrange("p c (b t) -> p c b t", b=2), own, ACT.Copy).then_inc(s["o_done"], 1)

                split(l, OUT0, 0, 2, 0)

                def root(q, src):
                    act.wait_ge(s["m_var"], nth(l, "m_var", q))
                    nc.scalar.activation(halves(sdm[:]), STAT[1], ACT.Sqrt, scale=1.0 / DA, bias=eps).then_inc(s["m_sd"], 1)

                def m_parts(q):
                    for c in range(CT):
                        act.wait_ge(s["m_f"], nth(l, "m_f", q * CT + c))
                        nc.scalar.activation(h_hi[:, q * CT + c, :], mt[:, c % 2, :], ACT.Copy).then_inc(s["m_hi"], 1)

                act.wait_ge(s["o_done"], nth(l, "o_done", 2 * CT - 1))
                act.wait_ge(s["o_free"], nth(l, "o_free", CT - 1))
                act.wait_ge(s["conv_done"], nth(l, "conv_done", CT // 2 - 1))
                act.wait_ge(s["conv_dve"], nth(l, "conv_dve", CT // 2 - 1))
                nc.scalar.activation(sqm[:], oT[:], ACT.Square).then_inc(s["m_sq"], 1)
                root(0, None)
                m_parts(0)
                act.wait_ge(s["m_sum"], l + 1)
                act.wait_ge(s["cv_st"], l * 32 + 32)
                nc.scalar.activation(halves(meanc[:]), STAT[0], ACT.Copy, scale=1.0 / DA).then_inc(s["m_mean"], 1)
                act.wait_ge(s["m_cent"], l + 1)
                nc.scalar.activation(sqm[:], y[:], ACT.Square).then_inc(s["m_sq"], 1)
                root(1, None)
                act.wait_ge(s["m_norm"], l + 1)
                for c in range(CT):
                    nc.scalar.activation(y[:, c, :], y[:, c, :], ACT.Silu, scale=vec[:, V_CG + c:V_CG + c + 1],
                                         bias=vec[:, V_CLB + c:V_CLB + c + 1]).then_inc(s["cz"], 1)
                act.wait_ge(s["cz"], nth(l, "cz", CT - 1))
                nc.scalar.activation(sqm[:], y[:], ACT.Square).then_inc(s["m_sq"], 1)
                root(2, None)
                m_parts(1)
                with act.Fori(0, N_OUT // 2) as i:
                    for u in range(2):
                        split(l, OUT0, i, 2, u + 1)
                        computed(l, OUT0, i, 2, u)
                        act.wait_ge(z_free[u], z_before(l, i, Z_OUT))
                        gated(l, gm[:, u], u, i * 2 + u, G1)
                act.wait_ge(s["k_st"], l * 16 + 16)
                act.wait_ge(s["v_st"], l * 16 + 16)
                act.wait_ge(s["cv_st"], l * 32 + 32)
                norm(l, 0)
                h_parts(l, 1)
                nc.scalar.preload_act_table(ACT.Silu)
                with act.Fori(0, FT) as i:
                    split(l, GU0, i, 2, 1)
                    computed(l, GU0, i, 2, 0)
                    act.wait_ge(z_free[1], z_before(l, i, Z_GU))
                    nc.scalar.activation(halves(gate[:]), Z[0], ACT.Silu).then_inc(z_free[0], 1)
                    split(l, GU0, i, 2, 2)
                    act.wait_ge(z_free[1], z_taken(l, i, Z_GU))
                    nc.scalar.activation(a_hi[:, i], af[:], ACT.Copy).then_inc(s["a_hi"], 1)

                def down(i, last):
                    for u in range(6):
                        if not (last and u == 5):
                            split(l, DN0, i, 6, u + 1)
                        if u % 3 == 2:
                            computed(l, DN0, i, 6, u)
                            act.wait_ge(z_free[u // 3], z_before(l, i, Z_DN))
                            gated(l, (gate, af)[u // 3], u // 3, i * 2 + u // 3, G2)

                with act.Fori(0, KT // 2 - 1) as i:
                    down(i, False)
                down(KT // 2 - 1, True)
                norm(l, 1)

        @block.vector
        def _(dve):
            st = Steps(dve, s["dve_steps"])

            def split(l, base, i, n, u):
                j, seq, _ = unit(l, base, i, n, u)
                dve.wait_ge(s["hi_ready"], seq + 1)
                nc.vector.tensor_tensor(w_lo[:, j, :], w_raw[:, j, :], w_hi[:, j, :].bitcast(F32), ALU.subtract)\
                    .then_inc(s["lo_ready"], 1)

            def computed(l, base, i, n, u):
                dve.wait_ge(s["w_used"], unit(l, base, i, n, u)[1] + 3)

            def per_seq(j):
                return j[:, :, 1:].unsqueeze(3).to_broadcast([P, KT, NB, NT])

            def modulate(l, q, m, sh, sc):
                hs4 = hs[:].rearrange("p k (b t) -> p k b t", b=NB)
                xs4 = x[:, :, SEQ:T].rearrange("p k (b t) -> p k b t", b=NB)
                st.link(nc.vector.tensor_tensor(hs4, xs4, per_seq(m(sc, KT)), ALU.mult))
                nc.vector.tensor_tensor(hs4, hs4, per_seq(m(sh, KT)), ALU.add).then_inc(s["hs_f"], 1)
                for kt in range(KT + 1):
                    if kt < KT:
                        if kt >= 2:
                            dve.wait_ge(s["h_lo"], nth(l, "h_lo", q * (KT + 1) + kt - 2))
                        nc.vector.tensor_scalar(hf[:, kt % 2, :], x[:, kt, 0:SEQ], m(sc + kt, 1)[:, :, 0:1].rearrange("p o c -> p (o c)"),
                                                m(sh + kt, 1)[:, :, 0:1].rearrange("p o c -> p (o c)"), ALU.mult, ALU.add).then_inc(s["h_f"], 1)
                    if kt:
                        k = kt - 1
                        dve.wait_ge(s["h_hi"], nth(l, "h_hi", q * KT + k))
                        nc.vector.tensor_tensor(h_lo[:, k, 0:SEQ], hf[:, k % 2, :], h_hi[:, k, 0:SEQ].bitcast(F32),
                                                ALU.subtract).then_inc(s["h_lo"], 1)
                dve.wait_ge(s["hs_hi"], nth(l, "hs_hi", q))
                nc.vector.tensor_tensor(h_lo[:, :, SEQ:T], hs[:], h_hi[:, :, SEQ:T].bitcast(F32), ALU.subtract)\
                    .then_inc(s["h_lo"], 1)

            def conv_tap(c, w, first=None):
                up = uP[:, c, bass.ds(w, SEQ)]
                us = uS[:, c, :, bass.ds(w, NT)]
                tap, bias = vec[:, bass.ds(w + (V_CW + c * CW), 1)], vec[:, V_CB + c:V_CB + c + 1]
                yp, ys = y[:, c, 0:SEQ], by_seq(y[:, c, SEQ:T])
                if isinstance(w, int) and w == 0:
                    st.of(nc.vector.tensor_scalar(yp, up, tap, bias, ALU.mult, ALU.add))
                    st.of(nc.vector.tensor_scalar(ys, us, tap, bias, ALU.mult, ALU.add))
                    return
                st.wait(st.n - 1)
                st.of(nc.vector.scalar_tensor_tensor(out=yp, in0=up, scalar=tap, in1=yp, op0=ALU.mult, op1=ALU.add))
                st.wait(st.n - 1)
                st.of(nc.vector.scalar_tensor_tensor(out=ys, in0=us, scalar=tap, in1=ys, op0=ALU.mult, op1=ALU.add))

            def residual(l, dst, u, i, m, g, z0, done_gm):
                out4 = Z[u][:, 1, HP_:H].rearrange("p (b t) -> p b t", b=NB)
                gs = mod[:, bass.ds(m + g, 1), 1:].rearrange("p o b -> p (o b)") if not isinstance(m, int) else mod[:, m + g, 1:]
                dve.wait_ge(s["gm_act"], done_gm)
                st.link(nc.vector.tensor_tensor(by_seq(dst[:, SEQ:T]), out4, gs.unsqueeze(2).to_broadcast([P, NB, NT]), ALU.mult))
                nc.vector.scalar_tensor_tensor(out=x[:, m, :], in0=x[:, m, :], scalar=ALPHA, in1=dst,
                                               op0=ALU.mult, op1=ALU.add).then_inc(z_free[u], 1)

            def norm(l, q, g, b):
                dve.wait_ge(s["ln_mean"], nth(l, "ln_mean", q))
                half = KT // 2
                for c in range(2):
                    part = x[:, c * half:(c + 1) * half]
                    nc.vector.tensor_tensor(part, part, mean[:].unsqueeze(1).to_broadcast([P, half, T]), ALU.subtract)\
                        .then_inc(s["ln_cent"], 1)
                dve.wait_ge(s["ln_sd"], nth(l, "ln_sd", q))
                st.link(nc.vector.reciprocal(rstd[:], sd[:]))
                for c in range(2):
                    part = x[:, c * half:(c + 1) * half]
                    st.of(nc.vector.tensor_tensor(part, part, rstd[:].unsqueeze(1).to_broadcast([P, half, T]), ALU.mult))
                st.wait(st.n)
                for kt in range(KT):
                    nc.vector.tensor_scalar(x[:, kt, :], x[:, kt, :], vec[:, g + kt:g + kt + 1], vec[:, b + kt:b + kt + 1],
                                            ALU.mult, ALU.add).then_inc(s["ln_done"], 1)
                behind(dve, s["ln_done"], nth(l, "ln_done", (q + 1) * KT - 1))
                st.restart()

            st.of(nc.vector.memset(ones[:], 1.0))
            st.of(nc.vector.memset(eps, EPS))
            def ada_bias(v, bank, dst, bias):
                dve.wait_ge(s["ada_t"], v + 2)
                nc.vector.tensor_tensor(dst, ps[:, bank, 0:KT * NC_].rearrange("p (k c) -> p k c", k=KT),
                                        bias.unsqueeze(2).to_broadcast([P, KT, NC_]), ALU.add).then_inc(s["ada_out"], 1)

            st.restart()
            dve.wait_ge(s["consts"], 16 * len(consts))
            with dve.Fori(0, V_EARLY) as v:
                ada_bias(v, 2, mod1[:, bass.ds(v * KT, KT)], b_ada[:, bass.ds(v * KT, KT)])
            dve.wait_ge(s["ada_out"], V_EARLY + FREE["ada_out"])
            for l in range(DEPTH):
                sc1 = mod1[:, 2 * l * KT + SC1:2 * l * KT + SC1 + KT]
                st.of(nc.vector.tensor_scalar(sc1, sc1, 1.0, None, ALU.add))
            st.restart()
            with dve.Fori(0, DEPTH) as l:
                split(l, IN0, 0, 2, 0)
                modulate(l, 0, lambda j, n: mod1[:, bass.ds(l * 2 * KT + j, n)], SH1, SC1)
                st.restart()
                with dve.Fori(0, CT) as i:
                    split(l, IN0, i, 2, 1)
                    split(l, IN0, i, 2, 2)
                    computed(l, IN0, i, 2, 1)
                    dve.wait_ge(z_free[0], z_taken(l, i, Z_IN))
                    st.of(nc.vector.tensor_tensor(uP[:, i, HIST:HIST + H], Z[1][:, 0], sg[:, 0:H], ALU.mult))
                    st.of(nc.vector.tensor_tensor(uP[:, i, HIST + H:HIST + SEQ], Z[1][:, 1, 0:HP_], sg[:, H:SEQ], ALU.mult))
                    st.restart()
                    nc.vector.tensor_tensor(uS[:, i, :, HIST:HIST + NT], by_seq(Z[1][:, 1, HP_:H]), by_seq(sg[:, SEQ:T]),
                                            ALU.mult).then_inc(z_free[1], 1)
                with dve.Fori(0, CT) as i:
                    for u in range(2):
                        split(l, IN0 + 2 * CT, i, 2, u + 1)
                        behind(dve, z_free[u], z_taken(l, i, Z_IN + CT))
                        st.of(nc.vector.stream_shuffle(zswap[:], zraw[:, u, :], SWAP))
                        st.of(nc.vector.tensor_tensor(zcos[:], zraw[:, u, :], rope[:, 0, :], ALU.mult))
                        st.wait(st.n - 1)
                        st.link(nc.vector.tensor_tensor(zswap[:], zswap[:], rope[:, 1, :], ALU.mult))
                        nc.vector.tensor_tensor(qk[:, i * 2 + u, :], zcos[:], zswap[:], ALU.add)\
                            .then_inc(s["rope_done"], 1)
                        behind(dve, s["rope_done"], l * 2 * CT + i * 2 + (u + 3))
                        st.restart()
                behind(dve, s["vec_in"], l * 16 + 16)
                behind(dve, s["hist"], l * 16 + 16)
                behind(dve, s["hist_zero"], l + 1)
                for u in range(CT):
                    if u < CT - 1:
                        split(l, IN0 + 4 * CT, 0, 2, u + 1)
                    for w in range(u * 8, min(u * 8 + 8, CW)):
                        conv_tap(CT - 1, w)
                st.wait(st.n)
                dve.sem_inc(s["conv_dve"], 1)
                conv_tap(CT - 2, 0)

                def stage_scores(i):
                    st.of(nc.vector.tensor_copy(Qst[:], qk[:, i, :]))
                    st.of(nc.vector.tensor_copy(Kst[:], qk[:, i + CT, 0:SEQ]))
                    for e in range(2):
                        own = Qbd[e * HD:(e + 1) * HD, 0, 0, e * NT:]
                        own = bass.AP(own.tensor, own.offset, [list(own.ap[0]), [CT * NH * NT, 2], [NH * NT + 2 * NT, CT], [1, NT]])
                        st.of(nc.vector.tensor_copy(
                            own, qk[e * HD:(e + 1) * HD, 0:CT, bass.ds(i * 2 * NT + SEQ, 2 * NT)]
                            .rearrange("p c (b t) -> p b c t", b=2)))
                    st.wait(st.n)
                    dve.sem_inc(s["qk_staged"], 1)

                def stage_outputs(i):
                    dve.wait_ge(s["o_ps"], l * CT + i + 1)
                    st.of(nc.vector.tensor_copy(Vst[:], vnat[:, 0:QB, bass.ds(i * P, P)]))
                    st.of(nc.vector.tensor_copy(mnst[:], msn[:, i]))
                    st.wait(st.n)
                    dve.sem_inc(s["v_staged"], 1)

                def attend(i, last):
                    def head_max(e):
                        dve.wait_ge(s["pt_ps"], (l * NH + i * 2) * QB + (e + 1) * QB)
                        for q in range(QB):
                            w = (q + 1) * P
                            if q != 1:
                                behind(dve, s["s_ps"], l * 3 * NH + i * 6 + (3 * e + max(q, 1) + FREE["s_ps"]))
                            bank, o = S_BANK[q]
                            nc.vector.tensor_tensor_reduce(E[:, e, E_OFF[q]:E_OFF[q] + w], ps[:, bank, o:o + w],
                                                           mp[:, 0, SEQ - w:SEQ], 1.0, LEAST, ALU.add, ALU.max,
                                                           mx4[e][:, q:q + 1]).then_inc(s["s_free"], 1)
                        dve.wait_ge(s["s_free"], (l * NH + i * 2) * QB + ((e + 1) * QB + FREE["s_free"]))
                        nc.vector.tensor_scalar(nm4[e], mx4[e], -SCALE, None, ALU.mult).then_inc(s["nm_ready"], 1)

                    def head_prob(e):
                        for q in range(QB):
                            blk = E[:, e, E_OFF[q]:E_OFF[q] + (q + 1) * P]
                            behind(dve, s["exp_ready"], (l * NH + i * 2) * QB + (e * QB + q + 1))
                            st.of(nc.vector.tensor_tensor_reduce(blk, blk, mp[:, 1, SEQ - (q + 1) * P:SEQ], 1.0, 0.0, ALU.mult,
                                                                 ALU.add, den4[e][:, q:q + 1]))
                        st.wait(st.n)
                        st.link(nc.vector.reciprocal(rden4[e], den4[e]))
                        for q in range(QB):
                            blk = E[:, e, E_OFF[q]:E_OFF[q] + (q + 1) * P]
                            nc.vector.tensor_scalar(blk, blk, rden4[e][:, q:q + 1], None, ALU.mult).then_inc(s["p_ready"], 1)

                    head_max(0)
                    dve.wait_ge(s["pts_ps"], l * CT + i + 1)
                    behind(dve, s["ss_ps"], l * CT + i + 2)
                    st.link(nc.vector.tensor_tensor_reduce(Es[:, 0:PAST], ps[:, 3, :], msc[:, 0], 1.0, LEAST, ALU.add, ALU.max,
                                                           mxs[:, 0:1]))
                    st.link(nc.vector.tensor_tensor_reduce(Es[:, PAST:T], ps[:, 7, 0:NS], mnst[:, 0], 1.0, mxs[:, 0:1], ALU.add,
                                                           ALU.max, mxs[:, 1:2]))
                    nc.vector.tensor_scalar(nms, mxs[:, 1:2], -SCALE, None, ALU.mult).then_inc(s["nms_ready"], 1)
                    head_max(1)
                    if not last:
                        stage_scores(i + 1)
                    head_prob(0)
                    behind(dve, s["exps_ready"], l * CT + i + 1)
                    st.link(nc.vector.tensor_tensor_reduce(Es[:, 0:PAST], Es[:, 0:PAST], msc[:, 1], 1.0, 0.0, ALU.mult, ALU.add,
                                                           dens[:, 0:1]))
                    st.link(nc.vector.tensor_tensor_reduce(Es[:, PAST:T], Es[:, PAST:T], mnst[:, 1], 1.0, dens[:, 0:1], ALU.mult,
                                                           ALU.add, dens[:, 1:2]))
                    st.link(nc.vector.reciprocal(rdens[:, 0:1], dens[:, 1:2]))
                    nc.vector.tensor_scalar(Es[:], Es[:], rdens[:, 0:1], None, ALU.mult).then_inc(s["ps_ready"], 1)
                    head_prob(1)
                    ada_bias(ada_before(l) + i, 0, mod[:, bass.ds(i * KT, KT)],
                             b_ada[:, bass.ds(l * V_LATE * KT + (i * KT + V_EARLY * KT), KT)])
                    if not last:
                        st.wait(st.n)
                        for w in range((CW - 1) // 3):
                            conv_tap(CT - 2, i * ((CW - 1) // 3) + (w + 1))
                        stage_outputs(i + 1)
                    st.restart()

                behind(dve, s["q_zero"], l + 1)
                stage_scores(0)
                dve.wait_ge(s["vnat_ready"], nth(l, "vnat_ready", QB))
                stage_outputs(0)
                st.restart()
                with dve.Fori(0, CT - 1) as i:
                    attend(i, False)
                dve.sem_inc(s["conv_dve"], 1)
                attend(CT - 1, True)
                dve.wait_ge(s["ada_out"], ada_before(l) + (V_LATE + FREE["ada_out"]))
                st.of(nc.vector.tensor_scalar(mod[:, SC2:SC2 + KT, :], mod[:, SC2:SC2 + KT, :], 1.0, None, ALU.add))
                split(l, OUT0, 0, 2, 0)

                def scaled(q, src, beta):
                    dve.wait_ge(s["m_sd"], nth(l, "m_sd", 0 if q == 0 else 2))
                    st.link(nc.vector.reciprocal(rstdm[:], sdm[:]))
                    for c in range(CT + 1):
                        if c < CT:
                            if c >= 2 or q:
                                dve.wait_ge(s["m_lo"], nth(l, "m_lo", q * CT + c - 2))
                            nc.vector.scalar_tensor_tensor(out=mt[:, c % 2, :], in0=src[:, c, :], scalar=vec[:, beta + c:beta + c + 1],
                                                           in1=rstdm[:], op0=ALU.mult, op1=ALU.mult).then_inc(s["m_f"], 1)
                        if c:
                            k = c - 1
                            dve.wait_ge(s["m_hi"], nth(l, "m_hi", q * CT + k))
                            nc.vector.tensor_tensor(h_lo[:, q * CT + k, :], mt[:, k % 2, :], h_hi[:, q * CT + k, :].bitcast(F32),
                                                    ALU.subtract).then_inc(s["m_lo"], 1)

                scaled(0, oT, V_BA)
                dve.wait_ge(s["m_mean"], l + 1)
                nc.vector.tensor_tensor(y[:], y[:], meanc[:].unsqueeze(1).to_broadcast([P, CT, T]), ALU.subtract)\
                    .then_inc(s["m_cent"], 1)
                dve.wait_ge(s["m_lo"], nth(l, "m_lo", CT - 1))
                dve.wait_ge(s["m_sd"], nth(l, "m_sd", 1))
                st.link(nc.vector.reciprocal(rstdm[:], sdm[:]))
                nc.vector.tensor_tensor(y[:], y[:], rstdm[:].unsqueeze(1).to_broadcast([P, CT, T]), ALU.mult)\
                    .then_inc(s["m_norm"], 1)
                scaled(1, y, V_BC)
                st.restart()
                with dve.Fori(0, N_OUT // 2) as i:
                    for u in range(2):
                        split(l, OUT0, i, 2, u + 1)
                        computed(l, OUT0, i, 2, u)
                        residual(l, gm[:, u], u, i, i * 2 + u, G1, Z_OUT, l * 4 * KT + i * 4 + (2 * u + 2))
                    st.restart()
                norm(l, 0, V_G1, V_B1)
                modulate(l, 1, lambda j, n: mod[:, j:j + n], SH2, SC2)
                st.restart()
                with dve.Fori(0, FT) as i:
                    split(l, GU0, i, 2, 1)
                    split(l, GU0, i, 2, 2)
                    computed(l, GU0, i, 2, 1)
                    dve.wait_ge(z_free[0], z_taken(l, i, Z_GU))
                    dve.wait_ge(s["a_lo"], l * FT + i + FREE["a_lo"])
                    nc.vector.tensor_tensor(halves(af[:]), Z[1], halves(gate[:]), ALU.mult).then_inc(z_free[1], 1)
                    dve.wait_ge(s["a_hi"], l * FT + i + 1)
                    nc.vector.tensor_tensor(a_lo[:, i], af[:], a_hi[:, i].bitcast(F32), ALU.subtract).then_inc(s["a_lo"], 1)

                def down(i, last):
                    for u in range(6):
                        if not (last and u == 5):
                            split(l, DN0, i, 6, u + 1)
                        if u % 3 == 2:
                            j = u // 3
                            computed(l, DN0, i, 6, u)
                            residual(l, (gate, af)[j][:], j, i, i * 2 + j, G2, Z_DN, l * 4 * KT + i * 4 + (2 * KT + 2 * j + 2))
                    st.restart()

                with dve.Fori(0, KT // 2 - 1) as i:
                    down(i, False)
                down(KT // 2 - 1, True)
                norm(l, 1, V_G2, V_B2)

        @block.tensor
        def _(pe):
            def product(l, base, i, n, u, hi, lo, k0, nk, z, first=True, last=True):
                j, seq, _ = unit(l, base, i, n, u)
                pe.wait_ge(s["lo_ready"], seq + 3)
                for k in range(nk):
                    w = slice(k * P, (k + 1) * P)
                    for t, (a, b) in enumerate(((w_hi, hi), (w_lo, hi), (w_hi, lo))):
                        for h in range(2):
                            ins = nc.tensor.matmul(z[:, h], a[:, j, w], b[:, k0 + k, h * H:(h + 1) * H],
                                                   start=first and k == 0 and t == 0, stop=last and k == nk - 1 and t == 2)
                ins.then_inc(s["w_used"], 1)

            def column_sums(src, stat, tiles, start=True, stop=True):
                for h in range(2):
                    for k in tiles:
                        ins = nc.tensor.matmul(stat[:, h], ones[:], src[:, k, h * H:(h + 1) * H],
                                               start=start and k == tiles[0], stop=stop and k == tiles[-1])
                return ins

            def norm(l, q, z0):
                for j in range(2):
                    pe.wait_ge(z_free[j], l * ZL + (z0 + KT // 2 + 1))
                column_sums(x, STAT[0], range(KT)).then_inc(s["ln_sum"], 1)
                half = KT // 2
                for c in range(2):
                    pe.wait_ge(s["ln_sq"], nth(l, "ln_sq", 2 * q + c))
                    ins = column_sums(sq, STAT[1], range(c * half, (c + 1) * half), c == 0, c == 1)
                ins.then_inc(s["ln_var"], 1)

            def ada_products(v, g, bank):
                pe.wait_ge(s["ada_sb"], v * 2 + (g + 1))
                for q in range(A_UNITS // 2):
                    pe.wait_ge(ada_in[q % A_SLOTS], v * 32 + (g + 1) * 16)
                    for k in range(2):
                        ins = nc.tensor.matmul(ps[0:NC_, bank, :], c_in[:, 2 * q + k, :], ada_w[q % A_SLOTS][:, k * 512:(k + 1) * 512],
                                               start=q + k == 0, stop=2 * q + k == KT - 1)
                    ins.then_inc(s["ada_used"], 1)

            def ada_turn(v, bank):
                pe.wait_ge(s["ada_out"], v + 1)
                behind(pe, s["ada_sb"], v * 2 + 4)
                for c in range(KT):
                    ins = nc.tensor.transpose(ps[:, bank, c * NC_:(c + 1) * NC_],
                                              ada_o[:, c // 4, c % 4 * P:(c % 4 + 1) * P], eye[0:NC_, 0:NC_])
                ins.then_inc(s["ada_t"], 1)

            pe.wait_ge(s["c_ready"], 1)
            pe.wait_ge(s["consts"], 16 * len(consts))
            with pe.Fori(0, V_EARLY) as v:
                for g in range(2):
                    ada_products(v, g, g)
                ada_turn(v, 2)
            with pe.Fori(0, DEPTH) as l:
                behind(pe, s["h_lo"], nth(l, "h_lo", KT))
                with pe.Fori(0, N_IN // 2) as i:
                    for u in range(2):
                        pe.wait_ge(z_free[u], z_before(l, i, Z_IN))
                        product(l, IN0, i, 2, u, h_hi, h_lo, 0, KT, Z[u])
                for j in range(2):
                    pe.wait_ge(z_free[j], l * ZL + (Z_OUT + 1))
                for t in range(QB + 1):
                    rows = P if t < QB else NS
                    if t == QB:
                        behind(pe, s["vnat_ready"], nth(l, "vnat_ready", 0))
                    for c in range(CT):
                        ins = nc.tensor.transpose(ps[0:rows, 4 + t % 4, c * P:(c + 1) * P], vT[:, c, t * P:t * P + rows], eye[:])
                    ins.then_inc(s["vt_ps"], 1)
                behind(pe, s["vnat_ready"], nth(l, "vnat_ready", QB))

                def head_scores(i, e):
                    f = slice(e * HD, (e + 1) * HD)
                    pe.wait_ge(s["s_free"], (l * NH + i * 2) * QB + (e + 1) * QB)
                    for q in range(QB):
                        bank, o = S_BANK[q]
                        ins = nc.tensor.matmul(ps[:, bank, o:o + (q + 1) * P], Qst[f, q * P:(q + 1) * P],
                                               Kst[f, 0:(q + 1) * P], start=True, stop=True)
                        if q:
                            ins.then_inc(s["s_ps"], 1)

                def scores(i):
                    pe.wait_ge(s["qk_staged"], l * CT + i + 1)
                    head_scores(i, 0)
                    for b in range(2):
                        rows = slice(b * HD, (b + 1) * HD)
                        pe.wait_ge(kc_in[b], (l * CT + i) * 16 + 16)
                        for c in range(CT):
                            nc.tensor.matmul(ps[rows, 3, :], Qbd[:, b, c, :], kc[:, b, c, :], start=c == 0, stop=c == CT - 1)
                        for c in range(CT):
                            ins = nc.tensor.matmul(ps[rows, 7, 0:NS], Qbd[:, b, c, :], qk[:, CT + c, SEQ:T],
                                                   start=c == 0, stop=c == CT - 1)
                    ins.then_inc(s["ss_ps"], 1)

                def pair(i):
                    def turn(e):
                        for k in range(QB):
                            pe.wait_ge(s["p_ready"], (l * NH + i * 2) * QB + (e + 1) * QB)
                            pe.wait_ge(s["pt_ready"], (l * NH + i * 2) * QB + (e * QB + k + 1))
                            for q in range(k, QB):
                                o = E_OFF[q] + k * P
                                ins = nc.tensor.transpose(ps[:, k % 2, (q - k) * P:(q - k + 1) * P], E[:, e, o:o + P], eye[:])
                            ins.then_inc(s["pt_ps"], 1)

                    def outputs(e):
                        f = slice(e * HD, (e + 1) * HD)
                        for k in range(QB):
                            n = (QB - k) * P
                            pe.wait_ge(s["pt_ready"], (l * NH + i * 2) * QB + (e * QB + k + 1 + FREE["pt_ready"]))
                            ins = nc.tensor.matmul(ps[f, 2, k * P:SEQ], Vst[:, k, f], PT[:, e, PT_OFF[k]:PT_OFF[k] + n],
                                                   start=k == 0, stop=k == QB - 1)
                        return ins

                    v = ada_before(l) + i
                    pe.wait_ge(s["o_free"], l * CT + i + 1)
                    ada_products(v, 0, 2)
                    head_scores(i, 1)
                    pe.wait_ge(s["pt_ready"], (l * NH + i * 2) * QB + FREE["pt_ready"])
                    ada_products(v, 1, 1)
                    pe.wait_ge(s["ada_sb"], v * 2 + 4)
                    pe.wait_ge(s["ada_out"], v + 1)
                    turn(0)
                    pe.wait_ge(s["v_staged"], l * CT + i + 1)
                    outputs(0)
                    turn(1)
                    outputs(1).then_inc(s["o_ps"], 1)
                    ada_turn(v, 0)
                    pe.wait_ge(s["ps_ready"], l * CT + i + 2)
                    for k in range(QB):
                        nc.tensor.transpose(ps[:, 3, k * P:(k + 1) * P], Es[:, k * P:(k + 1) * P], eye[:])
                    nc.tensor.transpose(ps[0:NS, 7, 0:P], Es[:, PAST:T], eye[:]).then_inc(s["pts_ps"], 1)
                    pe.wait_ge(s["pts_ready"], (l * CT + i) * 2 + 2)
                    for b in range(2):
                        rows = slice(b * HD, (b + 1) * HD)
                        pe.wait_ge(vc_in[b], (l * CT + i) * 16 + 16)
                        for k in range(QB):
                            nc.tensor.matmul(ps[rows, 3, :], PTs[:, k, rows], vc[:, b, k, :], start=k == 0, stop=False)
                        ins = nc.tensor.matmul(ps[rows, 3, :], PTs[0:NS, QB, rows], vnat[0:NS, QB, :], start=False, stop=True)
                    ins.then_inc(s["os_ps"], 1)
                    pe.wait_ge(s["os_ready"], l * CT + i + 1)
                    for c in range(CT):
                        ins = nc.tensor.transpose(ps[:, 7, c * P:(c + 1) * P], Os[:, c * P:(c + 1) * P], eye[:])
                    ins.then_inc(s["ost_ps"], 1)

                scores(0)
                with pe.Fori(0, CT - 1) as i:
                    pair(i)
                    pe.wait_ge(s["o_done"], (l * CT + i) * 2 + 2)
                    scores(i + 1)
                pair(CT - 1)
                pe.wait_ge(s["o_done"], nth(l, "o_done", 2 * CT - 1))
                for q in range(2):
                    pe.wait_ge(s["m_sq"], nth(l, "m_sq", q))
                    column_sums(sqm, STAT[1], range(CT)).then_inc(s["m_var"], 1)
                    if q == 0:
                        pe.wait_ge(s["conv_done"], nth(l, "conv_done", CT // 2 - 1))
                        pe.wait_ge(s["conv_dve"], nth(l, "conv_dve", CT // 2 - 1))
                        column_sums(y, STAT[0], range(CT)).then_inc(s["m_sum"], 1)
                        pe.wait_ge(s["m_sd"], nth(l, "m_sd", 0))
                pe.wait_ge(s["m_sd"], nth(l, "m_sd", 1))
                pe.wait_ge(s["m_sq"], nth(l, "m_sq", 2))
                column_sums(sqm, STAT[1], range(CT)).then_inc(s["m_var"], 1)
                behind(pe, s["m_lo"], nth(l, "m_lo", 2 * CT - 1))
                with pe.Fori(0, N_OUT // 2) as i:
                    for u in range(2):
                        pe.wait_ge(z_free[u], z_before(l, i, Z_OUT))
                        product(l, OUT0, i, 2, u, h_hi, h_lo, 0, KT, Z[u])
                norm(l, 0, Z_OUT)
                behind(pe, s["h_lo"], nth(l, "h_lo", 2 * KT + 1))
                with pe.Fori(0, FT) as i:
                    for u in range(2):
                        pe.wait_ge(z_free[u], z_before(l, i, Z_GU))
                        product(l, GU0, i, 2, u, h_hi, h_lo, 0, KT, Z[u])
                behind(pe, s["a_lo"], nth(l, "a_lo", FT - 1))
                with pe.Fori(0, KT // 2) as i:
                    for u in range(6):
                        r = u % 3
                        if r == 0:
                            pe.wait_ge(z_free[u // 3], z_before(l, i, Z_DN))
                        product(l, DN0, i, 6, u, a_hi, a_lo, sum(DN_K[:r]), DN_K[r], Z[u // 3], r == 0, r == 2)
                norm(l, 1, Z_DN)


def kernel(**v):
    import concourse.bacc as bacc
    from concourse.bass_utils import run_bass_kernel_spmd

    f = np.float32
    v = {k: np.asarray(a) for k, a in v.items()}

    def fm(a):
        return a.T.reshape(-1, P, a.shape[0]).transpose(1, 0, 2)

    def tiles(w):
        k, m = w.shape
        return w.reshape(k // P, P, m // P, P).transpose(2, 1, 0, 3).reshape(m // P, P, k)

    mix = []
    for l in range(DEPTH):
        wi = tiles(v["w_in"][l])
        wg, wu = tiles(v["w_gate"][l]), tiles(v["w_up"][l])
        g0 = 3 * CT
        glu = [wi[g0 + k] for c in range(CT) for k in (CT + c, c)]
        mix.append(np.stack(glu + list(wi[:g0]) + list(tiles(v["w_out"][l])) + [t for p in zip(wg, wu) for t in p]))
    vecs = []
    for l in range(DEPTH):
        cols = [v["conv_w"][l].T.reshape(CT, P, CW).transpose(1, 0, 2).reshape(P, -1)]
        for name in ("conv_b", "conv_ln_g", "conv_ln_b", "beta_attn", "beta_conv", "ln1_g", "ln1_b", "ln2_g", "ln2_b"):
            cols.append(v[name][l].reshape(-1, P).T)
        vecs.append(np.concatenate(cols, axis=1))

    wa = v["w_ada"].reshape(DEPTH, KT // 2, 2, P, 6, 2, 512).transpose(0, 4, 5, 1, 3, 2, 6).reshape(DEPTH, 6, A_UNITS, P, UNIT)
    ba = v["b_ada"].reshape(DEPTH, 6, KT, P)
    ba = np.concatenate([ba[:, 0:2].reshape(-1, P), ba[:, 2:6].reshape(-1, P)]).T

    pos = np.concatenate([np.arange(SEQ), np.tile(PAST + np.arange(NT), NB)]).astype(f)
    half = HD // 8
    inv = np.power(f(500000.0), -np.arange(half, dtype=f) * f(2.0) / f(2 * half)).astype(f)
    ang = (pos[None, :] * inv[:, None]).astype(f).astype(np.float64)
    cos, sin = np.ones((P, T)), np.zeros((P, T))
    for h0 in (0, HD):
        cos[h0:h0 + half] = cos[h0 + half:h0 + 2 * half] = np.cos(ang)
        sin[h0:h0 + half], sin[h0 + half:h0 + 2 * half] = -np.sin(ang), np.sin(ang)
    rope = np.stack([cos, sin], axis=1).astype(f)

    def masks(diff, bound4=PAST):
        ok = diff >= 0
        n = (ok & (diff <= 128)).astype(f) + (ok & (diff % 4 == 0) & (diff <= bound4)) + (ok & (diff % 16 == 0))
        return np.stack([np.where(n > 0, f(0), f(NEG)), n], axis=1).astype(f)

    i = np.arange(P)[:, None]
    mp = masks(np.concatenate([d * P + i - np.arange(P)[None] for d in range(QB - 1, -1, -1)], axis=1))
    t = i % NT
    msc = masks(PAST + t - np.arange(PAST)[None])
    msn = []
    for pair in range(CT):
        key = np.arange(NS)[None]
        same = key // NT == 2 * pair + i // HD
        msn.append(masks(np.where(same, t - key % NT, -1)))
    msn = np.stack(msn, axis=1)

    x_all = np.concatenate([v["x_prompt"][0], v["x_sample"].reshape(NS, D)], axis=0)
    c_all = np.concatenate([v["c_prompt"], v["c_sample"]], axis=0)
    ck = v["cache_k"].reshape(DEPTH, NB, PAST, CT, P).transpose(0, 1, 4, 3, 2)
    cv = v["cache_v"].reshape(DEPTH, NB, PAST // P, P, DA).transpose(0, 1, 3, 2, 4)
    sc = v["state_conv"].reshape(DEPTH, NB, HIST, CT, P).transpose(0, 4, 3, 1, 2)
    ins = dict(
        xT=fm(x_all), cT=fm(c_all), ba_d=ba, w_mod1=wa[:, 0:2].reshape(V_EARLY, A_UNITS, P, UNIT), w_mod2=wa[:, 2:6], w_mix=np.stack(mix),
        w_dn=np.stack([tiles(w) for w in v["w_down"]]), kc_d=ck, vc_d=cv, st_d=sc, vec_d=np.stack(vecs), rope_d=rope,
        eye_d=np.eye(P, dtype=f), mp_d=mp, msc_d=msc, msn_d=msn)
    outs = dict(y_d=(P, KT, T), k_d=(DEPTH, P, CT, T), v_d=(DEPTH, P, CT, T), cp_d=(DEPTH, P, CT, HIST),
                cs_d=(DEPTH, P, CT, NB, HIST))
    nc = bacc.Bacc("TRN2", target_bir_lowering=False, num_devices=1)
    arrays, args = {}, {}
    for name, a in ins.items():
        arrays[name] = np.ascontiguousarray(a)
        args[name] = nc.dram_tensor(name, a.shape, F32, kind="ExternalInput").ap()
    for name, shape in outs.items():
        args[name] = nc.dram_tensor(name, shape, F32, kind="ExternalOutput").ap()
    trunk(nc, **args)
    r = run_bass_kernel_spmd(nc, [arrays], core_ids=[0]).results[0]

    def rows(a):
        a = np.moveaxis(a, -1, -3)
        return np.swapaxes(a, -1, -2).reshape(*a.shape[:-2], -1)

    yy, kk, vv = rows(r["y_d"]), rows(r["k_d"]), rows(r["v_d"])
    heads = (NH, HD)
    cp = r["cp_d"].transpose(0, 3, 2, 1).reshape(DEPTH, 1, HIST, DA)
    cs = r["cs_d"].transpose(0, 3, 4, 2, 1).reshape(DEPTH, NB, HIST, DA)
    return (yy[None, :SEQ], yy[SEQ:].reshape(NB, NT, D),
            kk[:, None, :SEQ].reshape(DEPTH, 1, SEQ, *heads), vv[:, None, :SEQ].reshape(DEPTH, 1, SEQ, *heads), cp,
            kk[:, SEQ:].reshape(DEPTH, NB, NT, *heads), vv[:, SEQ:].reshape(DEPTH, NB, NT, *heads), cs)
```

```python
from contextlib import ExitStack

import numpy as np

import concourse.bass as bass
from concourse import mybir

F32 = mybir.dt.float32
F32R = mybir.dt.float32r
ACT = mybir.ActivationFunctionType
ALU = mybir.AluOpType

P = 128
D = 1024
DEPTH = 2
SEQ = 512
NB, NT = 8, 8
NS = NB * NT
T = SEQ + NS
H = T // 2
HP_ = SEQ - H
KT = D // P
HD = 64
NH = 8
DA = NH * HD
CT = DA // P
FF = 2816
FT = FF // P
CW = 31
HIST = CW - 1
PAST = 512
NVEC = CT * CW + 5 * CT + 4 * KT
EPS = 1e-5
ALPHA = (2 * DEPTH) ** 0.25
SCALE = HD ** -0.5
NEG = -1e30
LAG = 4
HF = 3
LEAST = -3.0e38
M_ORDER = [*range(4, 8), *range(4)]

UNIT = KT * P
N_IN, N_OUT, N_GU = 2 * CT + 3 * CT, KT, 2 * FT
DN_K = (8, 8, 6)
N_DN = KT * len(DN_K)
IN0 = 0
OUT0 = IN0 + N_IN
GU0 = OUT0 + N_OUT
DN0 = GU0 + N_GU
UL = DN0 + N_DN
NC_ = NB + 1
V_EARLY = 2 * DEPTH
V_LATE = 4
A_UNITS, A_SLOTS = KT, 4
Z_IN = 0
Z_OUT = Z_IN + N_IN // 2
Z_GU = Z_OUT + N_OUT // 2
Z_DN = Z_GU + N_GU // 2
ZL = Z_DN + KT // 2

V_CW = 0
V_CB = V_CW + CT * CW
V_CG = V_CB + CT
V_CLB = V_CG + CT
V_BA = V_CLB + CT
V_BC = V_BA + CT
V_G1 = V_BC + CT
V_B1 = V_G1 + KT
V_G2 = V_B1 + KT
V_B2 = V_G2 + KT
SH1, SC1 = 0, KT
G1, SH2, SC2, G2 = (j * KT for j in range(4))

QB = SEQ // P
E_OFF = [P * (q * (q + 1) // 2) for q in range(QB)]
E_ALL = P * QB * (QB + 1) // 2
PT_OFF = [0]
for _k in range(QB - 1):
    PT_OFF.append(PT_OFF[-1] + (QB - _k) * P)
S_BANK = [(4, 0), (4, P), (5, 0), (6, 0)]

SWAP = [i + 8 if i < 8 else i - 8 if i < 16 else i for i in range(32)]

KS = 3
PER = dict(lo_ready=UL, w_used=UL, hi_ready=UL, z_free=ZL, h_f=2 * KT, hs_f=2 * KT, h_hi=2 * KT, h_lo=2 * KT,
           rope_done=2 * CT, vt_ps=QB + 1, vnat_ready=QB + 1,
           q_zero=1, qk_staged=CT, v_staged=CT, s_ps=3 * NH, s_free=QB * NH, nm_ready=NH, exp_ready=QB * NH, p_ready=NH, pt_ps=QB * NH, pt_ready=QB * NH,
           o_ps=CT, o_free=CT, ss_ps=CT, nms_ready=CT, exps_ready=CT, ps_ready=CT, pts_ps=CT, pts_ready=2 * CT,
           os_ps=CT, os_ready=CT, ost_ps=CT, o_done=2 * CT, conv_done=CT // 2, conv_dve=1, m_sum=1, m_mean=1, m_cent=1, m_sq=4, m_var=4,
           m_sd=4, m_norm=1, cz=CT, m_f=2 * CT, m_hi=2 * CT, m_lo=2 * CT, gm_act=4 * KT, ln_sum=4, ln_mean=4,
           ln_cent=8, ln_acc=2, sq_half=1, vec_used=1,  ln_sq=8, ln_var=2, ln_rest=2, ln_sd=2, x_hat=2 * KT, sub_pool=2 * (KT - KS), ln_done=2 * KT, a_hi=FT, a_lo=FT, hist_zero=1)
FREE = dict(lo_ready=2, w_used=2, z_free=1, ada_used=A_SLOTS, ada_sb=2, ada_t=1, ada_out=1, s_free=QB, s_ps=6, pt_ps=2 * QB,
            pt_ready=2, o_ps=1, o_free=1, ss_ps=1, ps_ready=1, pts_ps=1, os_ps=1, rope_done=2, conv_done=1, x_hat=KT, vec_used=1, h_lo=HF, a_lo=1)


class Steps:

    def __init__(self, eng, sem):
        self.eng, self.sem, self.n = eng, sem, 0

    def of(self, ins):
        ins.then_inc(self.sem, 1)
        self.n += 1
        return self.n

    def wait(self, n):
        self.eng.wait_ge(self.sem, n)

    def link(self, ins):
        self.wait(self.of(ins))

    def restart(self):
        if self.n:
            self.wait(self.n)
            self.eng.sem_clear(self.sem)
            self.n = 0


def trunk(nc, xT, cT, ba_d, w_mod1, w_mod2, w_mix, w_dn, kc_d, vc_d, st_d, vec_d, rope_d, eye_d, mp_d, msc_d, msn_d,
          y_d, k_d, v_d, cp_d, cs_d):
    with ExitStack() as ctx:
        def sb(name, shape, dt=F32, where=ctx):
            return where.enter_context(nc.sbuf_tensor("sb_" + name, shape, dt))

        sems = {}
        for name in list(PER) + ["first_consts", "consts", "kc0", "kc1", "vc0", "vc1", "hist", "c_ready", "w_in0", "w_in1", "vec_in", "ada_used", "ada_sb", "ada_t", "ada_out", "mod_ready",
                                 "act_steps", "dve_steps", "pool_steps", "k_st", "v_st", "cv_st", "y_st", "carrier", "z_free1"]:
            sems[name] = ctx.enter_context(nc.semaphore(name))
        w_in = [sems["w_in0"], sems["w_in1"]]
        ada_in = [ctx.enter_context(nc.semaphore(f"ada_in{j}")) for j in range(A_SLOTS)]
        z_free = [sems["z_free"], sems["z_free1"]]
        kc_in = [sems["kc0"], sems["kc1"]]
        vc_in = [sems["vc0"], sems["vc1"]]

        def behind(eng, sem, value):
            eng.wait_ge(sem, value)
            eng.sem_inc(sems["carrier"], 1)

        def nth(l, name, k):
            return l * PER[name] + (k + 1 + FREE.get(name, 0))

        x = sb("x", [P, KT, T])
        w_raw = sb("w_raw", [P, 2, UNIT])
        with ExitStack() as a:
            ada_ring = sb("ada_ring", [P, 2, UNIT], where=a)
            ada_o = sb("ada_o", [NB + 1, 2, 512], where=a)
        w_hi = sb("w_hi", [P, 2, UNIT], F32R)
        w_lo = sb("w_lo", [P, 2, UNIT], F32R)
        eye = sb("eye", [P, P])
        ones = sb("ones", [P, P])
        rope = sb("rope", [P, 2, T])
        mp = sb("mp", [P, 2, SEQ])
        msc = sb("msc", [P, 2, PAST])
        msn = sb("msn", [P, CT, 2, NS])
        mod1 = sb("mod1", [P, (V_EARLY + 2) * KT, NC_])
        h_mul = sb("h_mul", [P, KT, NC_])
        h_add = sb("h_add", [P, KT, NC_])
        pend = sb("pend", [P, 2, KT])
        mod = sb("mod", [P, V_LATE * KT, NC_])
        b_ada = sb("b_ada", [P, (V_EARLY + DEPTH * V_LATE) * KT])
        vec = sb("vec", [P, NVEC])
        c_in = sb("c_in", [P, KT, NC_])
        small = sb("small", [P, 40])
        eps = small[:, 39:40]
        mx4, nm4, den4, rden4 = ([small[:, 8 * k + 4 * e:8 * k + 4 * e + 4] for e in range(2)] for k in range(4))
        mxs, dens, rdens, nms = small[:, 32:34], small[:, 34:36], small[:, 36:38], small[:, 38:39]
        with nc.sbuf_tensor("kc", [P, 2, CT, PAST], F32) as kc, nc.sbuf_tensor("vc", [P, 2, PAST // P, DA], F32) as vc:
            pass
        with ExitStack() as a:
            mean_h = sb("mean_h", [P, T], where=a)
            sq_h = sb("sq_h", [P, KT, T], where=a)
            acc_h = sb("acc_h", [P, T], where=a)
        h_hi = sb("h_hi", [P, KT, T], F32R)
        h_lo = sb("h_lo", [P, KT, T], F32R)
        with ExitStack() as a:
            qk = sb("qk", [P, 2 * CT, T], where=a)
            vT = sb("vT", [P, CT, T], where=a)
            vnat = sb("vnat", [P, QB + 1, DA], where=a)
            with ExitStack() as b:
                sqc = sb("sqc", [P, CT, T], where=b)
                meanc = sb("meanc", [P, T], where=b)
            uP = sb("uP", [P, CT, HIST + SEQ], where=a)
            uS = sb("uS", [P, CT, NB, HIST + NT], where=a)
            y = sb("y", [P, CT, T], where=a)
            oT = sb("oT", [P, CT, T], where=a)
            with ExitStack() as b:
                sg = sb("sg", [P, T], where=b)
                zraw = sb("zraw", [P, 2, T], where=b)
                zcos = sb("zcos", [P, T], where=b)
                zswap = sb("zswap", [P, T], where=b)
            with ExitStack() as b:
                E = sb("E", [P, 2, E_ALL], where=b)
                PT = sb("PT", [P, 2, E_ALL], where=b)
                Es = sb("Es", [P, T], where=b)
                PTs = sb("PTs", [P, QB + 1, P], where=b)
                Os = Es[:, 0:DA]
                Qbd = sb("Qbd", [P, 2, CT, NH * NT], where=b)
                Qst = sb("Qst", [P, SEQ], where=b)
                Kst = sb("Kst", [P, SEQ], where=b)
                Vst = sb("Vst", [P, QB, P], where=b)
                mnst = sb("mnst", [P, 2, NS], where=b)
                with ExitStack() as d:
                    sdc = sb("sdc", [P, T], where=d)
                    rstdc = sb("rstdc", [P, T], where=d)
                uPst = sb("uPst", [P, HIST + SEQ], where=b)
                uSst = sb("uSst", [P, NB, HIST + NT], where=b)
                cwst = sb("cwst", [P, CW + 1], where=b)
                yst = sb("yst", [P, 2, T], where=b)
            with ExitStack() as b:
                sqm = sb("sqm", [P, CT, T], where=b)
                sdm = sb("sdm", [P, T], where=b)
                rstdm = sb("rstdm", [P, T], where=b)
                mt = sb("mt", [P, 2, T], where=b)
                gm = sb("gm", [P, 2, T], where=b)
        with ExitStack() as a:
            a_hi = sb("a_hi", [P, FT, T], F32R, where=a)
            a_lo = sb("a_lo", [P, FT, T], F32R, where=a)
            gate = sb("gate", [P, T], where=a)
            af = sb("af", [P, T], where=a)
        with ExitStack() as a:
            sq_x = sb("sq_x", [P, KT, T], where=a)
            mean_x = sb("mean_x", [P, T], where=a)
            rest = sb("rest", [P, T], where=a)
            rest2 = sb("rest2", [P, T], where=a)
            sd = sb("sd", [P, T], where=a)
            rstd = sb("rstd", [P, T], where=a)
            hf = sb("hf", [P, HF, T], where=a)
            acc_x = sb("acc_x", [P, T], where=a)
        SQ, MEAN, ACC = (sq_x, sq_h), (mean_x, mean_h), (acc_x, acc_h)
        KM = 6
        CENTRED = ((0, 3), (3, 6), (6, 7), (7, 8))
        ps = ctx.enter_context(nc.psum_tensor("ps", [P, 8, 512], F32))
        Z = [ps[:, 0:2, 0:H], ps[:, 2:4, 0:H]]
        CONV_STAT = ps[:, 0:2, 0:H]
        STAT = [ps[:, 4:6, 0:H], ps[:, 6:8, 0:H]]

        ada_w = [w_raw[:, 0], w_raw[:, 1], ada_ring[:, 0], ada_ring[:, 1]]

        def halves(t):
            return t.rearrange("p (h n) -> p h n", h=2)

        def by_seq(t):
            return t.rearrange("p (b t) -> p b t", b=NB)

        def ada_before(l):
            return l * V_LATE + V_EARLY

        def unit(l, base, i, s, u):
            return u % 2, l * UL + i * s + (base + u), l * (UL // 2) + i * (s // 2) + (base // 2 + u // 2)

        def z_taken(l, i, z0):
            return l * ZL + i + (z0 + 2)

        def z_before(l, i, z0):
            return l * ZL + i + (z0 + 1)

        first_consts = [(c_in[:], cT), (b_ada[:], ba_d), (eye[:], eye_d)]
        consts = [(x[:], xT), (rope[:], rope_d), (mp[:], mp_d), (msc[:], msc_d), (msn[:], msn_d)]
        s = sems
        block = ctx.enter_context(nc.Block())

        @block.sync
        def _(sp):
            for name, n in FREE.items():
                sp.sem_inc(s[name], n)
            sp.sem_inc(s["z_free1"], 1)
            for dst, src in first_consts:
                sp.dma_start(dst, src).then_inc(s["first_consts"], 16)

            def fetch(l, base, i, st, u, src, n=UNIT):
                j, seq, _ = unit(l, base, i, st, u)
                sp.wait_ge(s["lo_ready"], seq + 1)
                sp.dma_start(w_raw[:, j, 0:n], src).then_inc(w_in[j], 16)

            def fetch_ada(v, src):
                for q in range(A_UNITS):
                    sp.wait_ge(s["ada_used"], v * A_UNITS + (q + 1))
                    sp.dma_start(ada_w[q % A_SLOTS], src(q)).then_inc(ada_in[q % A_SLOTS], 16)

            with sp.Fori(0, V_EARLY) as v:
                fetch_ada(v, lambda q: w_mod1[v, q])
            with sp.Fori(0, DEPTH) as l:
                behind(sp, s["ada_used"], ada_before(l) * A_UNITS + A_SLOTS - 2)
                behind(sp, s["vec_used"], l + 1)
                sp.dma_start(vec[:], vec_d[l]).then_inc(s["vec_in"], 16)
                with sp.Fori(0, N_IN // 2) as i:
                    for u in range(2):
                        fetch(l, IN0, i, 2, u, w_mix[l, i * 2 + u])
                behind(sp, s["w_used"], nth(l, "w_used", OUT0 - 1))

                def keys(i):
                    sp.wait_ge(s["ss_ps"], l * CT + i + 1)
                    for b in range(2):
                        sp.dma_start(kc[:, b], kc_d[l, i * 2 + b]).then_inc(kc_in[b], 16)

                def values(i):
                    sp.wait_ge(s["os_ps"], l * CT + i + 1)
                    for b in range(2):
                        sp.dma_start(vc[:, b], vc_d[l, i * 2 + b]).then_inc(vc_in[b], 16)

                keys(0)
                with sp.Fori(0, CT - 1) as i:
                    fetch_ada(ada_before(l) + i, lambda q: w_mod2[l, i, q])
                    values(i)
                    keys(i + 1)
                fetch_ada(ada_before(l) + (CT - 1), lambda q: w_mod2[l, CT - 1, q])
                values(CT - 1)
                behind(sp, s["ada_used"], ada_before(l) * A_UNITS + (V_LATE * A_UNITS + A_SLOTS - 2))
                with sp.Fori(0, N_OUT // 2) as i:
                    for u in range(2):
                        fetch(l, OUT0, i, 2, u, w_mix[l, i * 2 + (N_IN + u)])
                with sp.Fori(0, N_GU // 2) as i:
                    for u in range(2):
                        fetch(l, GU0, i, 2, u, w_mix[l, i * 2 + (N_IN + N_OUT + u)])
                with sp.Fori(0, KT // 2) as i:
                    for u in range(6):
                        k0 = sum(DN_K[:u % 3]) * P
                        n = DN_K[u % 3] * P
                        fetch(l, DN0, i, 6, u, w_dn[l, i * 2 + u // 3, :, k0:k0 + n], n)
            for k in range(0, KT, 2):
                sp.wait_ge(s["ln_done"], 2 * KT * DEPTH + k + 2)
                sp.dma_start(y_d[:, k:k + 2], x[:, k:k + 2]).then_inc(s["y_st"], 16)
            sp.wait_ge(s["y_st"], 16 * KT // 2)
            sp.wait_ge(s["k_st"], 16 * DEPTH)
            sp.wait_ge(s["v_st"], 16 * DEPTH)
            sp.wait_ge(s["cv_st"], 32 * DEPTH)

        @block.gpsimd
        def _(pool):
            st = Steps(pool, s["pool_steps"])

            def modulate(l, q):
                for kt in range(KT):
                    hs, xs = by_seq(hf[:, kt % HF, SEQ:T]), by_seq(x[:, kt, SEQ:T])
                    pool.wait_ge(s["x_hat"], l * 2 * KT + (q * KT + kt + 1))
                    pool.wait_ge(s["h_lo"], l * 2 * KT + (q * KT + kt + 1))
                    st.link(nc.gpsimd.tensor_tensor(hs, xs, h_mul[:, kt, 1:].unsqueeze(2).to_broadcast([P, NB, NT]), ALU.mult))
                    nc.gpsimd.tensor_tensor(hs, hs, h_add[:, kt, 1:].unsqueeze(2).to_broadcast([P, NB, NT]), ALU.add)\
                        .then_inc(s["hs_f"], 1)
                st.restart()

            pool.wait_ge(s["mod_ready"], 1)
            pool.wait_ge(s["consts"], 16 * len(consts))
            with pool.Fori(0, DEPTH) as l:
                modulate(l, 0)
                behind(pool, s["w_used"], nth(l, "w_used", IN0))
                pool.dma_start(uS[:, :, :, 0:HIST], st_d[l]).then_inc(s["hist"], 16)
                nc.gpsimd.memset(uP[:, :, 0:HIST], 0.0).then_inc(s["hist_zero"], 1)
                st.link(nc.gpsimd.memset(Qbd[:], 0.0))
                st.restart()
                pool.sem_inc(s["q_zero"], 1)
                behind(pool, z_free[1], z_taken(l, CT - 1, Z_IN))
                behind(pool, s["hist_zero"], l + 1)
                pool.dma_start(cp_d[l], uP[:, :, SEQ:SEQ + HIST]).then_inc(s["cv_st"], 16)
                behind(pool, s["hist"], l * 16 + 16)
                pool.dma_start(cs_d[l], uS[:, :, :, NT:NT + HIST]).then_inc(s["cv_st"], 16)
                behind(pool, s["vec_in"], l * 16 + 16)
                with pool.Fori(0, CT // 2) as i:
                    st.of(nc.gpsimd.tensor_copy(uPst[:], uP[:, i, :]))
                    st.of(nc.gpsimd.tensor_copy(uSst[:], uS[:, i]))
                    st.of(nc.gpsimd.tensor_copy(cwst[:, 0:CW], vec[:, bass.ds(i * CW + V_CW, CW)]))
                    st.link(nc.gpsimd.tensor_copy(cwst[:, CW:CW + 1], vec[:, bass.ds(i + V_CB, 1)]))
                    acc, prod = yst[:, 0], yst[:, 1]
                    for w in range(CW):
                        up, us, tap = uPst[:, w:w + SEQ], uSst[:, :, w:w + NT], cwst[:, w:w + 1]
                        if w == 0:
                            st.of(nc.gpsimd.tensor_scalar(acc[:, 0:SEQ], up, tap, cwst[:, CW:CW + 1], ALU.mult, ALU.add))
                            st.link(nc.gpsimd.tensor_scalar(by_seq(acc[:, SEQ:T]), us, tap, cwst[:, CW:CW + 1], ALU.mult, ALU.add))
                            continue
                        st.of(nc.gpsimd.tensor_tensor(prod[:, 0:SEQ], up, tap.to_broadcast([P, SEQ]), ALU.mult))
                        st.link(nc.gpsimd.tensor_tensor(by_seq(prod[:, SEQ:T]), us, tap.unsqueeze(2).to_broadcast([P, NB, NT]), ALU.mult))
                        st.link(nc.gpsimd.tensor_tensor(acc, acc, prod, ALU.add))
                    st.restart()
                    nc.gpsimd.tensor_copy(y[:, i, :], acc).then_inc(s["conv_done"], 1)
                    behind(pool, s["conv_done"], l * CT // 2 + i + 2)
                behind(pool, s["rope_done"], nth(l, "rope_done", 2 * CT - 1))
                pool.dma_start(k_d[l], qk[:, CT:2 * CT, :]).then_inc(s["k_st"], 16)
                for j in range(2):
                    behind(pool, z_free[j], l * ZL + (Z_OUT + 1))
                pool.dma_start(v_d[l], vT[:]).then_inc(s["v_st"], 16)
                for q, z0 in enumerate((Z_OUT, Z_DN)):
                    for m in range(1, KM):
                        behind(pool, z_free[m % 2], z_taken(l, m // 2, z0))
                        st.wait(st.n)
                        st.of(nc.gpsimd.tensor_tensor(ACC[q][:], (x[:, 0] if m == 1 else ACC[q][:]), x[:, m], ALU.add))
                    st.restart()
                    pool.sem_inc(s["ln_acc"], 1)
                    if q:
                        pool.wait_ge(s["ln_sq"], nth(l, "ln_sq", 4 * q + 1))
                        a, b = (slice(*CENTRED[c]) for c in range(2))
                        nc.gpsimd.tensor_tensor(SQ[q][:, a], SQ[q][:, a], SQ[q][:, b], ALU.add).then_inc(s["sq_half"], 1)
                    pool.wait_ge(s["ln_mean"], nth(l, "ln_mean", 2 * q + 1))
                    for k in range(KS, KT):
                        pool.wait_ge(s["ln_sq"], nth(l, "ln_sq", 4 * q + max(k - 4, 1)))
                        nc.gpsimd.tensor_tensor(x[:, k], x[:, k], rest[:], ALU.subtract).then_inc(s["sub_pool"], 1)
                    if q == 0:
                        modulate(l, 1)

        @block.scalar
        def _(act):
            st = Steps(act, s["act_steps"])

            def split(l, base, i, n, u):
                j, seq, half = unit(l, base, i, n, u)
                act.wait_ge(w_in[j], half * 16 + 16)
                act.wait_ge(s["w_used"], seq + 1)
                nc.scalar.activation(w_hi[:, j, :], w_raw[:, j, :], ACT.Copy).then_inc(s["hi_ready"], 1)

            def computed(l, base, i, n, u):
                act.wait_ge(s["w_used"], unit(l, base, i, n, u)[1] + 3)

            def modulate(l, q):
                for kt in range(KT + 1):
                    if kt < KT:
                        act.wait_ge(s["x_hat"], l * 2 * KT + (q * KT + kt + 1))
                        act.wait_ge(s["h_lo"], l * 2 * KT + (q * KT + kt + 1))
                        nc.scalar.activation(hf[:, kt % HF, 0:SEQ], x[:, kt, 0:SEQ], ACT.Identity, scale=h_mul[:, kt, 0:1],
                                             bias=h_add[:, kt, 0:1]).then_inc(s["h_f"], 1)
                    if kt:
                        k = kt - 1
                        act.wait_ge(s["h_f"], nth(l, "h_f", q * KT + k))
                        act.wait_ge(s["hs_f"], nth(l, "hs_f", q * KT + k))
                        nc.scalar.activation(h_hi[:, k, :], hf[:, k % HF, :], ACT.Copy).then_inc(s["h_hi"], 1)

            def restore(kt, g, b):
                xt = x[:, bass.ds(kt, 1), :].rearrange("p o n -> p (o n)")
                nc.scalar.activation(xt, xt, ACT.Identity, scale=g[:, bass.ds(kt, 1)], bias=b[:, bass.ds(kt, 1)])\
                    .then_inc(s["ln_done"], 1)

            def m_parts(l, n0, n1):
                for n in range(n0, n1):
                    act.wait_ge(s["m_f"], nth(l, "m_f", n))
                    nc.scalar.activation(h_hi[:, M_ORDER[n], :], mt[:, n % 2, :], ACT.Copy).then_inc(s["m_hi"], 1)

            def gated(l, dst, u, m, g):
                scale = mod[:, bass.ds(m + g, 1), 0] if not isinstance(m, int) else mod[:, m + g, 0:1]
                nc.scalar.activation(dst[:, 0:H], Z[u][:, 0], ACT.Copy, scale=scale).then_inc(s["gm_act"], 1)
                nc.scalar.activation(dst[:, H:SEQ], Z[u][:, 1, 0:HP_], ACT.Copy, scale=scale).then_inc(s["gm_act"], 1)

            def squares(l, q, c):
                act.wait_ge(s["ln_cent"], nth(l, "ln_cent", 4 * q + c))
                part = slice(*CENTRED[c])
                nc.scalar.activation(SQ[q][:, part], x[:, part], ACT.Square).then_inc(s["ln_sq"], 1)

            def norm_first(l, q, n):
                act.wait_ge(s["ln_sum"], nth(l, "ln_sum", 2 * q))
                nc.scalar.activation(halves(MEAN[q][:]), STAT[0], ACT.Copy, scale=1.0 / (KM * P)).then_inc(s["ln_mean"], 1)
                for c in range(n):
                    squares(l, q, c)

            def norm_last(l, q, n, ahead):
                for c in range(n, 4):
                    squares(l, q, c)
                ahead()
                act.wait_ge(s["ln_sum"], nth(l, "ln_sum", 2 * q + 1))
                nc.scalar.activation(halves(rest[:]), STAT[0], ACT.Copy, scale=1.0 / D).then_inc(s["ln_mean"], 1)
                act.wait_ge(s["ln_rest"], nth(l, "ln_rest", q))
                nc.scalar.activation(sd[:], rest2[:], ACT.Sqrt, bias=eps).then_inc(s["ln_sd"], 1)

            def ada_copy(v, g, bank):
                act.wait_ge(s["ada_used"], v * A_UNITS + (A_SLOTS + (g + 1) * A_UNITS // 2))
                act.wait_ge(s["ada_t"], v + 1)
                nc.scalar.activation(ada_o[:, g], ps[0:NC_, bank, :], ACT.Copy).then_inc(s["ada_sb"], 1)

            act.wait_ge(s["first_consts"], 16 * len(first_consts))
            nc.scalar.activation(c_in[:], c_in[:], ACT.Silu).then_inc(s["c_ready"], 1)
            for v in range(V_EARLY):
                for g in range(2):
                    ada_copy(v, g, g)
                for dst, src in (consts[0:1], consts[1:2], consts[2:], ())[v]:
                    act.dma_start(dst, src).then_inc(s["consts"], 16)
            act.wait_ge(s["mod_ready"], 1)
            act.wait_ge(s["consts"], 16 * len(consts))
            with act.Fori(0, DEPTH) as l:
                act.wait_ge(s["ada_used"], ada_before(l) * A_UNITS + A_SLOTS)
                for u in range(2):
                    split(l, IN0, 0, 2, u)
                modulate(l, 0)
                nc.scalar.preload_act_table(ACT.Sigmoid)
                with act.Fori(0, CT) as i:
                    computed(l, IN0, i, 2, 0)
                    act.wait_ge(z_free[1], z_before(l, i, Z_IN))
                    nc.scalar.activation(halves(sg[:]), Z[0], ACT.Sigmoid).then_inc(z_free[0], 1)
                    split(l, IN0, i, 2, 2)
                    split(l, IN0, i, 2, 3)
                    for j in range(KT // CT):
                        restore(i * (KT // CT) + j, pend[:, 0], pend[:, 1])
                with act.Fori(0, CT) as i:
                    for u in range(2):
                        computed(l, IN0 + 2 * CT, i, 2, u)
                        act.wait_ge(s["rope_done"], l * 2 * CT + i * 2 + (u + 1))
                        nc.scalar.activation(halves(zraw[:, u]), Z[u], ACT.Copy).then_inc(z_free[u], 1)
                        split(l, IN0 + 2 * CT, i, 2, u + 2)
                for u in range(CT):
                    computed(l, IN0 + 4 * CT, 0, 2, u)
                    nc.scalar.activation(halves(vT[:, u]), Z[u % 2], ACT.Copy).then_inc(z_free[u % 2], 1)
                    if u < CT - 2:
                        split(l, IN0 + 4 * CT, 0, 2, u + 2)
                for t in range(QB + 1):
                    rows = P if t < QB else NS
                    act.wait_ge(s["vt_ps"], nth(l, "vt_ps", t))
                    nc.scalar.activation(vnat[0:rows, t, :], ps[0:rows, 4 + t % 4, :], ACT.Copy).then_inc(s["vnat_ready"], 1)
                nc.scalar.preload_act_table(ACT.Exp)

                def attend(i, last):
                    def exps(e):
                        act.wait_ge(s["nm_ready"], l * NH + i * 2 + (e + 1))
                        for q in range(QB):
                            blk = E[:, e, E_OFF[q]:E_OFF[q] + (q + 1) * P]
                            nc.scalar.activation(blk, blk, ACT.Exp, bias=nm4[e][:, q:q + 1], scale=SCALE)\
                                .then_inc(s["exp_ready"], 1)

                    exps(0)
                    act.wait_ge(s["nms_ready"], l * CT + i + 1)
                    nc.scalar.activation(Es[:], Es[:], ACT.Exp, bias=nms, scale=SCALE).then_inc(s["exps_ready"], 1)
                    if last:
                        act.wait_ge(s["cv_st"], l * 32 + 32)
                        act.wait_ge(s["conv_done"], nth(l, "conv_done", CT // 2 - 1))
                        act.wait_ge(s["conv_dve"], l + 1)
                        act.wait_ge(s["m_sum"], l + 1)
                        nc.scalar.activation(halves(meanc[:]), CONV_STAT, ACT.Copy, scale=1.0 / DA).then_inc(s["m_mean"], 1)
                        act.wait_ge(s["m_cent"], l + 1)
                        nc.scalar.activation(sqc[:], y[:], ACT.Square).then_inc(s["m_sq"], 1)
                    exps(1)
                    if last:
                        root(0, CONV_STAT, halves(sdc[:]))
                    ada_copy(ada_before(l) + i, 0, 2)
                    for e in range(2):
                        if last and e:
                            act.wait_ge(s["m_norm"], l + 1)
                        for k in range(QB):
                            n = (QB - k) * P
                            act.wait_ge(s["pt_ps"], (l * NH + i * 2) * QB + (e * QB + k + 1 + FREE["pt_ps"]))
                            nc.scalar.activation(PT[:, e, PT_OFF[k]:PT_OFF[k] + n], ps[:, k % 2, 0:n], ACT.Copy)\
                                .then_inc(s["pt_ready"], 1)
                            if last and e:
                                nc.scalar.activation(y[:, k, :], y[:, k, :], ACT.Silu, scale=vec[:, V_CG + k:V_CG + k + 1],
                                                     bias=vec[:, V_CLB + k:V_CLB + k + 1]).then_inc(s["cz"], 1)
                    ada_copy(ada_before(l) + i, 1, 6)
                    act.wait_ge(s["o_ps"], l * CT + i + 2)
                    nc.scalar.activation(oT[:, i, 0:SEQ], ps[:, 2, :], ACT.Copy).then_inc(s["o_free"], 1)
                    act.wait_ge(s["pts_ps"], l * CT + i + 2)
                    nc.scalar.activation(PTs[:, 0:QB, :], ps[:, 3, :].rearrange("p (k n) -> p k n", k=QB), ACT.Copy)\
                        .then_inc(s["pts_ready"], 1)
                    nc.scalar.activation(PTs[0:NS, QB, :], ps[0:NS, 7, 0:P], ACT.Copy).then_inc(s["pts_ready"], 1)
                    if last:
                        act.wait_ge(s["cz"], nth(l, "cz", CT - 1))
                        nc.scalar.activation(sqc[:], y[:], ACT.Square).then_inc(s["m_sq"], 1)
                        act.wait_ge(s["o_free"], nth(l, "o_free", CT - 1))
                        nc.scalar.activation(sqm[:, :, 0:SEQ], oT[:, :, 0:SEQ], ACT.Square).then_inc(s["m_sq"], 1)
                        act.wait_ge(s["ada_used"], ada_before(l) * A_UNITS + (V_LATE * A_UNITS + A_SLOTS))
                        for u in range(2):
                            split(l, OUT0, 0, 2, u)
                    act.wait_ge(s["os_ps"], l * CT + i + 2)
                    nc.scalar.activation(Os[:], ps[:, 3, :], ACT.Copy).then_inc(s["os_ready"], 1)
                    if last:
                        root(1, STAT[0], halves(sdc[:]))
                        root(2, ps[:, 2, :], sdm[:, 0:SEQ])
                    act.wait_ge(s["ost_ps"], l * CT + i + 1)
                    for e in range(2):
                        own = ps[e * HD:(e + 1) * HD, 7, e * NT:]
                        own = bass.AP(own.tensor, own.offset, [list(own.ap[0]), [P + 2 * NT, CT], [NH * NT, 2], [1, NT]])
                        nc.scalar.activation(
                            oT[e * HD:(e + 1) * HD, :, bass.ds(i * 2 * NT + SEQ, 2 * NT)]
                            .rearrange("p c (b t) -> p c b t", b=2), own, ACT.Copy).then_inc(s["o_done"], 1)

                def root(q, stat, dst):
                    act.wait_ge(s["m_var"], nth(l, "m_var", q))
                    nc.scalar.activation(dst, stat, ACT.Sqrt, scale=1.0 / DA, bias=eps).then_inc(s["m_sd"], 1)

                with act.Fori(0, CT - 1) as i:
                    attend(i, False)
                attend(CT - 1, True)
                act.wait_ge(s["o_done"], nth(l, "o_done", 2 * CT - 1))
                nc.scalar.activation(sqm[:, :, SEQ:T], oT[:, :, SEQ:T], ACT.Square).then_inc(s["m_sq"], 1)
                m_parts(l, 0, 2)
                root(3, ps[:, 3, 0:NS], sdm[:, SEQ:T])
                m_parts(l, 2, 2 * CT)

                def out_tile(i, u):
                    computed(l, OUT0, i, 2, u)
                    act.wait_ge(z_free[u], z_before(l, i, Z_OUT))
                    gated(l, gm[:, u], u, i * 2 + u, G1)

                with act.Fori(0, N_OUT // 2 - 1) as i:
                    for u in range(2):
                        out_tile(i, u)
                        split(l, OUT0, i, 2, u + 2)
                last = N_OUT // 2 - 1
                out_tile(last, 0)
                split(l, OUT0, last, 2, 2)
                act.wait_ge(s["k_st"], l * 16 + 16)
                act.wait_ge(s["v_st"], l * 16 + 16)
                act.wait_ge(s["cv_st"], l * 32 + 32)
                norm_first(l, 0, 1)
                out_tile(last, 1)
                norm_last(l, 0, 1, lambda: split(l, OUT0, last, 2, 3))
                modulate(l, 1)
                nc.scalar.preload_act_table(ACT.Silu)

                def gate_up(i, before):
                    computed(l, GU0, i, 2, 0)
                    act.wait_ge(z_free[1], z_before(l, i, Z_GU))
                    nc.scalar.activation(halves(gate[:]), Z[0], ACT.Silu).then_inc(z_free[0], 1)
                    split(l, GU0, i, 2, 2)
                    act.wait_ge(z_free[1], z_taken(l, i, Z_GU))
                    nc.scalar.activation(a_hi[:, i], af[:], ACT.Copy).then_inc(s["a_hi"], 1)
                    split(l, GU0, i, 2, 3)
                    if before:
                        restore(i, vec[:, V_G1:V_G1 + KT], vec[:, V_B1:V_B1 + KT])

                with act.Fori(0, KT) as i:
                    gate_up(i, True)
                with act.Fori(KT, FT) as i:
                    gate_up(i, False)

                def down(i, last):
                    for u in range(6):
                        if not (last and u >= 4):
                            split(l, DN0, i, 6, u + 2)
                        if u % 3 == 2:
                            computed(l, DN0, i, 6, u)
                            act.wait_ge(z_free[u // 3], z_before(l, i, Z_DN))
                            gated(l, (gate, af)[u // 3], u // 3, i * 2 + u // 3, G2)
                        if last and u == 2:
                            norm_first(l, 1, 3)

                with act.Fori(0, KT // 2 - 1) as i:
                    down(i, False)
                down(KT // 2 - 1, True)
                norm_last(l, 1, 3, lambda: None)
            for k in range(KT):
                act.wait_ge(s["x_hat"], DEPTH * 2 * KT + k + 1)
                restore(k, pend[:, 0], pend[:, 1])

        @block.vector
        def _(dve):
            st = Steps(dve, s["dve_steps"])

            def split(l, base, i, n, u):
                j, seq, _ = unit(l, base, i, n, u)
                dve.wait_ge(s["hi_ready"], seq + 1)
                nc.vector.tensor_tensor(w_lo[:, j, :], w_raw[:, j, :], w_hi[:, j, :].bitcast(F32), ALU.subtract)\
                    .then_inc(s["lo_ready"], 1)

            def computed(l, base, i, n, u):
                dve.wait_ge(s["w_used"], unit(l, base, i, n, u)[1] + 3)

            def affine(g, b, sc, sh):
                g, b = g.unsqueeze(2).to_broadcast([P, KT, NC_]), b.unsqueeze(2).to_broadcast([P, KT, NC_])
                st.of(nc.vector.tensor_tensor(h_mul[:], sc, g, ALU.mult))
                st.link(nc.vector.tensor_tensor(h_add[:], sc, b, ALU.mult))
                st.link(nc.vector.tensor_tensor(h_add[:], h_add[:], sh, ALU.add))

            def modulate(l, q, ahead, scale=None):
                for kt in range(-2, KT + 1):
                    if scale and kt + 2 < KT:
                        scale(kt + 2)
                    if kt == 0 and len(ahead) > 1:
                        ahead[0]()
                    if kt > 0:
                        k = kt - 1
                        dve.wait_ge(s["h_hi"], nth(l, "h_hi", q * KT + k))
                        nc.vector.tensor_tensor(h_lo[:, k, :], hf[:, k % HF, :], h_hi[:, k, :].bitcast(F32), ALU.subtract)\
                            .then_inc(s["h_lo"], 1)
                    if kt == 1:
                        ahead[-1]()

            def conv_tap(c, w, first=None):
                up = uP[:, c, bass.ds(w, SEQ)]
                us = uS[:, c, :, bass.ds(w, NT)]
                tap, bias = vec[:, bass.ds(w + (V_CW + c * CW), 1)], vec[:, V_CB + c:V_CB + c + 1]
                yp, ys = y[:, c, 0:SEQ], by_seq(y[:, c, SEQ:T])
                if isinstance(w, int) and w == 0:
                    st.of(nc.vector.tensor_scalar(yp, up, tap, bias, ALU.mult, ALU.add))
                    st.of(nc.vector.tensor_scalar(ys, us, tap, bias, ALU.mult, ALU.add))
                    return
                st.wait(st.n - 1)
                st.of(nc.vector.scalar_tensor_tensor(out=yp, in0=up, scalar=tap, in1=yp, op0=ALU.mult, op1=ALU.add))
                st.wait(st.n - 1)
                st.of(nc.vector.scalar_tensor_tensor(out=ys, in0=us, scalar=tap, in1=ys, op0=ALU.mult, op1=ALU.add))

            def residual(l, dst, u, i, m, g, z0, done_gm):
                out4 = Z[u][:, 1, HP_:H].rearrange("p (b t) -> p b t", b=NB)
                gs = mod[:, bass.ds(m + g, 1), 1:].rearrange("p o b -> p (o b)") if not isinstance(m, int) else mod[:, m + g, 1:]
                dve.wait_ge(s["gm_act"], done_gm)
                st.link(nc.vector.tensor_tensor(by_seq(dst[:, SEQ:T]), out4, gs.unsqueeze(2).to_broadcast([P, NB, NT]), ALU.mult))
                nc.vector.scalar_tensor_tensor(out=x[:, m, :], in0=x[:, m, :], scalar=ALPHA, in1=dst,
                                               op0=ALU.mult, op1=ALU.add).then_inc(z_free[u], 1)

            def centre(l, q, c):
                if c >= 2:
                    dve.wait_ge(z_free[c - 2], z_taken(l, KT // 2 - 1, (Z_OUT, Z_DN)[q]))
                part = slice(*CENTRED[c])
                n = part.stop - part.start
                nc.vector.tensor_tensor(x[:, part], x[:, part], MEAN[q][:].unsqueeze(1).to_broadcast([P, n, T]), ALU.subtract)\
                    .then_inc(s["ln_cent"], 1)

            def norm_first(l, q):
                dve.wait_ge(s["ln_mean"], nth(l, "ln_mean", 2 * q))
                for c in range(3):
                    centre(l, q, c)

            def norm_last(l, q):
                centre(l, q, 3)
                dve.wait_ge(s["ln_cent"], nth(l, "ln_cent", 4 * q + 3))

                def variance():
                    st.wait(squared)
                    dve.wait_ge(s["ln_var"], nth(l, "ln_var", q))
                    nc.vector.scalar_tensor_tensor(out=halves(rest2[:]), in0=STAT[1], scalar=1.0 / D, in1=halves(rest2[:]),
                                                   op0=ALU.mult, op1=ALU.subtract).then_inc(s["ln_rest"], 1)

                dve.wait_ge(s["ln_mean"], nth(l, "ln_mean", 2 * q + 1))
                squared = st.of(nc.vector.tensor_tensor(rest2[:], rest[:], rest[:], ALU.mult))
                for k in range(KS):
                    if k == 2 and q:
                        variance()
                    if k >= 3:
                        dve.wait_ge(s["ln_sq"], nth(l, "ln_sq", 4 * q + 1))
                    st.of(nc.vector.tensor_tensor(x[:, k], x[:, k], rest[:], ALU.subtract))
                if q == 0:
                    variance()
                st.wait(st.n)
                dve.wait_ge(s["ln_sd"], nth(l, "ln_sd", q))
                st.link(nc.vector.reciprocal(rstd[:], sd[:]))

            def normalise(l, q, k):
                if k >= KS:
                    dve.wait_ge(s["sub_pool"], nth(l, "sub_pool", q * (KT - KS) + k - KS))
                nc.vector.tensor_tensor(x[:, k], x[:, k], rstd[:], ALU.mult).then_inc(s["x_hat"], 1)

            st.of(nc.vector.memset(ones[:], 1.0))
            st.of(nc.vector.memset(eps, EPS))
            st.of(nc.vector.memset(pend[:, 0], 1.0))
            st.of(nc.vector.memset(pend[:, 1], 0.0))
            st.of(nc.vector.memset(mod1[:, V_EARLY * KT:], 0.0))
            def ada_bias(v, bank, dst, bias):
                dve.wait_ge(s["ada_t"], v + 2)
                nc.vector.tensor_tensor(dst, ps[:, bank, 0:KT * NC_].rearrange("p (k c) -> p k c", k=KT),
                                        bias.unsqueeze(2).to_broadcast([P, KT, NC_]), ALU.add).then_inc(s["ada_out"], 1)

            st.restart()
            dve.wait_ge(s["first_consts"], 16 * len(first_consts))
            with dve.Fori(0, V_EARLY) as v:
                ada_bias(v, 2, mod1[:, bass.ds(v * KT, KT)], b_ada[:, bass.ds(v * KT, KT)])
            dve.wait_ge(s["ada_out"], V_EARLY + FREE["ada_out"])
            for l in range(DEPTH):
                sc1 = mod1[:, 2 * l * KT + SC1:2 * l * KT + SC1 + KT]
                st.of(nc.vector.tensor_scalar(sc1, sc1, 1.0, None, ALU.add))
            st.wait(st.n)
            affine(pend[:, 0], pend[:, 1], mod1[:, SC1:SC1 + KT], mod1[:, SH1:SH1 + KT])
            st.restart()
            dve.sem_inc(s["mod_ready"], 1)
            with dve.Fori(0, DEPTH) as l:
                modulate(l, 0, [lambda: split(l, IN0, 0, 2, 0), lambda: split(l, IN0, 0, 2, 1)])
                st.restart()
                with dve.Fori(0, CT) as i:
                    split(l, IN0, i, 2, 2)
                    computed(l, IN0, i, 2, 1)
                    dve.wait_ge(z_free[0], z_taken(l, i, Z_IN))
                    st.of(nc.vector.tensor_tensor(uP[:, i, HIST:HIST + H], Z[1][:, 0], sg[:, 0:H], ALU.mult))
                    st.of(nc.vector.tensor_tensor(uP[:, i, HIST + H:HIST + SEQ], Z[1][:, 1, 0:HP_], sg[:, H:SEQ], ALU.mult))
                    st.restart()
                    nc.vector.tensor_tensor(uS[:, i, :, HIST:HIST + NT], by_seq(Z[1][:, 1, HP_:H]), by_seq(sg[:, SEQ:T]),
                                            ALU.mult).then_inc(z_free[1], 1)
                    split(l, IN0, i, 2, 3)
                with dve.Fori(0, CT) as i:
                    for u in range(2):
                        behind(dve, z_free[u], z_taken(l, i, Z_IN + CT))
                        st.of(nc.vector.stream_shuffle(zswap[:], zraw[:, u, :], SWAP))
                        st.of(nc.vector.tensor_tensor(zcos[:], zraw[:, u, :], rope[:, 0, :], ALU.mult))
                        st.wait(st.n - 1)
                        st.link(nc.vector.tensor_tensor(zswap[:], zswap[:], rope[:, 1, :], ALU.mult))
                        nc.vector.tensor_tensor(qk[:, i * 2 + u, :], zcos[:], zswap[:], ALU.add)\
                            .then_inc(s["rope_done"], 1)
                        behind(dve, s["rope_done"], l * 2 * CT + i * 2 + (u + 3))
                        st.restart()
                        split(l, IN0 + 2 * CT, i, 2, u + 2)
                behind(dve, s["vec_in"], l * 16 + 16)
                behind(dve, s["hist"], l * 16 + 16)
                behind(dve, s["hist_zero"], l + 1)
                for u in range(CT):
                    if u in (1, 2):
                        split(l, IN0 + 4 * CT, 0, 2, u + 1)
                    for w in range(u * 4, u * 4 + 4):
                        conv_tap(CT - 1, w)
                conv_tap(CT - 2, 0)

                def stage_scores(i):
                    st.of(nc.vector.tensor_copy(Qst[:], qk[:, i, 0:SEQ]))
                    st.of(nc.vector.tensor_copy(Kst[:], qk[:, i + CT, 0:SEQ]))
                    for e in range(2):
                        own = Qbd[e * HD:(e + 1) * HD, 0, 0, e * NT:]
                        own = bass.AP(own.tensor, own.offset, [list(own.ap[0]), [CT * NH * NT, 2], [NH * NT + 2 * NT, CT], [1, NT]])
                        st.of(nc.vector.tensor_copy(
                            own, qk[e * HD:(e + 1) * HD, 0:CT, bass.ds(i * 2 * NT + SEQ, 2 * NT)]
                            .rearrange("p c (b t) -> p b c t", b=2)))
                    st.wait(st.n)
                    dve.sem_inc(s["qk_staged"], 1)

                def stage_outputs(i):
                    dve.wait_ge(s["o_ps"], l * CT + i + 1)
                    st.of(nc.vector.tensor_copy(Vst[:], vnat[:, 0:QB, bass.ds(i * P, P)]))
                    st.of(nc.vector.tensor_copy(mnst[:], msn[:, i]))
                    st.wait(st.n)
                    dve.sem_inc(s["v_staged"], 1)

                def attend(i, last):
                    def head_max(e):
                        dve.wait_ge(s["pt_ps"], (l * NH + i * 2) * QB + (e + 1) * QB)
                        for q in range(QB):
                            w = (q + 1) * P
                            if q != 1:
                                behind(dve, s["s_ps"], l * 3 * NH + i * 6 + (3 * e + max(q, 1) + FREE["s_ps"]))
                            bank, o = S_BANK[q]
                            nc.vector.tensor_tensor_reduce(E[:, e, E_OFF[q]:E_OFF[q] + w], ps[:, bank, o:o + w],
                                                           mp[:, 0, SEQ - w:SEQ], 1.0, LEAST, ALU.add, ALU.max,
                                                           mx4[e][:, q:q + 1]).then_inc(s["s_free"], 1)
                        dve.wait_ge(s["s_free"], (l * NH + i * 2) * QB + ((e + 1) * QB + FREE["s_free"]))
                        nc.vector.tensor_scalar(nm4[e], mx4[e], -SCALE, None, ALU.mult).then_inc(s["nm_ready"], 1)

                    def head_prob(e):
                        for q in range(QB):
                            blk = E[:, e, E_OFF[q]:E_OFF[q] + (q + 1) * P]
                            behind(dve, s["exp_ready"], (l * NH + i * 2) * QB + (e * QB + q + 1))
                            st.of(nc.vector.tensor_tensor_reduce(blk, blk, mp[:, 1, SEQ - (q + 1) * P:SEQ], 1.0, 0.0, ALU.mult,
                                                                 ALU.add, den4[e][:, q:q + 1]))
                        st.wait(st.n)
                        st.link(nc.vector.reciprocal(rden4[e], den4[e]))
                        for q in range(QB):
                            blk = E[:, e, E_OFF[q]:E_OFF[q] + (q + 1) * P]
                            nc.vector.tensor_scalar(blk, blk, rden4[e][:, q:q + 1], None, ALU.mult).then_inc(s["p_ready"], 1)

                    head_max(0)
                    dve.wait_ge(s["pts_ps"], l * CT + i + 1)
                    behind(dve, s["ss_ps"], l * CT + i + 2)
                    st.link(nc.vector.tensor_tensor_reduce(Es[:, 0:PAST], ps[:, 3, :], msc[:, 0], 1.0, LEAST, ALU.add, ALU.max,
                                                           mxs[:, 0:1]))
                    st.link(nc.vector.tensor_tensor_reduce(Es[:, PAST:T], ps[:, 7, 0:NS], mnst[:, 0], 1.0, mxs[:, 0:1], ALU.add,
                                                           ALU.max, mxs[:, 1:2]))
                    nc.vector.tensor_scalar(nms, mxs[:, 1:2], -SCALE, None, ALU.mult).then_inc(s["nms_ready"], 1)
                    if last:
                        dve.wait_ge(s["m_mean"], l + 1)
                        nc.vector.tensor_tensor(y[:], y[:], meanc[:].unsqueeze(1).to_broadcast([P, CT, T]), ALU.subtract)\
                            .then_inc(s["m_cent"], 1)
                    head_max(1)
                    if not last:
                        stage_scores(i + 1)
                    head_prob(0)
                    behind(dve, s["exps_ready"], l * CT + i + 1)
                    st.link(nc.vector.tensor_tensor_reduce(Es[:, 0:PAST], Es[:, 0:PAST], msc[:, 1], 1.0, 0.0, ALU.mult, ALU.add,
                                                           dens[:, 0:1]))
                    st.link(nc.vector.tensor_tensor_reduce(Es[:, PAST:T], Es[:, PAST:T], mnst[:, 1], 1.0, dens[:, 0:1], ALU.mult,
                                                           ALU.add, dens[:, 1:2]))
                    st.link(nc.vector.reciprocal(rdens[:, 0:1], dens[:, 1:2]))
                    nc.vector.tensor_scalar(Es[:], Es[:], rdens[:, 0:1], None, ALU.mult).then_inc(s["ps_ready"], 1)
                    head_prob(1)
                    if last:
                        dve.wait_ge(s["m_sd"], nth(l, "m_sd", 0))
                        st.link(nc.vector.reciprocal(rstdc[:], sdc[:]))
                        dve.wait_ge(s["m_cent"], l + 1)
                        nc.vector.tensor_tensor(y[:], y[:], rstdc[:].unsqueeze(1).to_broadcast([P, CT, T]), ALU.mult)\
                            .then_inc(s["m_norm"], 1)
                    if not last:
                        st.wait(st.n)
                        for w in range((CW - 1) // 3):
                            conv_tap(CT - 2, i * ((CW - 1) // 3) + (w + 1))
                        st.wait(st.n)
                        for w in range((CW - 16) // 3):
                            conv_tap(CT - 1, i * ((CW - 16) // 3) + (w + 16))
                    ada_bias(ada_before(l) + i, 0, mod[:, bass.ds(i * KT, KT)],
                             b_ada[:, bass.ds(l * V_LATE * KT + (i * KT + V_EARLY * KT), KT)])
                    if not last:
                        stage_outputs(i + 1)
                    st.restart()

                behind(dve, s["q_zero"], l + 1)
                stage_scores(0)
                dve.wait_ge(s["vnat_ready"], nth(l, "vnat_ready", QB))
                stage_outputs(0)
                st.restart()
                with dve.Fori(0, CT - 1) as i:
                    attend(i, False)
                dve.sem_inc(s["conv_dve"], 1)
                attend(CT - 1, True)
                dve.wait_ge(s["ada_out"], ada_before(l) + (V_LATE + FREE["ada_out"]))
                st.of(nc.vector.tensor_scalar(mod[:, SC2:SC2 + KT, :], mod[:, SC2:SC2 + KT, :], 1.0, None, ALU.add))
                def invert(which, rstd_, sd_):
                    dve.wait_ge(s["m_sd"], nth(l, "m_sd", which))
                    st.link(nc.vector.reciprocal(rstd_, sd_))

                def scaled(n0, rstd_, src, beta, between=None):
                    for c in range(CT + 1):
                        if c < CT:
                            n = n0 + c
                            if n >= 2:
                                dve.wait_ge(s["m_lo"], nth(l, "m_lo", n - 2))
                            nc.vector.scalar_tensor_tensor(out=mt[:, n % 2, :], in0=src[:, c, :], scalar=vec[:, beta + c:beta + c + 1],
                                                           in1=rstd_[:], op0=ALU.mult, op1=ALU.mult).then_inc(s["m_f"], 1)
                        if c == 1 and between:
                            between()
                        if c:
                            n = n0 + c - 1
                            dve.wait_ge(s["m_hi"], nth(l, "m_hi", n))
                            nc.vector.tensor_tensor(h_lo[:, M_ORDER[n], :], mt[:, n % 2, :], h_hi[:, M_ORDER[n], :].bitcast(F32),
                                                    ALU.subtract).then_inc(s["m_lo"], 1)

                for u in range(2):
                    split(l, OUT0, 0, 2, u)
                invert(1, rstdc[:], sdc[:])
                scaled(0, rstdc, y, V_BC, lambda: invert(2, rstdm[:, 0:SEQ], sdm[:, 0:SEQ]))
                invert(3, rstdm[:, SEQ:T], sdm[:, SEQ:T])
                scaled(CT, rstdm, oT, V_BA)
                st.restart()
                behind(dve, s["ln_done"], nth(l, "ln_done", KT - 1))

                def out_tile(i, u):
                    computed(l, OUT0, i, 2, u)
                    residual(l, gm[:, u], u, i, i * 2 + u, G1, Z_OUT, l * 4 * KT + i * 4 + (2 * u + 2))

                with dve.Fori(0, N_OUT // 2 - 1) as i:
                    for u in range(2):
                        out_tile(i, u)
                        split(l, OUT0, i, 2, u + 2)
                    st.restart()
                last = N_OUT // 2 - 1
                out_tile(last, 0)
                split(l, OUT0, last, 2, 2)
                norm_first(l, 0)
                affine(vec[:, V_G1:V_G1 + KT], vec[:, V_B1:V_B1 + KT], mod[:, SC2:SC2 + KT], mod[:, SH2:SH2 + KT])
                out_tile(last, 1)
                norm_last(l, 0)
                modulate(l, 1, [lambda: split(l, OUT0, last, 2, 3)], lambda k: normalise(l, 0, k))
                st.restart()
                with dve.Fori(0, FT) as i:
                    split(l, GU0, i, 2, 2)
                    computed(l, GU0, i, 2, 1)
                    dve.wait_ge(z_free[0], z_taken(l, i, Z_GU))
                    dve.wait_ge(s["a_lo"], l * FT + i + FREE["a_lo"])
                    nc.vector.tensor_tensor(halves(af[:]), Z[1], halves(gate[:]), ALU.mult).then_inc(z_free[1], 1)
                    dve.wait_ge(s["a_hi"], l * FT + i + 1)
                    nc.vector.tensor_tensor(a_lo[:, i], af[:], a_hi[:, i].bitcast(F32), ALU.subtract).then_inc(s["a_lo"], 1)
                    split(l, GU0, i, 2, 3)

                behind(dve, s["ln_done"], nth(l, "ln_done", 2 * KT - 1))

                def down(i, last):
                    for u in range(6):
                        if not (last and u >= 4):
                            split(l, DN0, i, 6, u + 2)
                        if u % 3 == 2:
                            j = u // 3
                            computed(l, DN0, i, 6, u)
                            residual(l, (gate, af)[j][:], j, i, i * 2 + j, G2, Z_DN, l * 4 * KT + i * 4 + (2 * KT + 2 * j + 2))
                        if last and u == 2:
                            norm_first(l, 1)
                            sc = mod1[:, bass.ds(l * 2 * KT + (2 * KT + SC1), KT)]
                            sh = mod1[:, bass.ds(l * 2 * KT + (2 * KT + SH1), KT)]
                            affine(vec[:, V_G2:V_G2 + KT], vec[:, V_B2:V_B2 + KT], sc, sh)
                            for j, v0 in enumerate((V_G2, V_B2)):
                                st.of(nc.vector.tensor_copy(pend[:, j], vec[:, v0:v0 + KT]))
                            st.wait(st.n)
                            dve.sem_inc(s["vec_used"], 1)
                    st.restart()

                with dve.Fori(0, KT // 2 - 1) as i:
                    down(i, False)
                down(KT // 2 - 1, True)
                norm_last(l, 1)
                for k in range(KT):
                    normalise(l, 1, k)
                behind(dve, s["x_hat"], nth(l, "x_hat", 2 * KT - 1))
                st.restart()

        @block.tensor
        def _(pe):
            def product(l, base, i, n, u, hi, lo, k0, nk, z, first=True, last=True):
                j, seq, _ = unit(l, base, i, n, u)
                pe.wait_ge(s["lo_ready"], seq + 3)
                for k in range(nk):
                    w = slice(k * P, (k + 1) * P)
                    for t, (a, b) in enumerate(((w_hi, hi), (w_lo, hi), (w_hi, lo))):
                        for h in range(2):
                            ins = nc.tensor.matmul(z[:, h], a[:, j, w], b[:, k0 + k, h * H:(h + 1) * H],
                                                   start=first and k == 0 and t == 0, stop=last and k == nk - 1 and t == 2)
                ins.then_inc(s["w_used"], 1)

            def products_by_tile(l, base, order, parts_ready):
                for step in range(KT + LAG):
                    if step in (0, LAG):
                        pe.wait_ge(s["lo_ready"], unit(l, base, 0, 2, step // LAG)[1] + 3)
                    if step < KT:
                        parts_ready(step)
                    for u in range(2):
                        n = step - u * LAG
                        if not 0 <= n < KT:
                            continue
                        k = order[n]
                        w = slice(k * P, (k + 1) * P)
                        for t, (a, b) in enumerate(((w_hi, h_hi), (w_lo, h_hi), (w_hi, h_lo))):
                            for h in range(2):
                                ins = nc.tensor.matmul(Z[u][:, h], a[:, u, w], b[:, k, h * H:(h + 1) * H],
                                                       start=n == 0 and t == 0, stop=n == KT - 1 and t == 2)
                        if n == KT - 1:
                            ins.then_inc(s["w_used"], 1)

            def h_ready(l, q):
                return lambda n: pe.wait_ge(s["h_lo"], nth(l, "h_lo", q * KT + n))

            def column_sums(src, stat, tiles, start=True, stop=True):
                for h in range(2):
                    for k in tiles:
                        ins = nc.tensor.matmul(stat[:, h], ones[:], src[:, k, h * H:(h + 1) * H],
                                               start=start and k == tiles[0], stop=stop and k == tiles[-1])
                return ins

            def norm_first(l, q, z0):
                pe.wait_ge(z_free[0], l * ZL + (z0 + KT // 2))
                pe.wait_ge(z_free[1], l * ZL + (z0 + KT // 2))
                pe.wait_ge(s["ln_acc"], nth(l, "ln_acc", q))
                for h in range(2):
                    ins = nc.tensor.matmul(STAT[0][:, h], ones[:], ACC[q][:, h * H:(h + 1) * H], start=True, stop=True)
                ins.then_inc(s["ln_sum"], 1)

            def norm_tile(l, q):
                pe.wait_ge(s["ln_mean"], nth(l, "ln_mean", 2 * q))
                pe.wait_ge(s["ln_cent"], nth(l, "ln_cent", 4 * q + 2))
                column_sums(x, STAT[0], (KM,), True, False)

            def norm_last(l, q, before, after):
                for c in before:
                    norm_squares(l, q, c, q == 0 and c == before[0])
                pe.wait_ge(s["ln_cent"], nth(l, "ln_cent", 4 * q + 3))
                column_sums(x, STAT[0], (KM + 1,), False, True).then_inc(s["ln_sum"], 1)
                for c in after:
                    ins = norm_squares(l, q, c, False, c == after[-1])
                ins.then_inc(s["ln_var"], 1)

            def norm_squares(l, q, c, first, last=False):
                pe.wait_ge(s["ln_sq"], nth(l, "ln_sq", 4 * q + c))
                return column_sums(SQ[q], STAT[1], range(*CENTRED[c]), first, last)

            def ada_unit(v, g, q, bank):
                pe.wait_ge(s["ada_sb"], v * 2 + (g + 1))
                pe.wait_ge(ada_in[q % A_SLOTS], v * 32 + (g + 1) * 16)
                for k in range(2):
                    ins = nc.tensor.matmul(ps[0:NC_, bank, :], c_in[:, 2 * q + k, :], ada_w[q % A_SLOTS][:, k * 512:(k + 1) * 512],
                                           start=q + k == 0, stop=2 * q + k == KT - 1)
                ins.then_inc(s["ada_used"], 1)

            def ada_turn(v, bank):
                pe.wait_ge(s["ada_out"], v + 1)
                behind(pe, s["ada_sb"], v * 2 + 4)
                for c in range(KT):
                    ins = nc.tensor.transpose(ps[:, bank, c * NC_:(c + 1) * NC_],
                                              ada_o[:, c // 4, c % 4 * P:(c % 4 + 1) * P], eye[0:NC_, 0:NC_])
                ins.then_inc(s["ada_t"], 1)

            pe.wait_ge(s["c_ready"], 1)
            with pe.Fori(0, V_EARLY) as v:
                for g in range(2):
                    for q in range(A_UNITS // 2):
                        ada_unit(v, g, q, g)
                ada_turn(v, 2)
            with pe.Fori(0, DEPTH) as l:
                for u in range(2):
                    pe.wait_ge(z_free[u], z_before(l, 0, Z_IN))
                products_by_tile(l, IN0, range(KT), h_ready(l, 0))
                with pe.Fori(1, N_IN // 2) as i:
                    for u in range(2):
                        pe.wait_ge(z_free[u], z_before(l, i, Z_IN))
                        product(l, IN0, i, 2, u, h_hi, h_lo, 0, KT, Z[u])
                for j in range(2):
                    pe.wait_ge(z_free[j], l * ZL + (Z_OUT + 1))
                for t in range(QB + 1):
                    rows = P if t < QB else NS
                    if t == QB:
                        behind(pe, s["vnat_ready"], nth(l, "vnat_ready", 0))
                    for c in range(CT):
                        ins = nc.tensor.transpose(ps[0:rows, 4 + t % 4, c * P:(c + 1) * P], vT[:, c, t * P:t * P + rows], eye[:])
                    ins.then_inc(s["vt_ps"], 1)
                behind(pe, s["vnat_ready"], nth(l, "vnat_ready", QB))

                def head_scores(i, e):
                    f = slice(e * HD, (e + 1) * HD)
                    pe.wait_ge(s["s_free"], (l * NH + i * 2) * QB + (e + 1) * QB)
                    for q in range(QB):
                        bank, o = S_BANK[q]
                        ins = nc.tensor.matmul(ps[:, bank, o:o + (q + 1) * P], Qst[f, q * P:(q + 1) * P],
                                               Kst[f, 0:(q + 1) * P], start=True, stop=True)
                        if q:
                            ins.then_inc(s["s_ps"], 1)

                def scores(i):
                    pe.wait_ge(s["qk_staged"], l * CT + i + 1)
                    head_scores(i, 0)
                    for b in range(2):
                        rows = slice(b * HD, (b + 1) * HD)
                        pe.wait_ge(kc_in[b], (l * CT + i) * 16 + 16)
                        for c in range(CT):
                            nc.tensor.matmul(ps[rows, 3, :], Qbd[:, b, c, :], kc[:, b, c, :], start=c == 0, stop=c == CT - 1)
                        for c in range(CT):
                            ins = nc.tensor.matmul(ps[rows, 7, 0:NS], Qbd[:, b, c, :], qk[:, CT + c, SEQ:T],
                                                   start=c == 0, stop=c == CT - 1)
                    ins.then_inc(s["ss_ps"], 1)

                def pair(i, last=False):
                    def turn(e):
                        for k in range(QB):
                            pe.wait_ge(s["p_ready"], (l * NH + i * 2) * QB + (e + 1) * QB)
                            pe.wait_ge(s["pt_ready"], (l * NH + i * 2) * QB + (e * QB + k + 1))
                            for q in range(k, QB):
                                o = E_OFF[q] + k * P
                                ins = nc.tensor.transpose(ps[:, k % 2, (q - k) * P:(q - k + 1) * P], E[:, e, o:o + P], eye[:])
                            ins.then_inc(s["pt_ps"], 1)
                            if k % 2:
                                ada_unit(v, 1, 2 * e + k // 2, 6)

                    def outputs(e):
                        f = slice(e * HD, (e + 1) * HD)
                        for k in range(QB):
                            n = (QB - k) * P
                            pe.wait_ge(s["pt_ready"], (l * NH + i * 2) * QB + (e * QB + k + 1 + FREE["pt_ready"]))
                            ins = nc.tensor.matmul(ps[f, 2, k * P:SEQ], Vst[:, k, f], PT[:, e, PT_OFF[k]:PT_OFF[k] + n],
                                                   start=k == 0, stop=k == QB - 1)
                        return ins

                    v = ada_before(l) + i
                    if last:
                        pe.wait_ge(s["pt_ready"], (l * NH + i * 2) * QB + FREE["pt_ready"])
                        pe.wait_ge(s["conv_done"], nth(l, "conv_done", CT // 2 - 1))
                        pe.wait_ge(s["conv_dve"], l + 1)
                        pe.wait_ge(s["ada_out"], v + 1)
                        column_sums(y, CONV_STAT, range(CT)).then_inc(s["m_sum"], 1)
                    head_scores(i, 1)
                    pe.wait_ge(s["o_free"], l * CT + i + 1)
                    for q in range(A_UNITS // 2):
                        ada_unit(v, 0, q, 2)
                    if last:
                        pe.wait_ge(s["m_sq"], nth(l, "m_sq", 0))
                        column_sums(sqc, CONV_STAT, range(CT)).then_inc(s["m_var"], 1)
                        pe.wait_ge(s["m_sd"], nth(l, "m_sd", 0))
                    pe.wait_ge(s["s_free"], (l * NH + i * 2) * QB + (2 * QB + FREE["s_free"]))
                    pe.wait_ge(s["ada_out"], v + 1)
                    turn(0)
                    pe.wait_ge(s["ada_sb"], v * 2 + 3)
                    pe.wait_ge(s["v_staged"], l * CT + i + 1)
                    outputs(0)
                    turn(1)
                    outputs(1).then_inc(s["o_ps"], 1)
                    pe.wait_ge(s["ps_ready"], l * CT + i + 2)
                    for k in range(QB):
                        nc.tensor.transpose(ps[:, 3, k * P:(k + 1) * P], Es[:, k * P:(k + 1) * P], eye[:])
                    nc.tensor.transpose(ps[0:NS, 7, 0:P], Es[:, PAST:T], eye[:]).then_inc(s["pts_ps"], 1)
                    ada_turn(v, 0)
                    pe.wait_ge(s["pts_ready"], (l * CT + i) * 2 + 2)
                    for b in range(2):
                        rows = slice(b * HD, (b + 1) * HD)
                        pe.wait_ge(vc_in[b], (l * CT + i) * 16 + 16)
                        for k in range(QB):
                            nc.tensor.matmul(ps[rows, 3, :], PTs[:, k, rows], vc[:, b, k, :], start=k == 0, stop=False)
                        ins = nc.tensor.matmul(ps[rows, 3, :], PTs[0:NS, QB, rows], vnat[0:NS, QB, :], start=False, stop=True)
                    ins.then_inc(s["os_ps"], 1)
                    if last:
                        pe.wait_ge(s["s_free"], (l * NH + NH) * QB + FREE["s_free"])
                        pe.wait_ge(s["m_sq"], nth(l, "m_sq", 1))
                        column_sums(sqc, STAT[0], range(CT)).then_inc(s["m_var"], 1)
                    if last:
                        pe.wait_ge(s["o_free"], nth(l, "o_free", CT - 1))
                        pe.wait_ge(s["m_sq"], nth(l, "m_sq", 2))
                        for c in range(CT):
                            ins = nc.tensor.matmul(ps[:, 2, :], ones[:], sqm[:, c, 0:SEQ], start=c == 0, stop=c == CT - 1)
                        ins.then_inc(s["m_var"], 1)
                    pe.wait_ge(s["os_ready"], l * CT + i + 1)
                    for c in range(CT):
                        ins = nc.tensor.transpose(ps[:, 7, c * P:(c + 1) * P], Os[:, c * P:(c + 1) * P], eye[:])
                    ins.then_inc(s["ost_ps"], 1)

                scores(0)
                with pe.Fori(0, CT - 1) as i:
                    pair(i)
                    pe.wait_ge(s["o_done"], (l * CT + i) * 2 + 2)
                    scores(i + 1)
                pair(CT - 1, True)
                pe.wait_ge(s["o_done"], nth(l, "o_done", 2 * CT - 1))
                pe.wait_ge(s["m_sq"], nth(l, "m_sq", 3))
                for c in range(CT):
                    ins = nc.tensor.matmul(ps[:, 3, 0:NS], ones[:], sqm[:, c, SEQ:T], start=c == 0, stop=c == CT - 1)
                ins.then_inc(s["m_var"], 1)
                for u in range(2):
                    pe.wait_ge(z_free[u], z_before(l, 0, Z_OUT))
                products_by_tile(l, OUT0, M_ORDER, lambda n: pe.wait_ge(s["m_lo"], nth(l, "m_lo", n)))
                with pe.Fori(1, N_OUT // 2 - 1) as i:
                    for u in range(2):
                        pe.wait_ge(z_free[u], z_before(l, i, Z_OUT))
                        product(l, OUT0, i, 2, u, h_hi, h_lo, 0, KT, Z[u])
                last = N_OUT // 2 - 1
                for u in range(2):
                    pe.wait_ge(z_free[u], z_before(l, last, Z_OUT))
                    product(l, OUT0, last, 2, u, h_hi, h_lo, 0, KT, Z[u])
                    if u == 0:
                        norm_first(l, 0, Z_OUT)
                norm_tile(l, 0)
                norm_last(l, 0, (0,), (1, 2, 3))
                for u in range(2):
                    pe.wait_ge(z_free[u], z_before(l, 0, Z_GU))
                products_by_tile(l, GU0, range(KT), h_ready(l, 1))
                with pe.Fori(1, FT) as i:
                    for u in range(2):
                        pe.wait_ge(z_free[u], z_before(l, i, Z_GU))
                        product(l, GU0, i, 2, u, h_hi, h_lo, 0, KT, Z[u])

                def down(i, last):
                    for u in range(6):
                        r = u % 3
                        if r == 0:
                            pe.wait_ge(z_free[u // 3], z_before(l, i, Z_DN))
                        pe.wait_ge(s["a_lo"], nth(l, "a_lo", sum(DN_K[:r + 1]) - 1))
                        product(l, DN0, i, 6, u, a_hi, a_lo, sum(DN_K[:r]), DN_K[r], Z[u // 3], r == 0, r == 2)
                        if last and u == 2:
                            norm_first(l, 1, Z_DN)
                        if last and u == 4:
                            norm_tile(l, 1)
                            norm_squares(l, 1, 2, True)

                with pe.Fori(0, KT // 2 - 1) as i:
                    down(i, False)
                down(KT // 2 - 1, True)
                pe.wait_ge(s["sq_half"], l + 1)
                norm_last(l, 1, (0,), (3,))


def kernel(**v):
    import concourse.bacc as bacc
    from concourse.bass_utils import run_bass_kernel_spmd

    f = np.float32
    v = {k: np.asarray(a) for k, a in v.items()}

    def fm(a):
        return a.T.reshape(-1, P, a.shape[0]).transpose(1, 0, 2)

    def tiles(w):
        k, m = w.shape
        return w.reshape(k // P, P, m // P, P).transpose(2, 1, 0, 3).reshape(m // P, P, k)

    mix = []
    for l in range(DEPTH):
        wi = tiles(v["w_in"][l])
        wg, wu = tiles(v["w_gate"][l]), tiles(v["w_up"][l])
        g0 = 3 * CT
        glu = [wi[g0 + k] for c in range(CT) for k in (CT + c, c)]
        mix.append(np.stack(glu + list(wi[:g0]) + list(tiles(v["w_out"][l])) + [t for p in zip(wg, wu) for t in p]))
    vecs = []
    for l in range(DEPTH):
        cols = [v["conv_w"][l].T.reshape(CT, P, CW).transpose(1, 0, 2).reshape(P, -1)]
        for name in ("conv_b", "conv_ln_g", "conv_ln_b", "beta_attn", "beta_conv", "ln1_g", "ln1_b", "ln2_g", "ln2_b"):
            cols.append(v[name][l].reshape(-1, P).T)
        vecs.append(np.concatenate(cols, axis=1))

    wa = v["w_ada"].reshape(DEPTH, KT // 2, 2, P, 6, 2, 512).transpose(0, 4, 5, 1, 3, 2, 6).reshape(DEPTH, 6, A_UNITS, P, UNIT)
    ba = v["b_ada"].reshape(DEPTH, 6, KT, P)
    ba = np.concatenate([ba[:, 0:2].reshape(-1, P), ba[:, 2:6].reshape(-1, P)]).T

    pos = np.concatenate([np.arange(SEQ), np.tile(PAST + np.arange(NT), NB)]).astype(f)
    half = HD // 8
    inv = np.power(f(500000.0), -np.arange(half, dtype=f) * f(2.0) / f(2 * half)).astype(f)
    ang = (pos[None, :] * inv[:, None]).astype(f).astype(np.float64)
    cos, sin = np.ones((P, T)), np.zeros((P, T))
    for h0 in (0, HD):
        cos[h0:h0 + half] = cos[h0 + half:h0 + 2 * half] = np.cos(ang)
        sin[h0:h0 + half], sin[h0 + half:h0 + 2 * half] = -np.sin(ang), np.sin(ang)
    rope = np.stack([cos, sin], axis=1).astype(f)

    def masks(diff, bound4=PAST):
        ok = diff >= 0
        n = (ok & (diff <= 128)).astype(f) + (ok & (diff % 4 == 0) & (diff <= bound4)) + (ok & (diff % 16 == 0))
        return np.stack([np.where(n > 0, f(0), f(NEG)), n], axis=1).astype(f)

    i = np.arange(P)[:, None]
    mp = masks(np.concatenate([d * P + i - np.arange(P)[None] for d in range(QB - 1, -1, -1)], axis=1))
    t = i % NT
    msc = masks(PAST + t - np.arange(PAST)[None])
    msn = []
    for pair in range(CT):
        key = np.arange(NS)[None]
        same = key // NT == 2 * pair + i // HD
        msn.append(masks(np.where(same, t - key % NT, -1)))
    msn = np.stack(msn, axis=1)

    x_all = np.concatenate([v["x_prompt"][0], v["x_sample"].reshape(NS, D)], axis=0)
    c_all = np.concatenate([v["c_prompt"], v["c_sample"]], axis=0)
    ck = v["cache_k"].reshape(DEPTH, NB, PAST, CT, P).transpose(0, 1, 4, 3, 2)
    cv = v["cache_v"].reshape(DEPTH, NB, PAST // P, P, DA).transpose(0, 1, 3, 2, 4)
    sc = v["state_conv"].reshape(DEPTH, NB, HIST, CT, P).transpose(0, 4, 3, 1, 2)
    ins = dict(
        xT=fm(x_all), cT=fm(c_all), ba_d=ba, w_mod1=wa[:, 0:2].reshape(V_EARLY, A_UNITS, P, UNIT), w_mod2=wa[:, 2:6], w_mix=np.stack(mix),
        w_dn=np.stack([tiles(w) for w in v["w_down"]]), kc_d=ck, vc_d=cv, st_d=sc, vec_d=np.stack(vecs), rope_d=rope,
        eye_d=np.eye(P, dtype=f), mp_d=mp, msc_d=msc, msn_d=msn)
    outs = dict(y_d=(P, KT, T), k_d=(DEPTH, P, CT, T), v_d=(DEPTH, P, CT, T), cp_d=(DEPTH, P, CT, HIST),
                cs_d=(DEPTH, P, CT, NB, HIST))
    nc = bacc.Bacc("TRN2", target_bir_lowering=False, num_devices=1)
    arrays, args = {}, {}
    for name, a in ins.items():
        arrays[name] = np.ascontiguousarray(a)
        args[name] = nc.dram_tensor(name, a.shape, F32, kind="ExternalInput").ap()
    for name, shape in outs.items():
        args[name] = nc.dram_tensor(name, shape, F32, kind="ExternalOutput").ap()
    trunk(nc, **args)
    r = run_bass_kernel_spmd(nc, [arrays], core_ids=[0]).results[0]

    def rows(a):
        a = np.moveaxis(a, -1, -3)
        return np.swapaxes(a, -1, -2).reshape(*a.shape[:-2], -1)

    yy, kk, vv = rows(r["y_d"]), rows(r["k_d"]), rows(r["v_d"])
    heads = (NH, HD)
    cp = r["cp_d"].transpose(0, 3, 2, 1).reshape(DEPTH, 1, HIST, DA)
    cs = r["cs_d"].transpose(0, 3, 4, 2, 1).reshape(DEPTH, NB, HIST, DA)
    return (yy[None, :SEQ], yy[SEQ:].reshape(NB, NT, D),
            kk[:, None, :SEQ].reshape(DEPTH, 1, SEQ, *heads), vv[:, None, :SEQ].reshape(DEPTH, 1, SEQ, *heads), cp,
            kk[:, SEQ:].reshape(DEPTH, NB, NT, *heads), vv[:, SEQ:].reshape(DEPTH, NB, NT, *heads), cs)
```
